# Optimizing a Trainium2 kernel written in Bass

```python
import jax, jax.numpy as jnp
from jax import lax
import numpy as np

D_MODEL = 1024
BATCH = 1
SEQ = 512
DEPTH = 1

CHUNK = 64
Q_BLOCK = 128
EPS = 1e-6

A_HEADS = 8
A_HEAD_DIM = 64
IDX_HEADS = 4
IDX_DIM = 64
TOPK_MAX = 256

B_HEADS = 8
B_HEAD_DIM = 64

C_HEADS = 4
C_KEY_DIM = 64
C_VAL_DIM = 128
C_GATE_RANK = 16
C_GATE_TAU = 16.0

PEER_HEADS = 8
PEER_NKEYS = 128
PEER_EXPERTS = PEER_NKEYS * PEER_NKEYS
PEER_QDIM = 256
PEER_TOPK = 16
TOKEN_BLOCK = 128

N_BRANCH = 3
BRANCH_WIDTH = 512
COL_WIDTHS = (
    A_HEADS * A_HEAD_DIM,
    A_HEAD_DIM,
    A_HEAD_DIM,
    IDX_HEADS * IDX_DIM,
    IDX_DIM,
    IDX_HEADS,
    B_HEADS * B_HEAD_DIM,
    B_HEADS * B_HEAD_DIM,
    B_HEADS * B_HEAD_DIM,
    C_HEADS * C_KEY_DIM,
    C_HEADS * C_KEY_DIM,
    C_HEADS * C_VAL_DIM,
    C_HEADS * C_VAL_DIM,
    C_GATE_RANK,
    N_BRANCH * D_MODEL,
)
IN_COLS = sum(COL_WIDTHS)

kernel_name = "hybrid_dsa_stickbreak_gla_peer_trunk"

def rms_norm(x, g):
    xf = x.astype(jnp.float32)
    y = xf * lax.rsqrt(jnp.mean(xf * xf, axis=-1, keepdims=True) + EPS)
    return y.astype(x.dtype) * g

def to_blocks(x, nb):
    b, t = x.shape[:2]
    return jnp.moveaxis(x.reshape(b, nb, t // nb, *x.shape[2:]), 1, 0)

def from_blocks(y):
    y = jnp.moveaxis(y, 0, 1)
    return y.reshape(y.shape[0], y.shape[1] * y.shape[2], *y.shape[3:])

def dsa_attention(q, k, v, q_idx, k_idx, w_idx, q_gain, k_gain):
    bsz, t_len = q.shape[:2]
    n_sel = min(TOPK_MAX, t_len // 4)
    nb = t_len // Q_BLOCK
    q = rms_norm(q, q_gain)
    k = rms_norm(k, k_gain)
    scale = A_HEAD_DIM ** -0.5
    gather = jax.vmap(lambda table, idx: table[idx])
    keys_pos = jnp.arange(t_len)

    def block(args):
        i, qb, qib, wb = args
        t = i * Q_BLOCK + jnp.arange(Q_BLOCK)
        limit = (t // CHUNK + 1) * CHUNK
        admissible = keys_pos[None, :] < limit[:, None]
        rel = jax.nn.relu(jnp.einsum('bqhd,bsd->bqhs', qib, k_idx).astype(jnp.float32))
        score = jnp.einsum('bqh,bqhs->bqs', wb.astype(jnp.float32), rel)
        score = jnp.where(admissible[None], score, -jnp.inf)
        _, sel = lax.top_k(score, n_sel)
        valid = sel < limit[None, :, None]
        k_sel = gather(k, sel)
        v_sel = gather(v, sel)
        logits = jnp.einsum('bqhd,bqkd->bqhk', qb, k_sel).astype(jnp.float32) * scale
        logits = jnp.where(valid[:, :, None, :], logits, -jnp.inf)
        p = jax.nn.softmax(logits, axis=-1).astype(v.dtype)
        return jnp.einsum('bqhk,bqkd->bqhd', p, v_sel)

    out = lax.map(block, (jnp.arange(nb), to_blocks(q, nb), to_blocks(q_idx, nb), to_blocks(w_idx, nb)))
    return from_blocks(out).reshape(bsz, t_len, -1)

def stick_breaking_attention(q, k, v, q_gain, k_gain):
    bsz, t_len = q.shape[:2]
    nb = t_len // Q_BLOCK
    q = rms_norm(q, q_gain)
    k = rms_norm(k, k_gain)
    scale = B_HEAD_DIM ** -0.5
    keys_pos = jnp.arange(t_len)

    def block(args):
        i, qb = args
        t = i * Q_BLOCK + jnp.arange(Q_BLOCK)
        strict = keys_pos[None, :] < t[:, None]
        z = jnp.einsum('bqhd,bshd->bhqs', qb, k).astype(jnp.float32) * scale
        log_beta = jax.nn.log_sigmoid(z)
        log_keep = jnp.where(strict, jax.nn.log_sigmoid(-z), 0.0)
        later = lax.cumsum(log_keep, axis=3, reverse=True) - log_keep
        a = jnp.where(strict, jnp.exp(log_beta + later), 0.0).astype(v.dtype)
        return jnp.einsum('bhqs,bshd->bqhd', a, v)

    out = lax.map(block, (jnp.arange(nb), to_blocks(q, nb)))
    return from_blocks(out).reshape(bsz, t_len, -1)

def gla_attention(q, k, v, r, a_low, w_alpha, b_alpha, out_gain):
    bsz, t_len = q.shape[:2]
    nc = t_len // CHUNK
    f32 = jnp.float32
    log_alpha = jax.nn.log_sigmoid((a_low @ w_alpha + b_alpha).astype(f32)) / C_GATE_TAU
    log_alpha = log_alpha.reshape(bsz, t_len, C_HEADS, C_KEY_DIM)
    qs = q.astype(f32) * (C_KEY_DIM ** -0.5)

    def chunks(x):
        return jnp.swapaxes(to_blocks(x, nc), 2, 3)

    causal = jnp.tril(jnp.ones((CHUNK, CHUNK), dtype=bool))

    def step(state, inp):
        qc, kc, vc, lac = inp
        b = jnp.cumsum(lac, axis=2)
        o_inter = jnp.einsum('bhtk,bhkv->bhtv', qc * jnp.exp(b), state)
        diff = b[:, :, :, None, :] - b[:, :, None, :, :]
        decay = jnp.exp(jnp.where(causal[:, :, None], diff, -jnp.inf))
        att = jnp.einsum('bhtk,bhsk,bhtsk->bhts', qc, kc, decay)
        o_intra = jnp.einsum('bhts,bhsv->bhtv', att, vc)
        b_last = b[:, :, -1:, :]
        state = state * jnp.exp(b_last[:, :, 0, :, None]) + jnp.einsum(
            'bhsk,bhsv->bhkv', kc * jnp.exp(b_last - b), vc)
        return state, o_inter + o_intra

    state0 = jnp.zeros((bsz, C_HEADS, C_KEY_DIM, C_VAL_DIM), f32)
    _, o = lax.scan(step, state0, (chunks(qs), chunks(k.astype(f32)), chunks(v.astype(f32)), chunks(log_alpha)))
    o = from_blocks(jnp.swapaxes(o, 2, 3)).astype(q.dtype)
    o = rms_norm(o, out_gain.reshape(C_HEADS, C_VAL_DIM)) * jax.nn.silu(r)
    return o.reshape(bsz, t_len, -1)

def hybrid_mixer(n, w_in, b_gate, a_qn_g, a_kn_g, b_qn_g, b_kn_g, c_w_alpha, c_b_alpha, c_on_g,
                 w_oa, w_ob, w_oc, w_out):
    bsz, t_len, d = n.shape
    z = n @ w_in
    (aq, ak, av, iq, ik, iw, bq, bk, bv, cq, ck, cv, cr, ca, gl) = jnp.split(
        z, np.cumsum(COL_WIDTHS)[:-1].tolist(), axis=-1)
    ya = dsa_attention(aq.reshape(bsz, t_len, A_HEADS, A_HEAD_DIM), ak, av,
                       iq.reshape(bsz, t_len, IDX_HEADS, IDX_DIM), ik, iw, a_qn_g, a_kn_g)
    yb = stick_breaking_attention(bq.reshape(bsz, t_len, B_HEADS, B_HEAD_DIM),
                                  bk.reshape(bsz, t_len, B_HEADS, B_HEAD_DIM),
                                  bv.reshape(bsz, t_len, B_HEADS, B_HEAD_DIM), b_qn_g, b_kn_g)
    yc = gla_attention(cq.reshape(bsz, t_len, C_HEADS, C_KEY_DIM), ck.reshape(bsz, t_len, C_HEADS, C_KEY_DIM),
                       cv.reshape(bsz, t_len, C_HEADS, C_VAL_DIM), cr.reshape(bsz, t_len, C_HEADS, C_VAL_DIM),
                       ca, c_w_alpha, c_b_alpha, c_on_g)
    gates = jax.nn.sigmoid((gl + b_gate).astype(jnp.float32)).astype(n.dtype).reshape(bsz, t_len, N_BRANCH, d)
    merged = gates[:, :, 0] * (ya @ w_oa) + gates[:, :, 1] * (yb @ w_ob) + gates[:, :, 2] * (yc @ w_oc)
    return merged @ w_out

def peer_ffn(xn, w_pq, sub_keys, u_tab, v_tab):
    bsz, t_len, d = xn.shape
    nblk = (bsz * t_len) // TOKEN_BLOCK
    xt = xn.reshape(nblk, TOKEN_BLOCK, d)

    def block(xb):
        q = (xb @ w_pq).reshape(TOKEN_BLOCK, PEER_HEADS, 2, PEER_QDIM // 2)
        s = jnp.einsum('nhpd,hpkd->nhpk', q, sub_keys).astype(jnp.float32)
        top_s, top_i = lax.top_k(s, PEER_TOPK)
        cand = (top_s[:, :, 0, :, None] + top_s[:, :, 1, None, :]).reshape(TOKEN_BLOCK, PEER_HEADS, -1)
        cand_idx = (top_i[:, :, 0, :, None] * PEER_NKEYS + top_i[:, :, 1, None, :]).reshape(
            TOKEN_BLOCK, PEER_HEADS, -1)
        best_s, best_j = lax.top_k(cand, PEER_TOPK)
        expert = jnp.take_along_axis(cand_idx, best_j, axis=-1)
        g = jax.nn.softmax(best_s, axis=-1)
        u = u_tab[expert]
        vv = v_tab[expert]
        act = jax.nn.gelu(jnp.einsum('nd,nhkd->nhk', xb, u).astype(jnp.float32), approximate=False)
        return jnp.einsum('nhk,nhkd->nd', (g * act).astype(xb.dtype), vv)

    return lax.map(block, xt).reshape(bsz, t_len, d)

def setup_inputs(seed: int = 0) -> dict:
    key = jax.random.key(seed)
    ks = jax.random.split(key, 24)
    L, D = DEPTH, D_MODEL

    def nrm(k, shape, std):
        return jax.random.normal(k, shape, jnp.float32) * std

    return {
        "x": nrm(ks[0], (BATCH, SEQ, D), 1.0),
        "c": nrm(ks[1], (BATCH, D), 1.0),
        "norm1_g": 1.0 + nrm(ks[2], (L, D), 0.02),
        "norm2_g": 1.0 + nrm(ks[3], (L, D), 0.02),
        "w_mod": nrm(ks[4], (L, D, 6 * D), 0.5 * D ** -0.5),
        "b_mod": nrm(ks[5], (L, 6 * D), 0.02),
        "w_in": nrm(ks[6], (L, D, IN_COLS), D ** -0.5),
        "b_gate": nrm(ks[7], (L, N_BRANCH * D), 0.02),
        "a_qn_g": 1.0 + nrm(ks[8], (L, A_HEAD_DIM), 0.02),
        "a_kn_g": 1.0 + nrm(ks[9], (L, A_HEAD_DIM), 0.02),
        "b_qn_g": 1.0 + nrm(ks[10], (L, B_HEAD_DIM), 0.02),
        "b_kn_g": 1.0 + nrm(ks[11], (L, B_HEAD_DIM), 0.02),
        "c_w_alpha": nrm(ks[12], (L, C_GATE_RANK, C_HEADS * C_KEY_DIM), C_GATE_RANK ** -0.5),
        "c_b_alpha": nrm(ks[13], (L, C_HEADS * C_KEY_DIM), 0.02),
        "c_on_g": 1.0 + nrm(ks[14], (L, C_HEADS * C_VAL_DIM), 0.02),
        "w_oa": nrm(ks[15], (L, A_HEADS * A_HEAD_DIM, D), (A_HEADS * A_HEAD_DIM) ** -0.5),
        "w_ob": nrm(ks[16], (L, B_HEADS * B_HEAD_DIM, D), (B_HEADS * B_HEAD_DIM) ** -0.5),
        "w_oc": nrm(ks[17], (L, C_HEADS * C_VAL_DIM, D), (C_HEADS * C_VAL_DIM) ** -0.5),
        "w_out": nrm(ks[18], (L, D, D), D ** -0.5),
        "peer_wq": nrm(ks[19], (L, D, PEER_HEADS * PEER_QDIM), D ** -0.5),
        "peer_subkeys": nrm(ks[20], (L, PEER_HEADS, 2, PEER_NKEYS, PEER_QDIM // 2), (PEER_QDIM // 2) ** -0.5),
        "peer_u": nrm(ks[21], (L, PEER_EXPERTS, D), D ** -0.5),
        "peer_v": nrm(ks[22], (L, PEER_EXPERTS, D), 1.0),
    }

def reference(x, c, norm1_g, norm2_g, w_mod, b_mod, w_in, b_gate, a_qn_g, a_kn_g, b_qn_g, b_kn_g,
              c_w_alpha, c_b_alpha, c_on_g, w_oa, w_ob, w_oc, w_out,
              peer_wq, peer_subkeys, peer_u, peer_v):
    bsz, t_len, d = x.shape
    h = x
    c_act = jax.nn.silu(c)
    for l in range(DEPTH):
        mod = (c_act @ w_mod[l] + b_mod[l]).reshape(bsz, 6, 1, d)
        shift1, scale1, gate1 = mod[:, 0], mod[:, 1], mod[:, 2]
        shift2, scale2, gate2 = mod[:, 3], mod[:, 4], mod[:, 5]
        n = rms_norm(h, norm1_g[l]) * (1.0 + scale1) + shift1
        y = hybrid_mixer(n, w_in[l], b_gate[l], a_qn_g[l], a_kn_g[l], b_qn_g[l], b_kn_g[l],
                         c_w_alpha[l], c_b_alpha[l], c_on_g[l], w_oa[l], w_ob[l], w_oc[l], w_out[l])
        h = h + gate1 * y
        n = rms_norm(h, norm2_g[l]) * (1.0 + scale2) + shift2
        h = h + gate2 * peer_ffn(n, peer_wq[l], peer_subkeys[l], peer_u[l], peer_v[l])
    return h


_drawn_inputs = setup_inputs


def setup_inputs(seed=0):
    import zlib

    import numpy as np

    out = dict(_drawn_inputs(seed))
    spreads = {}
    factors = {'norm1_g': 3.559,
     'b_gate': 8.0,
     'a_qn_g': 31.846,
     'a_kn_g': 30.103,
     'b_qn_g': 116.182,
     'b_kn_g': 110.634,
     'c_b_alpha': 8.0,
     'c_on_g': 20.768,
     'norm2_g': 8.0}
    for name, (base, spread) in spreads.items():
        noise = np.random.default_rng([zlib.crc32(name.encode()), seed]).standard_normal(out[name].shape)
        drawn = base * np.exp(spread * noise) if base else spread * noise
        out[name] = __import__('jax').numpy.asarray(drawn.astype(out[name].dtype))
    for name, factor in factors.items():
        out[name] = (out[name] * factor).astype(out[name].dtype)
    return out
```

```python
from contextlib import ExitStack

import numpy as np

import concourse.bass as bass
from concourse import mybir

ALU = mybir.AluOpType
ACT = mybir.ActivationFunctionType
F32 = mybir.dt.float32
U32 = mybir.dt.uint32
AX = mybir.AxisListType.X

P = 128
T, D = 512, 1024
KT, TT = D // P, T // P
EPS = 1e-6
HA = HB = 8
HD = 64
NI = 4
TOPK = T // 4
HC, CV = 4, 128
CH = 64
NCH = T // CH
TAU = 16.0
PH, NK, PK = 8, 128, 16
NE = NK * NK
QT = 2 * PH
LEVELS = (32, 16, 8, 4, 2, 1)
MASKED = -1e30
HIDDEN, PICKED = -3.0e38, -3.4e38
SMALL = 84
WSLOT, NSLOT = 4608, 3
NMOD = 6 * KT

C_ID, C_LATER, C_ONES, C_PAST, C_SEL, C_RESET = 0, 128, 256, 384, 512, 640
C_SELT, C_LEVEL = 1152, 2176
C_IOTA = C_LEVEL + 128 * (len(LEVELS) + 1)
C_END = C_IOTA + 16
V_C, V_BMOD, V_G1, V_G2, V_BG, V_BA, V_GAIN, V_ONG = 0, 8, 56, 64, 72, 96, 98, 102
V_END = V_ONG + HC * CV

B_OFF = (0, 512, 1024, 896)
B_COLS = 1280
A_OFF = (0, 128, 384, 768)


def shape_constants():
    c = np.zeros((P, C_END), np.float32)
    p = np.arange(P)[:, None]
    f = np.arange(P)[None, :]
    c[:, C_ID:C_ID + P] = p == f
    c[:, C_LATER:C_LATER + P] = p > f
    c[:, C_ONES:C_ONES + P] = 1.0
    c[:, C_PAST:C_PAST + P] = p < f
    for t in range(8):
        c[:, C_SEL + 16 * t:C_SEL + 16 * (t + 1)] = np.arange(16)[None, :] == 2 * t + p // HD
        c[0:16, C_SELT + P * t:C_SELT + P * (t + 1)] = p[0:16] == 2 * t + f // HD
    c[:, C_RESET:C_RESET + T] = np.arange(T)[None, :] % CH != 0
    for i, w in enumerate(LEVELS):
        same = p // (2 * w) == f // (2 * w)
        c[:, C_LEVEL + P * i:C_LEVEL + P * (i + 1)] = same & (p % (2 * w) < w) & (f % (2 * w) >= w)
    c[:, C_LEVEL + P * len(LEVELS):C_LEVEL + P * (len(LEVELS) + 1)] = p == f
    c[:, C_IOTA:C_IOTA + 16] = np.arange(16)[None, :]
    return c


def places(sizes):
    at, end = {}, 0
    for name, n in sizes:
        at[name] = end
        end += n
    return at, end


AT, SPACE_END = places([
    ("const", C_END), ("vec", V_END), ("mod", 64), ("stat", 320), ("walpha", 256), ("wsmall", KT * SMALL),
    ("w", WSLOT * NSLOT), ("n", KT * T), ("x", TT * D),
    ("qa", 4 * T), ("ka", T), ("iq", 2 * T), ("ik", T), ("qb", 4 * T), ("kb", 4 * T),
    ("cq", 2 * T), ("ck", 2 * T), ("ca", T), ("va", TT * 68), ("vb", TT * T), ("vc", TT * T), ("rc", TT * T),
    ("ya", 4 * T), ("yb", 4 * T), ("yc", 4 * T), ("sq", 2 * T), ("pen", 1280),
])


def jobs_of_projection():
    jobs = [("d", 4, i, ("qa", i), i) for i in range(4)]
    jobs += [("d", 5, 0, ("ka", 0), 4), ("d", 5, 1, ("iq", 0), None), ("d", 5, 2, ("iq", 1), None),
             ("d", 5, 3, ("ik", 0), None)]
    jobs += [("s", None, t, "va", None) for t in range(TT)] + [("c", None, 0, "ca", None)]
    jobs += [("d", 6, i, ("qb", i), 5 + i) for i in range(4)] + [("d", 7, i, ("kb", i), 9 + i) for i in range(4)]
    jobs += [("t", 8, t, "vb", None) for t in range(TT)] + [("t", 9, t, "vc", None) for t in range(TT)]
    jobs += [("d", 10, i, (("cq", 0), ("cq", 1), ("ck", 0), ("ck", 1))[i], None) for i in range(4)]
    jobs += [("t", 11, t, "rc", None) for t in range(TT)]
    return jobs


def encoder_layer(nc, cst, vec, x, w_mod, w_proj, w_small, w_alpha, w_merge, w_out, w_pq, subkeys,
                  u_table, v_table, out):
    with ExitStack() as ctx:
        sb = ctx.enter_context(nc.sbuf_tensor("sb", [P, SPACE_END + 32], F32))
        ps = ctx.enter_context(nc.psum_tensor("ps", [P, 8 * 512], F32))

        sems = {}

        def sem(name):
            sems[name] = ctx.enter_context(nc.semaphore(name))
            return sems[name]

        def area(name, lo=0, n=None, p0=0, p1=P):
            a = AT[name] + lo
            return sb[p0:p1, a:a + n]

        def bank(b, n=512, lo=0, p0=0, p1=P):
            return ps[p0:p1, 512 * b + lo:512 * b + lo + n]

        def tiles(ap, n):
            return ap.rearrange("p (a b) -> p a b", a=n)

        ident = area("const", C_ID, P)
        later_tri = area("const", C_LATER, P)
        ones = area("const", C_ONES, P)
        past_tri = area("const", C_PAST, P)
        reset = area("const", C_RESET, T)

        def vcol(i, n=1):
            return area("vec", i, n)

        mod = area("mod", 0, NMOD)
        SH1, SC1, GT1, SH2, SC2, GT2 = (8 * i for i in range(6))

        def mcol(i, n=1):
            return area("mod", i, n)

        amp1 = area("mod", 48, 8)
        amp2 = area("mod", 56, 8)
        cact = area("stat", 0, 8)
        xss, xvar, xrt, xr, xt1 = (area("stat", 8 + 4 * i, 4) for i in range(5))
        top8 = area("stat", 28, 8)
        amax = area("stat", 40, 32)
        anmax = area("stat", 72, 32)
        asum = area("stat", 104, 32)
        arcp = area("stat", 136, 32)
        ebl = area("stat", 168, 16)
        css, cvar, crt, crs, ct1 = (area("stat", 184 + 16 * i, 16) for i in range(5))
        walpha = area("walpha", 0, 256, 0, 16)
        wsmall = tiles(area("wsmall", 0, KT * SMALL), KT)
        n_t = tiles(area("n", 0, KT * T), KT)
        x_tm = tiles(area("x", 0, TT * D), TT)
        xhat = tiles(area("vb", 0, TT * D), TT)
        qa, ka = tiles(area("qa", 0, 4 * T), 4), area("ka", 0, T)
        iq, ik = tiles(area("iq", 0, 2 * T), 2), area("ik", 0, T)
        qb, kb = tiles(area("qb", 0, 4 * T), 4), tiles(area("kb", 0, 4 * T), 4)
        cqk = area("cq", 0, 4 * T)
        ca = area("ca", 0, T, 0, 16)
        va = tiles(area("va", 0, TT * 68), TT)
        vb, vc, rc = (tiles(area(k, 0, TT * T), TT) for k in ("vb", "vc", "rc"))
        ya, yb, yc = (tiles(area(k, 0, 4 * T), 4) for k in ("ya", "yb", "yc"))
        sq = [area("sq", T * i, T) for i in range(2)]

        def pen(qt):
            return area("pen", A_OFF[qt], P * (qt + 1))

        irelu = [area("yb", T * i, T) for i in range(2)]
        st_var, st_rt, st_r, st_t = (area("ya", T * i, T, 0, 16) for i in range(4))
        prob = [area("x", T * i, T) for i in range(3)]
        probT = [area("x", 1536 + T * i, T) for i in range(2)]
        o_tm = area("x", 2560, T)
        spb = [area("x", B_COLS * i, B_COLS) for i in range(2)]
        keep = [area("x", 2 * B_COLS, B_COLS), area("qa", 0, B_COLS)]
        beta = [area("qa", B_COLS, B_COLS), area("qa", 2 * B_COLS, B_COLS), area("pen", 0, B_COLS)]
        c_qk = [area("x", 0, 4 * T), area("x", 4 * T, 4 * T)]
        c_e = area("qa", 0, 4 * T)
        c_qk0 = area("qa", 4 * T, 4 * T)
        c_att = area("qb", 0, 4 * T)
        c_state = area("kb", 0, 2 * P * NCH)
        c_b = area("sq", 0, 2 * T)
        c_kdt = area("pen", 0, 2 * T)

        def kv_at(c, i):
            return 1024 * (c % 2) + 2 * P * (c // 2) + P * i

        def head_at(t, h):
            return P * (8 * (h % 2) + 2 * t + h // 2)

        merged = tiles(area("qb", 0, KT * T), KT)
        gates = [area("qa", 4 * T + T * i, T) for i in range(2)]
        gated = area("qa", 6 * T, T)

        h_t = tiles(area("ya", 0, KT * T), KT)
        yg = [area("yc", T * i, T) for i in range(2)]
        nvar, nrt, nr, ntmp = (area("yc", T * i, T) for i in range(4))
        h_tm = x_tm
        n2_tm = tiles(area("vb", 0, TT * D), TT)
        sk = tiles(area("cq", 0, QT * NK), QT)
        qp = sq
        scores = area("qa", 0, TT * QT * NK)
        g2row = area("yc", 0, D)
        g2tmp = tiles(area("yc", D, D), KT)
        NU = TT * PH
        R = 8
        u_ring = [area("w", D * i, D) for i in range(R)]
        v_ring = [area("w", D * (R + i), D) for i in range(R)]
        at = AT["ya"]
        n2_cur = [sb[:, at + D * i:at + D * (i + 1)] for i in range(2)]
        acc_tmp = sb[:, at + 3 * D:at + 4 * D]
        PICK_STEPS = 20
        at = AT["rc"]
        pick = {}
        for nm, n in (("sc", 2 * NK), ("left", 2 * NK), ("top", 32), ("best", 16), ("cand", 256), ("cleft", 256),
                      ("eq", 512), ("hl", 32), ("ixf", 32), ("ef", 32)):
            pick[nm] = sb[:, at:at + n]
            at += n
        ix_u = sb[:, at:at + 32].bitcast(U32)
        bj_u = sb[:, at + 32:at + 48].bitcast(U32)
        hl_u = sb[:, at + 48:at + 80].bitcast(U32)
        assert at + 80 <= AT["rc"] + TT * T
        at = AT["const"] + C_RESET
        dgw = [sb[:, at + P * i:at + P * (i + 1)] for i in range(4)]
        idx_all = area("pen", 0, 16 * NU).bitcast(U32)
        best_all = area("pen", 16 * NU, 16 * NU)
        at = AT["stat"]
        idx_u = [sb[:, at + 16 * i:at + 16 * (i + 1)].bitcast(U32) for i in range(2)]
        idx_v = [sb[:, at + 176 + 16 * i:at + 192 + 16 * i].bitcast(U32) for i in range(2)]
        dots = [sb[:, at + 32 + 16 * i:at + 48 + 16 * i] for i in range(2)]
        gelu = [sb[:, at + 64 + 16 * i:at + 80 + 16 * i] for i in range(2)]
        ebest = [sb[:, at + 96 + 16 * i:at + 112 + 16 * i] for i in range(2)]
        wgt = [sb[:, at + 128 + 16 * i:at + 144 + 16 * i] for i in range(2)]
        zsum = [sb[:, at + 160 + i:at + 161 + i] for i in range(2)]
        zinv = [sb[:, at + 162 + i:at + 163 + i] for i in range(2)]

        ld_const, ld_vec, ld_x, ld_ws, ld_wa = (sem(s) for s in ("ld_const", "ld_vec", "ld_x", "ld_ws", "ld_wa"))
        w_in = [sem(f"w_in{i}") for i in range(NSLOT)]
        w_used = sem("w_used")
        v_step, a_step, g_step = sem("v_step"), sem("a_step"), sem("g_step")
        names = """csig cact_ready xss_ready xvar_ready xrt_ready xhat_ready mod1_done mod1_read tr_done nt_ready
                   proj_done proj_out sq_ready sq_used stat_var stat_rt stat_r xa_done xa_read xi_done xi_read
                   irelu_used xb_done xb_read pen_ready mod2_done mod2_read
                   la_done la_read nmax_ready prob_ready pt_done pt_out pv_done o_ready ot_done ot_out
                   zb_done zb_abs zb_relu zb_min sp_ready beta_ready keep_ready lt_done sum_ready b_exp a_exp b_ready yb_done yb_out
                   cu_done cu_ready cabs csp cb_ready ce_ready cex_ready cqk_ready kdt_done kdt_out kv_done ebl_ready st_ready
                   cmin lev_done lev_read att_ready co_done css_ready cvar_ready crt_ready rsil rgain co_ready yct_done yct_out
                   gl_done gate_ready ob_done gate_used merged_ready yo_done yg_ready yg_used xt_done ht_ready
                   hsq_ready hsq_used nvar_ready nrt_ready nr_ready n2_ready att_zero ld_sk ld_x2
                   tm_done tm_out pq_done pq_out sc_done sc_out g2t_ready g2_done g2_ready picked idx_ready pool_go
                   n2c_ready u_used dots_ready gelu_ready z_ready w_ready dg_ready dg_used acc_done added p_step stored zi_ready gated2 idv_ready p_go""".split()
        u_in = [sem(f"u_in{i}") for i in range(R)]
        v_in = [sem(f"v_in{i}") for i in range(R)]
        s = {nm: sem(nm) for nm in names}

        def slot_view(i):
            return area("w", WSLOT * (i % NSLOT), WSLOT)

        jobs = jobs_of_projection()
        NJ = len(jobs)
        N_STAT = sum(j[4] is not None for j in jobs)
        J_SMALL = max(i for i, j in enumerate(jobs) if j[0] == "c")
        M_SLOTS = (12, 20)
        G_SLOT, O_SLOT, PQ_SLOT, N_SLOTS = 20, 28, 30, 34

        block = ctx.enter_context(nc.Block())

        @block.sync
        def _(sp):
            sp.dma_start(area("const", 0, C_END), cst).then_inc(ld_const, 16)
            sp.dma_start(area("vec", 0, V_END), vec).then_inc(ld_vec, 16)
            sp.dma_start(x_tm[:, :, :], x.rearrange("(t p) d -> p t d", p=P)).then_inc(ld_x, 16)
            wm = w_mod.rearrange("(k p) n -> p k n", p=P)
            for i in range(N_SLOTS):
                if i >= NSLOT:
                    sp.wait_ge(w_used, i - NSLOT + 1)
                dst = slot_view(i)
                if i < 4:
                    dst, src = tiles(dst[:, 0:4096], 2), wm[:, 2 * i:2 * i + 2, 0:2 * D]
                elif i < M_SLOTS[0]:
                    dst, src = dst[:, 0:4096], w_proj[i - 4]
                elif i < M_SLOTS[1]:
                    dst, src = dst[:, 0:4096], wm[:, i - M_SLOTS[0], 2 * D:6 * D]
                elif i < O_SLOT:
                    src = w_merge[i - G_SLOT]
                elif i < PQ_SLOT:
                    dst, src = dst[:, 0:4096], w_out[i - O_SLOT]
                else:
                    dst, src = dst[:, 0:4096], w_pq[i - PQ_SLOT]
                sp.dma_start(dst, src).then_inc(w_in[i % NSLOT], 16)
                if i == 3:
                    sp.dma_start(area("wsmall", 0, KT * SMALL), w_small).then_inc(ld_ws, 16)
                    sp.dma_start(walpha, w_alpha).then_inc(ld_wa, 16)
                if i == G_SLOT:
                    sp.wait_ge(s["lev_done"], len(LEVELS) + 1)
                    sp.dma_start(x_tm[:, :, :], x.rearrange("(t p) d -> p t d", p=P)).then_inc(s["ld_x2"], 16)
                    sp.dma_start(sk, subkeys).then_inc(s["ld_sk"], 16)
            for t in range(TT):
                sp.wait_ge(s["added"], PH * (t + 1))
                sp.dma_start(out[P * t:P * (t + 1), :], h_tm[:, t, :]).then_inc(s["stored"], 16)
            sp.wait_ge(s["stored"], 16 * TT)

        def slot_ready(pe, i):
            pe.wait_ge(w_in[i % NSLOT], 16 * (i // NSLOT + 1))

        @block.tensor
        def _(pe):
            pe.wait_ge(s["cact_ready"], 1)
            for i in range(4):
                slot_ready(pe, i)
                w = tiles(slot_view(i)[:, 0:4096], 2)
                for k in range(2):
                    for j in range(16):
                        mm = pe.matmul(bank(7, 1, j), w[:, k, P * j:P * (j + 1)], cact[:, 2 * i + k:2 * i + k + 1],
                                       start=(i == 0 and k == 0 and j == 0), stop=(i == 3 and k == 1),
                                       skip_group_check=True)
                mm.then_inc(w_used, 1)
            pe.wait_ge(w_used, 4)
            pe.sem_inc(s["mod1_done"], 1)
            pe.wait_ge(ld_const, 16)
            pe.wait_ge(s["xhat_ready"], TT)
            for k in range(KT):
                if k >= 4:
                    pe.wait_ge(s["nt_ready"], k - 3)
                for t in range(TT):
                    mm = pe.transpose(bank(k % 4, P, P * t), xhat[:, t, P * k:P * (k + 1)], ident)
                mm.then_inc(s["tr_done"], 1)
            pe.wait_ge(s["nt_ready"], KT)
            pe.wait_ge(ld_ws, 16)

            def square_sums(i):
                pe.wait_ge(s["sq_ready"], i + 1)
                t, b = (i, 6) if i < 5 else (i - 5, 7)
                if i == 5:
                    pe.wait_ge(s["mod1_read"], 1)
                sel = area("const", C_SEL + 16 * t, 16)
                pe.matmul(bank(b, T, 0, 0, 16), sel, sq[i % 2], start=(t == 0), stop=(i in (4, N_STAT - 1)))\
                  .then_inc(s["sq_used"], 1)

            def spread(done, read, i, t, n0):
                if n0 + i >= 2:
                    pass
                sel = area("const", C_SELT + P * t, P, 0, 16)
                pe.matmul(bank(4 + i % 2), sel, st_r, start=True, stop=True).then_inc(done, 1)

            waiting = []
            for j, (kind, slot, i, dst, stat) in enumerate(jobs):
                if kind in "dt" and i == 0:
                    slot_ready(pe, slot)
                if j >= 4:
                    pe.wait_ge(s["proj_out"], j - 3)
                for k in range(KT):
                    if kind == "d":
                        w = slot_view(slot)[:, 0:4096].rearrange("p (i k n) -> p i k n", i=4, k=KT)
                        mm = pe.matmul(bank(j % 4), w[:, i, k, :], n_t[:, k, :], start=(k == 0), stop=(k == KT - 1))
                    elif kind == "t":
                        w = tiles(slot_view(slot)[:, 0:4096], KT)
                        mm = pe.matmul(bank(j % 4), n_t[:, k, P * i:P * (i + 1)], w[:, k, :],
                                       start=(k == 0), stop=(k == KT - 1))
                    elif kind == "s":
                        mm = pe.matmul(bank(j % 4, 68), n_t[:, k, P * i:P * (i + 1)], wsmall[:, k, 0:68],
                                       start=(k == 0), stop=(k == KT - 1))
                    else:
                        mm = pe.matmul(bank(j % 4, T, 0, 0, 16), wsmall[:, k, 68:84], n_t[:, k, :],
                                       start=(k == 0), stop=(k == KT - 1))
                mm.then_inc(s["proj_done"], 1)
                if kind in "dt" and i == 3:
                    pe.wait_ge(s["proj_done"], j + 1)
                    pe.sem_inc(w_used, 1)
                while waiting:
                    square_sums(waiting.pop())
                if stat is not None:
                    waiting.append(stat)
                if j == J_SMALL:
                    pe.wait_ge(s["stat_r"], 1)
                    for t in range(5):
                        if t >= 2:
                            pe.wait_ge(s["xa_read"], t - 1)
                        spread(s["xa_done"], s["xa_read"], t, t, 0)
                    pe.wait_ge(s["proj_out"], J_SMALL + 1)
                    pe.wait_ge(s["xa_read"], 5)
                    m = 0
                    for qt in range(1, TT):
                        for h in range(NI):
                            if m >= 2:
                                pe.wait_ge(s["xi_read"], m - 1)
                            r = HD * (h % 2)
                            pe.matmul(bank(4 + m % 2, P * (qt + 1)), iq[r:r + HD, h // 2, P * qt:P * (qt + 1)],
                                      ik[r:r + HD, 0:P * (qt + 1)], start=True, stop=True).then_inc(s["xi_done"], 1)
                            m += 1
            pe.wait_ge(s["stat_r"], 1)
            for k in range(KT):
                slot_ready(pe, M_SLOTS[0] + k)
                w = slot_view(M_SLOTS[0] + k)
                for j in range(32):
                    mm = pe.matmul(bank(6, 1, j), w[:, P * j:P * (j + 1)], cact[:, k:k + 1],
                                   start=(k == 0 and j == 0), stop=(k == KT - 1), skip_group_check=True)
                mm.then_inc(w_used, 1)
            pe.wait_ge(w_used, M_SLOTS[1])
            pe.sem_inc(s["mod2_done"], 1)
            pe.wait_ge(s["stat_r"], 2)
            pe.wait_ge(s["xi_read"], 12)
            for t in range(8):
                if t >= 2:
                    pe.wait_ge(s["xb_read"], t - 1)
                spread(s["xb_done"], s["xb_read"], t, t, 2)

            pe.wait_ge(s["proj_out"], NJ)
            pe.wait_ge(s["mod2_read"], 1)
            NA = TT * HA
            for it in range(NA + 5):
                if it < NA:
                    qt, h = divmod(it, HA)
                    r = HD * (h % 2)
                    if it == 0:
                        pe.wait_ge(s["xa_read"], 5)
                    if it >= 2:
                        pe.wait_ge(s["la_read"], it - 1)
                    pe.matmul(bank(it % 2, P * (qt + 1)), qa[r:r + HD, h // 2, P * qt:P * (qt + 1)],
                              ka[r:r + HD, 0:P * (qt + 1)], start=True, stop=True).then_inc(s["la_done"], 1)
                if 1 <= it <= NA:
                    j = it - 1
                    qt = j // HA
                    pe.wait_ge(s["prob_ready"], j + 1)
                    if j >= 2:
                        pe.wait_ge(s["pt_out"], j - 1)
                    for st in range(qt + 1):
                        mm = pe.transpose(bank(2 + j % 2, P, P * st), prob[j % 3][:, P * st:P * (st + 1)], ident)
                    mm.then_inc(s["pt_done"], 1)
                if 2 <= it <= NA + 1:
                    j = it - 2
                    qt, h = divmod(j, HA)
                    pe.wait_ge(s["pt_out"], j + 1)
                    if j == 0:
                        pe.wait_ge(s["xb_read"], 8)
                    if h == 0 and qt >= 2:
                        pe.wait_ge(s["o_ready"], qt - 1)
                    for st in range(qt + 1):
                        mm = pe.matmul(bank(4 + qt % 2, HD, HD * h), probT[j % 2][:, P * st:P * (st + 1)],
                                       va[:, st, 0:HD], start=(st == 0), stop=(st == qt))
                    mm.then_inc(s["pv_done"], 1)
                if it >= 4 and (it - 4) % HA == HA - 1:
                    qt = (it - 4) // HA
                    pe.wait_ge(s["o_ready"], qt + 1)
                    if qt >= 1:
                        pe.wait_ge(s["ot_out"], qt)
                    for f in range(4):
                        mm = pe.transpose(bank(6, P, P * f), o_tm[:, P * f:P * (f + 1)], ident)
                    mm.then_inc(s["ot_done"], 1)

            pe.wait_ge(s["ot_out"], TT)
            for it in range(HB + 2):
                if it < HB:
                    r = HD * (it % 2)
                    if it >= 1:
                        pe.wait_ge(s["zb_abs"], it)
                        pe.wait_ge(s["zb_relu"], it)
                        pe.wait_ge(s["zb_min"], it)
                    for st in range(TT):
                        n = T - P * st
                        mm = pe.matmul(ps[:, B_OFF[st]:B_OFF[st] + n], kb[r:r + HD, it // 2, P * st:P * (st + 1)],
                                       qb[r:r + HD, it // 2, P * st:T], start=True, stop=True)
                    mm.then_inc(s["zb_done"], 1)
                if 1 <= it <= HB:
                    h = it - 1
                    pe.wait_ge(s["keep_ready"], h + 1)
                    if h >= 1:
                        pe.wait_ge(s["sum_ready"], h)
                    for st in range(TT):
                        o = 1536 + B_OFF[st]
                        mm = pe.matmul(ps[:, o:o + T - P * st], later_tri, keep[h % 2][:, B_OFF[st]:B_OFF[st] + T - P * st],
                                       start=True, stop=(st == TT - 1), skip_group_check=True)
                        for jt in range(st + 1, TT):
                            mm = pe.matmul(ps[:, o + P * (jt - st):o + T - P * st], ones,
                                           keep[h % 2][:, B_OFF[jt]:B_OFF[jt] + T - P * jt],
                                           start=False, stop=(jt == TT - 1), skip_group_check=True)
                    mm.then_inc(s["lt_done"], 1)
                if it >= 2:
                    h = it - 2
                    pe.wait_ge(s["b_ready"], h + 1)
                    if h % 2 == 0 and h >= 4:
                        pe.wait_ge(s["yb_out"], h // 2 - 1)
                    r = HD * (h % 2)
                    for st in range(TT):
                        mm = pe.matmul(bank(6 + h // 2 % 2, T - P * st, P * st, r, r + HD), vb[:, st, HD * h:HD * (h + 1)],
                                       beta[h % 3][:, B_OFF[st]:B_OFF[st] + T - P * st],
                                       start=(st == 0), stop=(st == TT - 1), skip_group_check=True)
                    mm.then_inc(s["yb_done"], 1)

            pe.wait_ge(ld_wa, 16)
            pe.wait_ge(s["zb_abs"], HB)
            pe.wait_ge(s["zb_relu"], HB)
            pe.wait_ge(s["zb_min"], HB)
            for i in range(2):
                mm = pe.matmul(bank(i), walpha[:, P * i:P * (i + 1)], ca, start=True, stop=True)
            mm.then_inc(s["cu_done"], 1)
            pe.wait_ge(s["cqk_ready"], 1)
            pe.wait_ge(s["sum_ready"], HB)
            for t in range(TT):
                for i in range(2):
                    mm = pe.transpose(bank(4, P, 2 * P * t + P * i), c_qk0[:, 2 * T + T * i + P * t:2 * T + T * i + P * (t + 1)], ident)
            mm.then_inc(s["kdt_done"], 1)
            pe.wait_ge(s["kdt_out"], 1)
            pe.wait_ge(s["cu_ready"], 1)
            kdt = tiles(c_kdt, TT)
            for c in range(NCH):
                for h in range(HC):
                    r, q = CH * (c % 2), HD * (h % 2)
                    o = kv_at(c, h // 2)
                    mm = pe.matmul(ps[q:q + HD, o:o + P], kdt[r:r + CH, c // 2, HD * h:HD * (h + 1)],
                                   vc[r:r + CH, c // 2, CV * h:CV * (h + 1)], start=True, stop=True)
            mm.then_inc(s["kv_done"], 1)
            pe.wait_ge(s["yb_out"], 4)
            for lv in range(len(LEVELS) + 1):
                pe.wait_ge(s["cqk_ready"], min(lv + 2, len(LEVELS) + 1))
                if lv == 1:
                    pe.wait_ge(s["st_ready"], NCH - 1)
                if lv >= 2:
                    pe.wait_ge(s["lev_read"], lv - 1)
                qk = cqk if lv == len(LEVELS) else c_qk[lv % 2]
                base = 2048 if lv % 2 == 0 else 0
                for t in range(TT):
                    for h in range(HC):
                        q = HD * (h % 2)
                        a = T * (h // 2) + P * t
                        mm = pe.matmul(ps[:, base + head_at(t, h):base + head_at(t, h) + P],
                                       qk[q:q + HD, 2 * T + a:2 * T + a + P], qk[q:q + HD, a:a + P],
                                       start=True, stop=True)
                mm.then_inc(s["lev_done"], 1)
            pe.wait_ge(s["lev_read"], len(LEVELS))
            pe.wait_ge(s["att_ready"], 1)
            for t in range(TT):
                for h in range(HC):
                    o = head_at(t, h)
                    pe.matmul(ps[:, o:o + CV], c_att[:, o:o + CV], vc[:, t, CV * h:CV * (h + 1)],
                              start=(t % 2 == 0 and h < 2), stop=True, skip_group_check=True)
            for t in range(TT):
                for c in (2 * t, 2 * t + 1):
                    if c == 0:
                        continue
                    for h in range(HC):
                        r, q = CH * (c % 2), HD * (h % 2)
                        a = T * (h // 2) + CH * c
                        so = 2 * P * c + P * (h // 2)
                        o = head_at(t, h)
                        mm = pe.matmul(ps[r:r + CH, o:o + CV], c_qk0[q:q + HD, a:a + CH],
                                       c_state[q:q + HD, so:so + P], start=False, stop=True, skip_group_check=True)
            mm.then_inc(s["co_done"], 1)
            pe.wait_ge(s["co_ready"], 1)
            for f in range(4):
                for t in range(TT):
                    mm = pe.transpose(bank(4 + f, P, P * t), c_e[:, head_at(t, f):head_at(t, f) + P], ident)
            mm.then_inc(s["yct_done"], 1)

            for n in range(3 * KT):
                c, b = divmod(n, 3)
                if b == 0:
                    slot_ready(pe, G_SLOT + c)
                w = slot_view(G_SLOT + c)[:, 0:WSLOT]
                if n >= 2:
                    pe.wait_ge(s["gate_ready"], n - 1)
                for k in range(KT):
                    o = (b * KT + k) * P
                    mm = pe.matmul(bank(n % 2), w[:, o:o + P], n_t[:, k, :], start=(k == 0), stop=(k == KT - 1))
                mm.then_inc(s["gl_done"], 1)
                if n == 0:
                    pe.wait_ge(s["yct_out"], 1)
                if n >= 2:
                    pe.wait_ge(s["gate_used"], n - 1)
                y = (ya, yb, yc)[b]
                for k in range(4):
                    o = (3 * KT + b * 4 + k) * P
                    mm = pe.matmul(bank(2 + n % 2), w[:, o:o + P], y[:, k, :], start=(k == 0), stop=(k == 3))
                mm.then_inc(s["ob_done"], 1)
                if b == 2:
                    pe.wait_ge(s["ob_done"], n + 1)
                    pe.sem_inc(w_used, 1)

            pe.wait_ge(s["merged_ready"], KT)
            pe.wait_ge(s["ld_x2"], 16)
            pe.wait_ge(s["gate_ready"], 3 * KT)
            for c in range(KT + 1):
                if c < KT:
                    if c % 4 == 0:
                        slot_ready(pe, O_SLOT + c // 4)
                    w = slot_view(O_SLOT + c // 4)[:, 0:4096].rearrange("p (i k n) -> p i k n", i=4, k=KT)
                    if c >= 2:
                        pe.wait_ge(s["yg_ready"], c - 1)
                    for k in range(KT):
                        mm = pe.matmul(bank(4 + c % 2), w[:, c % 4, k, :], merged[:, k, :], start=(k == 0), stop=(k == KT - 1))
                    mm.then_inc(s["yo_done"], 1)
                    if c >= 2:
                        pe.wait_ge(s["ht_ready"], c - 1)
                    for t in range(TT):
                        mm = pe.transpose(bank(6 + c % 2, P, P * t), x_tm[:, t, P * c:P * (c + 1)], ident)
                    mm.then_inc(s["xt_done"], 1)
                    if c % 4 == 3:
                        pe.wait_ge(s["yo_done"], c + 1)
                        pe.sem_inc(w_used, 1)
                if c >= 1:
                    pe.wait_ge(s["hsq_ready"], c)
                    pe.matmul(bank(0), ones, sq[(c - 1) % 2], start=(c == 1), stop=(c == KT)).then_inc(s["hsq_used"], 1)

            def to_tokens(m):
                src, q = (h_t, m) if m < 2 * TT else (n_t, m - 2 * TT)
                if m == 0:
                    pe.wait_ge(s["ht_ready"], KT)
                if m >= 2:
                    pe.wait_ge(s["tm_out"], m - 1)
                for f in range(4):
                    mm = pe.transpose(bank(6 + m % 2, P, P * f), src[:, 4 * (q % 2) + f, P * (q // 2):P * (q // 2 + 1)], ident)
                mm.then_inc(s["tm_done"], 1)

            for m in range(2 * TT):
                to_tokens(m)
            pe.wait_ge(s["n2_ready"], KT)
            pe.wait_ge(s["ld_sk"], 16)
            for i in range(QT + 1):
                if i < QT:
                    if i % 4 == 0:
                        slot_ready(pe, PQ_SLOT + i // 4)
                    w = slot_view(PQ_SLOT + i // 4)[:, 0:4096].rearrange("p (i k n) -> p i k n", i=4, k=KT)
                    if i >= 2:
                        pe.wait_ge(s["pq_out"], i - 1)
                    for k in range(KT):
                        mm = pe.matmul(bank(1 + i % 2), w[:, i % 4, k, :], n_t[:, k, :], start=(k == 0), stop=(k == KT - 1))
                    mm.then_inc(s["pq_done"], 1)
                    if i % 4 == 3:
                        pe.wait_ge(s["pq_done"], i + 1)
                        pe.sem_inc(w_used, 1)
                if i >= 1:
                    j = i - 1
                    pe.wait_ge(s["pq_out"], j + 1)
                    if j >= 2:
                        pe.wait_ge(s["sc_out"], j - 1)
                    for t in range(TT):
                        mm = pe.matmul(bank(4 + j % 2, P, P * t), qp[j % 2][:, P * t:P * (t + 1)], sk[:, j, :],
                                       start=True, stop=True)
                    mm.then_inc(s["sc_done"], 1)
                if i < 2 * TT:
                    to_tokens(2 * TT + i)
            pe.wait_ge(s["g2t_ready"], 1)
            pe.wait_ge(s["pq_out"], QT)
            for c in range(KT):
                mm = pe.matmul(ps[:, 512 + P * c:512 + P * (c + 1)], g2tmp[:, c, :], ident, start=True, stop=True)
            mm.then_inc(s["g2_done"], 1)
            pe.wait_ge(s["g2_ready"], 1)

            def weigh(u, par):
                for i in range(PK):
                    pe.wait_ge(s["dg_ready"], u * PK + i + 1)
                    pe.wait_ge(v_in[i % R], (u * (PK // R) + i // R + 1) * 16)
                    for f in range(2):
                        mm = pe.matmul(bank(2 * par + f), dgw[i % 4], v_ring[i % R][:, T * f:T * (f + 1)],
                                       start=(i == 0), stop=(i == PK - 1))
                    if i == PK - 1:
                        mm.then_inc(s["acc_done"], 1)
                        pe.wait_ge(s["acc_done"], u + 1)
                        pe.sem_inc(s["dg_used"], 1)
                    else:
                        mm.then_inc(s["dg_used"], 1)

            weigh(0, 0)
            weigh(1, 1)
            with pe.Fori(1, NU // 2) as b:
                for par in range(2):
                    u = b * 2 + par
                    pe.wait_ge(s["added"], u - 1)
                    weigh(u, par)

        @block.scalar
        def _(act):
            act.wait_ge(ld_vec, 16)
            act.activation(ct1[:, 0:8], vcol(V_C, 8), ACT.Sigmoid).then_inc(s["csig"], 1)
            act.wait_ge(ld_x, 16)
            for t in range(TT):
                act.activation(area("ya", D * t, D), x_tm[:, t, :], ACT.Square, accum_out=xss[:, t:t + 1])\
                   .then_inc(s["xss_ready"], 1)
            act.wait_ge(s["xvar_ready"], 1)
            act.activation(xrt, xvar, ACT.Sqrt).then_inc(s["xrt_ready"], 1)
            for j, (kind, slot, i, dst, stat) in enumerate(jobs):
                act.wait_ge(s["proj_done"], j + 1)
                if kind == "d":
                    o = area(dst[0], T * dst[1], T)
                    scale = HD ** -0.5 if dst[0] == "cq" else 1.0
                    c = act.activation(o, bank(j % 4), ACT.Copy, scale=scale)
                    if stat is not None:
                        if stat >= 2:
                            act.wait_ge(s["sq_used"], stat - 1)
                        act.activation(sq[stat % 2], bank(j % 4), ACT.Square).then_inc(s["sq_ready"], 1)
                        act.wait_ge(s["sq_ready"], stat + 1)
                        act.sem_inc(s["proj_out"], 1)
                    else:
                        c.then_inc(s["proj_out"], 1)
                elif kind == "t":
                    act.activation(area(dst, T * i, T), bank(j % 4), ACT.Copy).then_inc(s["proj_out"], 1)
                elif kind == "s":
                    act.activation(va[:, i, :], bank(j % 4, 68), ACT.Copy).then_inc(s["proj_out"], 1)
                else:
                    act.activation(ca, bank(j % 4, T, 0, 0, 16), ACT.Copy).then_inc(s["proj_out"], 1)
                if j == J_SMALL:
                    act.wait_ge(s["stat_var"], 1)
                    act.activation(st_rt, st_var, ACT.Sqrt).then_inc(s["stat_rt"], 1)
                    for m in range(12):
                        w = P * (m // NI + 2)
                        act.wait_ge(s["xi_done"], m + 1)
                        if m >= 2:
                            act.wait_ge(s["irelu_used"], m - 1)
                        act.activation(irelu[m % 2][:, 0:w], bank(4 + m % 2, w), ACT.Relu).then_inc(s["xi_read"], 1)
            act.wait_ge(s["stat_var"], 2)
            act.activation(st_rt, st_var, ACT.Sqrt).then_inc(s["stat_rt"], 1)

            NA = TT * HA
            for it in range(NA + 5):
                if it < NA:
                    n = P * (it // HA + 1)
                    act.wait_ge(s["nmax_ready"], it + 1)
                    act.activation(prob[it % 3][:, 0:n], prob[it % 3][:, 0:n], ACT.Exp, bias=anmax[:, it:it + 1],
                                   accum_out=asum[:, it:it + 1]).then_inc(s["prob_ready"], 1)
                if 1 <= it <= NA:
                    j = it - 1
                    n = P * (j // HA + 1)
                    act.wait_ge(s["pt_done"], j + 1)
                    if j >= 2:
                        act.wait_ge(s["pv_done"], j - 1)
                    act.activation(probT[j % 2][:, 0:n], bank(2 + j % 2, n), ACT.Copy).then_inc(s["pt_out"], 1)
                if it >= 4 and (it - 4) % HA == HA - 1:
                    qt = (it - 4) // HA
                    act.wait_ge(s["ot_done"], qt + 1)
                    if qt == 0:
                        act.wait_ge(s["stat_r"], 2)
                        act.wait_ge(s["xb_read"], 8)
                    act.activation(ya[:, :, P * qt:P * (qt + 1)], tiles(bank(6), 4), ACT.Copy).then_inc(s["ot_out"], 1)

            for it in range(HB + 2):
                if it < HB:
                    z = ps[:, 0:B_COLS]
                    sp_, kp = spb[it % 2], keep[it % 2]
                    act.wait_ge(s["zb_done"], it + 1)
                    if it >= 2:
                        act.wait_ge(s["keep_ready"], it - 1)
                        act.wait_ge(s["beta_ready"], it - 1)
                    act.activation(sp_, z, ACT.Abs, scale=HD ** -0.5).then_inc(s["zb_abs"], 1)
                    if it >= 2:
                        act.wait_ge(s["lt_done"], it - 1)
                    act.activation(kp, z, ACT.Relu, scale=HD ** -0.5).then_inc(s["zb_relu"], 1)
                    act.wait_ge(s["zb_abs"], it + 1)
                    act.activation(sp_, sp_, ACT.Exp, scale=-1.0).then_inc(s["b_exp"], 1)
                    act.wait_ge(s["b_exp"], it + 1)
                    act.activation(sp_, sp_, ACT.Ln, bias=1.0).then_inc(s["sp_ready"], 1)
                if 1 <= it <= HB:
                    h = it - 1
                    act.wait_ge(s["sum_ready"], h + 1)
                    act.activation(beta[h % 3], beta[h % 3], ACT.Exp).then_inc(s["a_exp"], 1)
                if it >= 2 and it % 2 == 1:
                    h = it - 2
                    act.wait_ge(s["yb_done"], h + 1)
                    act.activation(yb[:, h // 2, :], bank(6 + h // 2 % 2), ACT.Copy).then_inc(s["yb_out"], 1)

            act.activation(area("rc", 0, TT * T), area("rc", 0, TT * T), ACT.Silu).then_inc(s["rsil"], 1)
            act.wait_ge(s["cu_ready"], 1)
            sp_ = c_e[:, 2 * T:4 * T]
            act.activation(sp_, c_e[:, 0:2 * T], ACT.Abs).then_inc(s["cabs"], 1)
            act.wait_ge(s["cabs"], 1)
            act.activation(sp_, sp_, ACT.Exp, scale=-1.0).then_inc(s["cabs"], 1)
            act.wait_ge(s["cabs"], 2)
            act.activation(sp_, sp_, ACT.Ln, bias=1.0).then_inc(s["csp"], 1)
            act.wait_ge(s["cb_ready"], 1)
            act.activation(tiles(ebl, 2), c_b.rearrange("p (i c l) -> p i c l", i=2, l=CH)[:, :, :, CH - 1], ACT.Exp,
                           scale=1 / TAU).then_inc(s["ebl_ready"], 1)
            for lv in range(len(LEVELS) + 1):
                act.wait_ge(s["ce_ready"], lv + 1)
                act.activation(c_e, c_e, ACT.Exp, scale=1 / TAU).then_inc(s["cex_ready"], 1)
                if lv == 1:
                    act.wait_ge(s["kdt_done"], 1)
                    act.activation(c_kdt, ps[:, 2048:2048 + 2 * T], ACT.Copy).then_inc(s["kdt_out"], 1)
            act.wait_ge(s["co_done"], 1)
            act.activation(c_e, ps[:, 0:4 * T], ACT.Square).then_inc(s["css_ready"], 1)
            act.wait_ge(s["cvar_ready"], 1)
            act.activation(crt, cvar, ACT.Sqrt).then_inc(s["crt_ready"], 1)
            act.wait_ge(s["yct_done"], 1)
            act.activation(area("yc", 0, 4 * T), ps[:, 2048:4096], ACT.Copy).then_inc(s["yct_out"], 1)

            for n in range(3 * KT):
                c, b = divmod(n, 3)
                act.wait_ge(s["gl_done"], n + 1)
                if n >= 2:
                    act.wait_ge(s["gate_used"], n - 1)
                act.activation(gates[n % 2], bank(n % 2), ACT.Sigmoid, bias=vcol(V_BG + b * KT + c))\
                   .then_inc(s["gate_ready"], 1)

            for c in range(KT + 1):
                if c < KT:
                    act.wait_ge(s["yo_done"], c + 1)
                    if c >= 2:
                        act.wait_ge(s["ht_ready"], c - 1)
                    act.activation(yg[c % 2], bank(4 + c % 2), ACT.Copy, scale=mcol(GT1 + c)).then_inc(s["yg_ready"], 1)
                if c >= 1:
                    act.wait_ge(s["ht_ready"], c)
                    if c >= 3:
                        act.wait_ge(s["hsq_used"], c - 2)
                    act.activation(sq[(c - 1) % 2], h_t[:, c - 1, :], ACT.Square).then_inc(s["hsq_ready"], 1)

            def tokens_out(m):
                act.wait_ge(s["tm_done"], m + 1)
                dst, q = (h_tm, m) if m < 2 * TT else (n2_tm, m - 2 * TT)
                act.activation(dst[:, q // 2, T * (q % 2):T * (q % 2 + 1)], bank(6 + m % 2), ACT.Copy).then_inc(s["tm_out"], 1)

            act.wait_ge(s["nvar_ready"], 1)
            act.activation(nrt, nvar, ACT.Sqrt).then_inc(s["nrt_ready"], 1)
            for m in range(2 * TT):
                tokens_out(m)
            for i in range(QT):
                act.wait_ge(s["pq_done"], i + 1)
                if i >= 2:
                    act.wait_ge(s["sc_done"], i - 1)
                act.activation(qp[i % 2], bank(1 + i % 2), ACT.Copy).then_inc(s["pq_out"], 1)
                if i < 2 * TT:
                    tokens_out(2 * TT + i)

            def norm_of(u, par):
                src = area("vb", 0, TT * D)[:, bass.ds(u // PH * D, D)]
                act.activation(n2_cur[par], src, ACT.Copy).then_inc(s["n2c_ready"], 1)

            def weights(u, par):
                act.wait_ge(s["dots_ready"], u + 1)
                act.activation(gelu[par], dots[par], ACT.Gelu).then_inc(s["gelu_ready"], 1)
                act.activation(ebest[par], best_all[:, bass.ds(u * PK, PK)], ACT.Exp, accum_out=zsum[par]).then_inc(s["z_ready"], 1)

            def diagonals(u, par, first=False):
                act.wait_ge(s["w_ready"], u + 1)
                for i in range(PK):
                    if not (first and i < 4):
                        act.wait_ge(s["dg_used"], u * PK + i - 3)
                    act.activation(dgw[i % 4], ident, ACT.Copy, scale=wgt[par][:, i:i + 1]).then_inc(s["dg_ready"], 1)

            act.wait_ge(s["tm_out"], 4 * TT)
            act.wait_ge(s["picked"], 1)
            norm_of(0, 0)
            norm_of(1, 1)
            weights(0, 0)
            diagonals(0, 0, True)
            with act.Fori(0, NU // 2 - 1) as b:
                for par in (1, 0):
                    u = b * 2 + (1 if par else 2)
                    act.wait_ge(s["dots_ready"], u)
                    norm_of(u + 1, 1 - par)
                    weights(u, par)
                    diagonals(u, par)
            weights(NU - 1, 1)
            diagonals(NU - 1, 1)

        @block.vector
        def _(dve):
            def done(ins):
                v_count[0] += 1
                ins.then_inc(v_step, 1)
                dve.wait_ge(v_step, v_count[0])

            v_count = [0]

            def inverse_root(r, root, var, tmp):
                done(dve.reciprocal(r, root))
                done(dve.tensor_tensor(tmp, r, r, ALU.mult))
                done(dve.tensor_tensor(tmp, tmp, var, ALU.mult))
                done(dve.tensor_scalar(tmp, tmp, -0.5, 1.5, ALU.mult, ALU.add))
                return dve.tensor_tensor(r, r, tmp, ALU.mult)

            dve.wait_ge(s["csig"], 1)
            dve.tensor_tensor(cact, vcol(V_C, 8), ct1[:, 0:8], ALU.mult).then_inc(s["cact_ready"], 1)
            dve.wait_ge(s["xss_ready"], TT)
            dve.tensor_scalar(xvar, xss, 1 / D, EPS, ALU.mult, ALU.add).then_inc(s["xvar_ready"], 1)
            dve.wait_ge(s["xrt_ready"], 1)
            done(inverse_root(xr, xrt, xvar, xt1))
            for t in range(TT):
                dve.tensor_scalar(xhat[:, t, :], x_tm[:, t, :], xr[:, t:t + 1], None, ALU.mult).then_inc(s["xhat_ready"], 1)
            dve.wait_ge(s["mod1_done"], 1)
            dve.tensor_tensor(mcol(0, 16), bank(7, 16), vcol(V_BMOD, 16), ALU.add).then_inc(s["mod1_read"], 1)
            dve.wait_ge(s["mod1_read"], 1)
            done(dve.scalar_tensor_tensor(amp1, mcol(SC1, 8), 1.0, vcol(V_G1, 8), ALU.add, ALU.mult))
            for k in range(KT):
                dve.wait_ge(s["tr_done"], k + 1)
                dve.tensor_scalar(n_t[:, k, :], bank(k % 4), amp1[:, k:k + 1], mcol(SH1 + k), ALU.mult, ALU.add)\
                   .then_inc(s["nt_ready"], 1)

            def head_factors(n, b):
                dve.wait_ge(s["sq_used"], (5, N_STAT)[n - 1])
                dve.tensor_scalar(st_var, bank(b, T, 0, 0, 16), 1 / HD, EPS, ALU.mult, ALU.add).then_inc(s["stat_var"], 1)
                dve.wait_ge(s["stat_rt"], n)
                inverse_root(st_r, st_rt, st_var, st_t).then_inc(s["stat_r"], 1)

            head_factors(1, 6)
            dve.wait_ge(s["proj_out"], 5)
            for t in range(5):
                dst = qa[:, t, :] if t < 4 else ka
                dve.wait_ge(s["xa_done"], t + 1)
                dve.scalar_tensor_tensor(dst, dst, vcol(V_GAIN + t // 4), bank(4 + t % 2), ALU.mult, ALU.mult)\
                   .then_inc(s["xa_read"], 1)
            m = 0
            for qt in range(1, TT):
                for h in range(NI):
                    dve.wait_ge(s["xi_read"], m + 1)
                    wcol = va[:, qt, HD + h:HD + h + 1]
                    if h == 0:
                        ins = dve.tensor_scalar(pen(qt), irelu[m % 2][:, 0:P * (qt + 1)], wcol, None, ALU.mult)
                    else:
                        dve.wait_ge(s["irelu_used"], m)
                        ins = dve.scalar_tensor_tensor(pen(qt), irelu[m % 2][:, 0:P * (qt + 1)], wcol, pen(qt),
                                                       ALU.mult, ALU.add)
                    ins.then_inc(s["irelu_used"], 1)
                    m += 1
            dve.wait_ge(s["irelu_used"], m)
            for qt in range(1, TT):
                done(dve.memset(pen(qt)[0:CH, P * qt + CH:P * (qt + 1)], HIDDEN))
            for qt in range(1, TT):
                for r in range(TOPK // 8):
                    done(dve.max(out=top8, in_=pen(qt)))
                    done(dve.match_replace(out=pen(qt), in_to_replace=top8, in_values=pen(qt), imm_value=PICKED))
                done(dve.tensor_scalar(pen(qt), pen(qt), (HIDDEN + PICKED) / 2, MASKED, ALU.is_gt, ALU.mult))
            done(dve.memset(pen(0), 0.0))
            done(dve.memset(pen(0)[0:CH, CH:P], MASKED))
            head_factors(2, 7)
            for t in range(8):
                dst = (qb, kb)[t // 4][:, t % 4, :]
                dve.wait_ge(s["xb_done"], t + 1)
                dve.scalar_tensor_tensor(dst, dst, vcol(V_GAIN + 2 + t // 4), bank(4 + t % 2), ALU.mult, ALU.mult)\
                   .then_inc(s["xb_read"], 1)
            dve.wait_ge(s["mod2_done"], 1)
            dve.tensor_tensor(mcol(16, 32), bank(6, 32), vcol(V_BMOD + 16, 32), ALU.add).then_inc(s["mod2_read"], 1)
            dve.wait_ge(s["mod2_read"], 1)
            done(dve.scalar_tensor_tensor(amp2, mcol(SC2, 8), 1.0, vcol(V_G2, 8), ALU.add, ALU.mult))

            NA = TT * HA
            for it in range(NA + 3):
                if it < NA:
                    qt = it // HA
                    n = P * (qt + 1)
                    dve.wait_ge(s["la_done"], it + 1)
                    if it >= 3:
                        dve.wait_ge(s["pt_done"], it - 2)
                    dve.tensor_tensor_reduce(out=prob[it % 3][:, 0:n], in0=bank(it % 2, n), in1=pen(qt),
                                             scale=HD ** -0.5, scalar=-3.4e38, op0=ALU.add, op1=ALU.max,
                                             accum_out=amax[:, it:it + 1]).then_inc(s["la_read"], 1)
                    dve.wait_ge(s["la_read"], it + 1)
                    dve.tensor_scalar(anmax[:, it:it + 1], amax[:, it:it + 1], -1.0, None, ALU.mult).then_inc(s["nmax_ready"], 1)
                if it >= 3 and (it - 3) % HA == HA - 1:
                    qt = (it - 3) // HA
                    c = slice(HA * qt, HA * (qt + 1))
                    dve.wait_ge(s["prob_ready"], HA * (qt + 1))
                    done(dve.reciprocal(arcp[:, c], asum[:, c]))
                    dve.wait_ge(s["pv_done"], HA * (qt + 1))
                    if qt >= 1:
                        dve.wait_ge(s["ot_done"], qt)
                    dve.tensor_tensor(tiles(o_tm, HA), tiles(bank(4 + qt % 2), HA),
                                      arcp[:, c].unsqueeze(2).broadcast_to([P, HA, HD]), ALU.mult).then_inc(s["o_ready"], 1)

            dve.wait_ge(s["ot_out"], TT)
            for it in range(HB + 1):
                if it < HB:
                    z = ps[:, 0:B_COLS]
                    kp, bt, sp_ = keep[it % 2], beta[it % 3], spb[it % 2]
                    dve.wait_ge(s["zb_relu"], it + 1)
                    if it >= 3:
                        dve.wait_ge(s["yb_done"], it - 2)
                    dve.tensor_scalar(bt, z, HD ** -0.5, 0.0, ALU.mult, ALU.min).then_inc(s["zb_min"], 1)
                    dve.wait_ge(s["sp_ready"], it + 1)
                    done(dve.scalar_tensor_tensor(kp, kp, -1.0, sp_, ALU.mult, ALU.subtract))
                    for st in range(TT):
                        d = kp[:, B_OFF[st]:B_OFF[st] + P]
                        ins = dve.tensor_tensor(d, d, past_tri, ALU.mult)
                    ins.then_inc(s["keep_ready"], 1)
                if it >= 1:
                    h = it - 1
                    dve.wait_ge(s["lt_done"], h + 1)
                    dve.wait_ge(s["beta_ready"], h + 1)
                    dve.tensor_tensor(beta[h % 3], beta[h % 3], ps[:, 1536:1536 + B_COLS], ALU.add).then_inc(s["sum_ready"], 1)

            dve.wait_ge(s["cu_done"], 1)
            dve.wait_ge(s["yb_done"], HB)
            for i in range(2):
                u = dve.tensor_scalar(c_e[:, T * i:T * (i + 1)], bank(i), vcol(V_BA + i), None, ALU.add)
            u.then_inc(s["cu_ready"], 1)
            dve.wait_ge(s["cabs"], 1)
            done(dve.tensor_scalar(c_e[:, 0:2 * T], c_e[:, 0:2 * T], 0.0, None, ALU.min))
            dve.wait_ge(s["csp"], 1)
            done(dve.tensor_tensor(c_e[:, 0:2 * T], c_e[:, 0:2 * T], c_e[:, 2 * T:4 * T], ALU.subtract))
            for i in range(2):
                last = dve.tensor_tensor_scan(c_b[:, T * i:T * (i + 1)], reset, c_e[:, T * i:T * (i + 1)], 0.0,
                                              ALU.mult, ALU.add)
            last.then_inc(s["cb_ready"], 1)
            dve.wait_ge(s["cb_ready"], 1)
            bch = c_b.rearrange("p (c l) -> p c l", l=CH)
            dve.tensor_copy(c_e[:, 0:2 * T], c_b)
            dve.tensor_tensor(c_e[:, 2 * T:4 * T].rearrange("p (c l) -> p c l", l=CH),
                              bch[:, :, CH - 1:CH].broadcast_to([P, 2 * NCH, CH]), bch, ALU.subtract).then_inc(s["ce_ready"], 1)
            dve.wait_ge(s["cex_ready"], 1)
            dve.tensor_tensor(c_qk0, cqk, c_e, ALU.mult).then_inc(s["cqk_ready"], 1)
            dve.wait_ge(s["cqk_ready"], 1)

            def level(lv):
                w = LEVELS[lv]
                e0 = c_e[:, 0:2 * T].rearrange("p (c l) -> p c l", l=2 * w)
                bb = c_b.rearrange("p (c l) -> p c l", l=2 * w)
                done(dve.tensor_tensor(e0, bb, bb[:, :, w - 1:w].broadcast_to([P, T // w, 2 * w]), ALU.subtract))
                done(dve.tensor_scalar(c_e[:, 2 * T:4 * T], c_e[:, 0:2 * T], -1.0, 0.0, ALU.mult, ALU.min))
                dve.tensor_scalar(c_e[:, 0:2 * T], c_e[:, 0:2 * T], 0.0, None, ALU.min).then_inc(s["ce_ready"], 1)
                dve.wait_ge(s["cex_ready"], lv + 2)
                if lv >= 2:
                    dve.wait_ge(s["lev_done"], lv - 1)
                dve.tensor_tensor(c_qk[lv % 2], cqk, c_e, ALU.mult).then_inc(s["cqk_ready"], 1)
                dve.wait_ge(s["cqk_ready"], lv + 2)

            def level_read(lv):
                base = 2048 if lv % 2 == 0 else 0
                m = area("const", C_LEVEL + P * lv, P).bitcast(U32)
                dve.wait_ge(s["lev_done"], lv + 1)
                dve.copy_predicated(out=tiles(c_att, 16), mask=m.unsqueeze(1).broadcast_to([P, 16, P]),
                                    data=tiles(ps[:, base:base + 2048], 16)).then_inc(s["lev_read"], 1)
                dve.wait_ge(s["lev_read"], lv + 1)

            level(0)
            level(1)
            dve.wait_ge(s["kv_done"], 1)
            dve.wait_ge(s["ebl_ready"], 1)
            for c in range(1, NCH):
                for i in range(2):
                    new = c_state[:, 2 * P * c + P * i:2 * P * c + P * (i + 1)]
                    old = c_state[:, 2 * P * (c - 1) + P * i:2 * P * (c - 1) + P * (i + 1)]
                    kv = ps[:, kv_at(c - 1, i):kv_at(c - 1, i) + P]
                    if c == 1:
                        ins = dve.tensor_copy(new, kv)
                    else:
                        ins = dve.scalar_tensor_tensor(new, old, ebl[:, NCH * i + c - 1:NCH * i + c], kv, ALU.mult, ALU.add)
                ins.then_inc(s["st_ready"], 1)
                dve.wait_ge(s["st_ready"], c)
            dve.wait_ge(s["att_zero"], 1)
            for lv in range(len(LEVELS) + 1):
                level_read(lv)
                if lv + 2 < len(LEVELS):
                    level(lv + 2)
            dve.sem_inc(s["att_ready"], 1)
            dve.wait_ge(s["css_ready"], 1)
            done(dve.tensor_reduce(css, tiles(c_e, 16), AX, ALU.add))
            dve.tensor_scalar(cvar, css, 1 / CV, EPS, ALU.mult, ALU.add).then_inc(s["cvar_ready"], 1)
            dve.wait_ge(s["crt_ready"], 1)
            done(inverse_root(crs, crt, cvar, ct1))
            done(dve.tensor_tensor(tiles(c_e, 16), tiles(ps[:, 0:4 * T], 16), crs.unsqueeze(2).broadcast_to([P, 16, CV]),
                                   ALU.mult))
            dve.wait_ge(s["rgain"], 1)
            for b in range(2):
                e = c_e[:, 2 * T * b:2 * T * (b + 1)].rearrange("p (t a v) -> p t a v", t=TT, v=CV)
                g = area("rc", 0, TT * T).rearrange("p (t a b v) -> p t a b v", t=TT, b=2, v=CV)[:, :, :, b, :]
                ins = dve.tensor_tensor(e, e, g, ALU.mult)
            ins.then_inc(s["co_ready"], 1)

            for n in range(3 * KT):
                c, b = divmod(n, 3)
                dve.wait_ge(s["gate_ready"], n + 1)
                dve.wait_ge(s["ob_done"], n + 1)
                if b == 0:
                    done(dve.tensor_tensor(merged[:, c, :], gates[n % 2], bank(2 + n % 2), ALU.mult))
                    dve.sem_inc(s["gate_used"], 1)
                else:
                    dve.tensor_tensor(gated, gates[n % 2], bank(2 + n % 2), ALU.mult).then_inc(s["gate_used"], 1)
                    dve.wait_ge(s["gate_used"], n + 1)
                    done(dve.tensor_tensor(merged[:, c, :], merged[:, c, :], gated, ALU.add))
                if b == 2:
                    dve.sem_inc(s["merged_ready"], 1)

            for c in range(KT):
                dve.wait_ge(s["yg_ready"], c + 1)
                dve.wait_ge(s["xt_done"], c + 1)
                dve.tensor_tensor(h_t[:, c, :], yg[c % 2], bank(6 + c % 2), ALU.add).then_inc(s["ht_ready"], 1)
            dve.wait_ge(s["hsq_used"], KT)
            dve.tensor_scalar(nvar, bank(0), 1 / D, EPS, ALU.mult, ALU.add).then_inc(s["nvar_ready"], 1)
            dve.wait_ge(s["nrt_ready"], 1)
            done(inverse_root(nr, nrt, nvar, ntmp))
            for c in range(KT):
                done(dve.scalar_tensor_tensor(n_t[:, c, :], h_t[:, c, :], amp2[:, c:c + 1], nr, ALU.mult, ALU.mult))
                dve.tensor_scalar(n_t[:, c, :], n_t[:, c, :], mcol(SH2 + c), None, ALU.add).then_inc(s["n2_ready"], 1)
            for c in range(KT):
                ins = dve.tensor_scalar(g2tmp[:, c, :], ones, mcol(GT2 + c), None, ALU.mult)
            ins.then_inc(s["g2t_ready"], 1)
            by_tile = scores.rearrange("p (t n) -> p t n", t=TT)
            for j in range(QT):
                dve.wait_ge(s["sc_done"], j + 1)
                dve.tensor_copy(by_tile[:, :, NK * j:NK * (j + 1)], tiles(bank(4 + j % 2), TT)).then_inc(s["sc_out"], 1)
            dve.wait_ge(s["g2_done"], 1)
            dve.tensor_copy(g2row, ps[:, 512:512 + D]).then_inc(s["g2_ready"], 1)

            k = pick
            P_COUNT = []
            iota = area("const", C_IOTA, 16)

            def pick_experts(u):
                n = [0]
                base = u * PICK_STEPS

                def step(ins, own=False):
                    n[0] += 1
                    ins.then_inc(s["p_step"], 1)
                    dve.wait_ge(s["p_step"], base + n[0])
                    if own:
                        dve.sem_inc(s["p_go"], 1)

                step(dve.tensor_copy(k["sc"], scores[:, bass.ds(u * 2 * NK, 2 * NK)]), own=True)
                for c in range(2):
                    row, left = k["sc"][:, NK * c:NK * (c + 1)], k["left"][:, NK * c:NK * (c + 1)]
                    t0, t1 = k["top"][:, 16 * c:16 * c + 8], k["top"][:, 16 * c + 8:16 * c + 16]
                    step(dve.max(out=t0, in_=row), own=True)
                    dve.max_index(out=ix_u[:, 16 * c:16 * c + 8], in_max=t0, in_values=row)
                    step(dve.match_replace(out=left, in_to_replace=t0, in_values=row, imm_value=PICKED), own=True)
                    step(dve.max(out=t1, in_=left), own=True)
                    step(dve.max_index(out=ix_u[:, 16 * c + 8:16 * c + 16], in_max=t1, in_values=left), own=True)
                step(dve.tensor_tensor(tiles(k["cand"], 16), k["top"][:, 0:16].unsqueeze(2).broadcast_to([P, 16, 16]),
                                       k["top"][:, 16:32].unsqueeze(1).broadcast_to([P, 16, 16]), ALU.add), own=True)
                b0, b1 = k["best"][:, 0:8], k["best"][:, 8:16]
                step(dve.max(out=b0, in_=k["cand"]), own=True)
                dve.max_index(out=bj_u[:, 0:8], in_max=b0, in_values=k["cand"])
                step(dve.match_replace(out=k["cleft"], in_to_replace=b0, in_values=k["cand"], imm_value=PICKED), own=True)
                step(dve.max(out=b1, in_=k["cleft"]), own=True)
                step(dve.max_index(out=bj_u[:, 8:16], in_max=b1, in_values=k["cleft"]))
                dve.tensor_scalar(hl_u[:, 0:16], bj_u, 4, None, ALU.logical_shift_right)
                step(dve.tensor_scalar(hl_u[:, 16:32], bj_u, 15, None, ALU.bitwise_and))
                dve.tensor_copy(k["hl"], hl_u)
                step(dve.tensor_copy(k["ixf"], ix_u))
                step(dve.tensor_tensor(tiles(k["eq"], 32), iota.unsqueeze(1).broadcast_to([P, 32, 16]),
                                       k["hl"].unsqueeze(2).broadcast_to([P, 32, 16]), ALU.is_equal))
                e = k["eq"].rearrange("p (c j a) -> p c j a", c=2, j=16)
                step(dve.tensor_tensor(e, e, tiles(k["ixf"], 2).unsqueeze(2).broadcast_to([P, 2, 16, 16]), ALU.mult))
                step(dve.tensor_reduce(k["ef"], tiles(k["eq"], 32), AX, ALU.add))
                dve.scalar_tensor_tensor(idx_all[:, bass.ds(u * PK, PK)], k["ef"][:, 0:16], float(NK), k["ef"][:, 16:32],
                                         ALU.mult, ALU.add)
                step(dve.tensor_scalar(best_all[:, bass.ds(u * PK, PK)], k["best"], k["best"][:, 0:1], None, ALU.subtract))
                dve.sem_inc(s["picked"], 1)
                assert n[0] == PICK_STEPS

            def dot(u, par):
                dve.wait_ge(s["n2c_ready"], u + 1)
                for i in range(PK):
                    dve.wait_ge(u_in[i % R], (u * (PK // R) + i // R + 1) * 16)
                    dve.tensor_tensor_reduce(out=u_ring[i % R], in0=u_ring[i % R], in1=n2_cur[par], scale=1.0, scalar=0.0,
                                             op0=ALU.mult, op1=ALU.add, accum_out=dots[par][:, i:i + 1]).then_inc(s["u_used"], 1)
                dve.wait_ge(s["u_used"], (u + 1) * PK)
                dve.sem_inc(s["dots_ready"], 1)

            def weight(u, par):
                dve.wait_ge(s["z_ready"], u + 1)
                dve.reciprocal(zinv[par], zsum[par]).then_inc(s["zi_ready"], 1)
                dve.wait_ge(s["zi_ready"], u + 1)
                dve.wait_ge(s["gelu_ready"], u + 1)
                dve.scalar_tensor_tensor(wgt[par], gelu[par], zinv[par], ebest[par], ALU.mult, ALU.mult).then_inc(s["w_ready"], 1)

            def add(u, par):
                dve.wait_ge(s["acc_done"], u + 1)
                dve.tensor_tensor(acc_tmp, ps[:, D * par:D * (par + 1)], g2row, ALU.mult).then_inc(s["gated2"], 1)
                dve.wait_ge(s["gated2"], u + 1)
                at = area("x", 0, TT * D)[:, bass.ds(u // PH * D, D)]
                dve.tensor_tensor(at, at, acc_tmp, ALU.add).then_inc(s["added"], 1)
                dve.wait_ge(s["added"], u + 1)

            for u in range(3):
                pick_experts(u)
            dot(0, 0)
            weight(0, 0)
            dve.wait_ge(s["tm_out"], 4 * TT)
            with dve.Fori(0, NU // 2 - 2) as b:
                for par in (1, 0):
                    u = b * 2 + (1 if par else 2)
                    dot(u, par)
                    pick_experts(u + 2)
                    weight(u, par)
                    add(u - 1 + 0, 1 - par)
            for u in (NU - 3, NU - 2, NU - 1):
                dot(u, u % 2)
                if u == NU - 3:
                    pick_experts(NU - 1)
                weight(u, u % 2)
                add(u - 1, (u - 1) % 2)
            add(NU - 1, 1)

        @block.gpsimd
        def _(pool):
            for it in range(HB + 1):
                if it < HB:
                    pool.wait_ge(s["zb_min"], it + 1)
                    pool.wait_ge(s["sp_ready"], it + 1)
                    pool.tensor_tensor(beta[it % 3], beta[it % 3], spb[it % 2], ALU.subtract).then_inc(s["beta_ready"], 1)
                if it >= 1:
                    h = it - 1
                    pool.wait_ge(s["a_exp"], h + 1)
                    for st in range(TT):
                        d = beta[h % 3][:, B_OFF[st]:B_OFF[st] + P]
                        ins = pool.tensor_tensor(d, d, past_tri, ALU.mult)
                    ins.then_inc(s["b_ready"], 1)
            pool.wait_ge(s["zb_done"], HB)
            pool.memset(c_att, 0.0).then_inc(s["att_zero"], 1)
            pool.wait_ge(s["rsil"], 1)
            pool.tensor_tensor(rc, rc, vcol(V_ONG, T).unsqueeze(1).broadcast_to([P, TT, T]), ALU.mult).then_inc(s["rgain"], 1)

            def gather(table, idx, ring, arrived, used, u, first):
                for i in range(PK):
                    if i % 4 == 0 and not (first and i < R):
                        pool.wait_ge(used, u * PK + i + 4 - R)
                        pool.sem_inc(s["pool_go"], 1)
                    pool.indirect_dma_start(out=ring[i % R], out_offset=None, in_=table,
                                            in_offset=bass.IndirectOffsetOnAxis(ap=idx[:, i:i + 1], axis=0))\
                        .then_inc(arrived[i % R], 16)

            def rows_u(u, par, first=False):
                pool.wait_ge(s["picked"], u + 1)
                pool.sem_inc(s["pool_go"], 1)
                pool.tensor_copy(idx_u[par], idx_all[:, bass.ds(u * PK, PK)]).then_inc(s["idx_ready"], 1)
                pool.wait_ge(s["idx_ready"], u + 1)
                pool.sem_inc(s["pool_go"], 1)
                gather(u_table, idx_u[par], u_ring, u_in, s["u_used"], u, first)

            def rows_v(u, par, first=False):
                pool.tensor_copy(idx_v[par], idx_all[:, bass.ds(u * PK, PK)]).then_inc(s["idv_ready"], 1)
                pool.wait_ge(s["idv_ready"], u + 1)
                pool.sem_inc(s["pool_go"], 1)
                gather(v_table, idx_v[par], v_ring, v_in, s["dg_used"], u, first)

            pool.wait_ge(w_used, N_SLOTS)
            rows_u(0, 0, True)
            rows_u(1, 1)
            rows_v(0, 0, True)
            with pool.Fori(0, NU // 2 - 1) as b:
                for par in (0, 1):
                    u = b * 2 + 2 + par
                    rows_u(u, par)
                    rows_v(u - 1, 1 - par)
            rows_v(NU - 1, 1)


def laid_out(inp):
    d = {k: np.asarray(v) for k, v in inp.items()}
    w = d["w_in"][0]
    o = np.cumsum([0, 512, 64, 64, 256, 64, 4, 512, 512, 512, 256, 256, 512, 512, 16, 3 * D])
    aq, ak, av, iq, ik, iw, bq, bk, bv, cq, ck, cv, cr, ca, gl = (w[:, o[i]:o[i + 1]] for i in range(15))

    def by_tile(m):
        return m.reshape(-1, P, m.shape[1] // P, P).transpose(1, 2, 0, 3).reshape(P, -1)

    def by_row(m):
        return m.reshape(-1, P, m.shape[1]).transpose(1, 0, 2).reshape(P, -1)

    proj = np.stack([by_tile(aq), by_tile(np.concatenate([ak, ak, iq, ik, ik], 1)), by_tile(bq), by_tile(bk),
                     by_row(bv), by_row(cv), by_tile(np.concatenate([cq, ck], 1)), by_row(cr)])
    merge = []
    wo = [d[k][0] for k in ("w_oa", "w_ob", "w_oc")]
    for c in range(KT):
        cols = slice(P * c, P * (c + 1))
        merge.append(np.concatenate([by_row(gl[:, D * b:D * (b + 1)][:, cols]) for b in range(3)]
                                    + [by_row(m[:, cols]) for m in wo], 1))

    def groups(m):
        return np.stack([by_tile(m[:, 512 * g:512 * (g + 1)]) for g in range(m.shape[1] // 512)])

    def col(v):
        return v.reshape(-1, P).T

    vec = np.concatenate(
        [col(d["c"][0]), col(d["b_mod"][0]), col(d["norm1_g"][0]), col(d["norm2_g"][0]), col(d["b_gate"][0]),
         col(d["c_b_alpha"][0])] + [np.tile(d[k][0], 2)[:, None] for k in ("a_qn_g", "a_kn_g", "b_qn_g", "b_kn_g")]
        + [np.tile(d["c_on_g"][0], (P, 1))], 1)
    small = np.concatenate([av, iw, ca], 1)
    return {
        "cst": shape_constants(), "vec": vec, "x": d["x"][0], "w_mod": d["w_mod"][0], "w_proj": proj,
        "w_small": by_row(small), "w_alpha": d["c_w_alpha"][0], "w_merge": np.stack(merge),
        "w_out": groups(d["w_out"][0]), "w_pq": groups(d["peer_wq"][0]),
        "subkeys": d["peer_subkeys"][0].reshape(QT, NK, P).transpose(2, 0, 1),
        "u_table": d["peer_u"][0], "v_table": d["peer_v"][0],
    }


def kernel(**inputs):
    import concourse.bacc as bacc
    from concourse.bass_utils import run_bass_kernel_spmd

    nc = bacc.Bacc("TRN2", target_bir_lowering=False, num_devices=1)
    arrays = {k: np.ascontiguousarray(v) for k, v in laid_out(inputs).items()}
    args = [nc.dram_tensor(k, a.shape, mybir.dt.from_np(a.dtype), kind="ExternalInput").ap() for k, a in arrays.items()]
    out = nc.dram_tensor("out", (T, D), F32, kind="ExternalOutput").ap()
    encoder_layer(nc, *args, out)
    r = run_bass_kernel_spmd(nc, [arrays], core_ids=[0])
    return np.asarray(r.results[0]["out"]).reshape(1, T, D)
```

```python
from contextlib import ExitStack

import numpy as np

import concourse.bass as bass
from concourse import mybir

ALU = mybir.AluOpType
ACT = mybir.ActivationFunctionType
F32 = mybir.dt.float32
U32 = mybir.dt.uint32
AX = mybir.AxisListType.X

P = 128
T, D = 512, 1024
KT, TT = D // P, T // P
EPS = 1e-6
HA = HB = 8
HD = 64
NI = 4
TOPK = T // 4
HC, CV = 4, 128
CH = 64
NCH = T // CH
TAU = 16.0
PH, NK, PK = 8, 128, 16
NE = NK * NK
QT = 2 * PH
LEVELS = (32, 16, 8, 4, 2, 1)
MASKED = -1e30
HIDDEN, PICKED = -3.0e38, -3.4e38
SMALL = 84
WSLOT, NSLOT = 4608, 3
NMOD = 6 * KT

C_ID, C_LATER, C_ONES, C_PAST, C_SEL, C_RESET = 0, 128, 256, 384, 512, 640
C_SELT, C_LEVEL = 1152, 2176
C_IOTA = C_LEVEL + 128 * (len(LEVELS) + 1)
C_END = C_IOTA + 16
V_C, V_BMOD, V_G1, V_G2, V_BG, V_BA, V_GAIN, V_ONG = 0, 8, 56, 64, 72, 96, 98, 102
V_END = V_ONG + HC * CV

B_OFF = (0, 512, 1024, 896)
B_COLS = 1280
A_OFF = (0, 128, 384, 768)


def shape_constants():
    c = np.zeros((P, C_END), np.float32)
    p = np.arange(P)[:, None]
    f = np.arange(P)[None, :]
    c[:, C_ID:C_ID + P] = p == f
    c[:, C_LATER:C_LATER + P] = p > f
    c[:, C_ONES:C_ONES + P] = 1.0
    c[:, C_PAST:C_PAST + P] = p < f
    for t in range(8):
        c[:, C_SEL + 16 * t:C_SEL + 16 * (t + 1)] = np.arange(16)[None, :] == 2 * t + p // HD
        c[0:16, C_SELT + P * t:C_SELT + P * (t + 1)] = p[0:16] == 2 * t + f // HD
    c[:, C_RESET:C_RESET + T] = np.arange(T)[None, :] % CH != 0
    for i, w in enumerate(LEVELS):
        same = p // (2 * w) == f // (2 * w)
        c[:, C_LEVEL + P * i:C_LEVEL + P * (i + 1)] = same & (p % (2 * w) < w) & (f % (2 * w) >= w)
    c[:, C_LEVEL + P * len(LEVELS):C_LEVEL + P * (len(LEVELS) + 1)] = p == f
    c[:, C_IOTA:C_IOTA + 16] = np.arange(16)[None, :]
    return c


def places(sizes):
    at, end = {}, 0
    for name, n in sizes:
        at[name] = end
        end += n
    return at, end


AT, SPACE_END = places([
    ("const", C_END), ("vec", V_END), ("mod", 64), ("stat", 320), ("walpha", 256), ("wsmall", KT * SMALL),
    ("w", WSLOT * NSLOT), ("n", KT * T), ("x", TT * D),
    ("qa", 4 * T), ("ka", T), ("iq", 2 * T), ("ik", T), ("qb", 4 * T), ("kb", 4 * T),
    ("cq", 2 * T), ("ck", 2 * T), ("ca", T), ("va", TT * 68), ("vb", TT * T), ("vc", TT * T), ("rc", TT * T),
    ("ya", 4 * T), ("yb", 4 * T), ("yc", 4 * T), ("sq", 2 * T), ("pen", 1280),
])


def jobs_of_projection():
    jobs = [("d", 4, i, ("qa", i), i) for i in range(4)]
    jobs += [("d", 5, 0, ("ka", 0), 4), ("d", 5, 1, ("iq", 0), None), ("d", 5, 2, ("iq", 1), None),
             ("d", 5, 3, ("ik", 0), None)]
    jobs += [("s", None, t, "va", None) for t in range(TT)] + [("c", None, 0, "ca", None)]
    jobs += [("d", 6, i, ("qb", i), 5 + i) for i in range(4)] + [("d", 7, i, ("kb", i), 9 + i) for i in range(4)]
    jobs += [("t", 8, t, "vb", None) for t in range(TT)] + [("t", 9, t, "vc", None) for t in range(TT)]
    jobs += [("d", 10, i, (("cq", 0), ("cq", 1), ("ck", 0), ("ck", 1))[i], None) for i in range(4)]
    jobs += [("t", 11, t, "rc", None) for t in range(TT)]
    return jobs


def encoder_layer(nc, cst, vec, x, w_mod, w_proj, w_small, w_alpha, w_merge, w_out, w_pq,
                  u_table, v_table, out):
    with ExitStack() as ctx:
        sb = ctx.enter_context(nc.sbuf_tensor("sb", [P, SPACE_END + 32], F32))
        ps = ctx.enter_context(nc.psum_tensor("ps", [P, 8 * 512], F32))

        sems = {}

        def sem(name):
            sems[name] = ctx.enter_context(nc.semaphore(name))
            return sems[name]

        def area(name, lo=0, n=None, p0=0, p1=P):
            a = AT[name] + lo
            return sb[p0:p1, a:a + n]

        def bank(b, n=512, lo=0, p0=0, p1=P):
            return ps[p0:p1, 512 * b + lo:512 * b + lo + n]

        def tiles(ap, n):
            return ap.rearrange("p (a b) -> p a b", a=n)

        ident = area("const", C_ID, P)
        later_tri = area("const", C_LATER, P)
        ones = area("const", C_ONES, P)
        past_tri = area("const", C_PAST, P)
        reset = area("const", C_RESET, T)

        def vcol(i, n=1):
            return area("vec", i, n)

        mod = area("mod", 0, NMOD)
        SH1, SC1, GT1, SH2, SC2, GT2 = (8 * i for i in range(6))

        def mcol(i, n=1):
            return area("mod", i, n)

        amp1 = area("mod", 48, 8)
        amp2 = area("mod", 56, 8)
        cact = area("stat", 0, 8)
        xss, xvar, xrt, xr, xt1 = (area("stat", 8 + 4 * i, 4) for i in range(5))
        top8 = area("stat", 28, 8)
        amax = area("stat", 40, 32)
        anmax = area("stat", 72, 32)
        asum = area("stat", 104, 32)
        arcp = area("stat", 136, 32)
        ebl = area("stat", 168, 16)
        css, cvar, crt, crs, ct1 = (area("stat", 184 + 16 * i, 16) for i in range(5))
        walpha = area("walpha", 0, 256, 0, 16)
        wsmall = tiles(area("wsmall", 0, KT * SMALL), KT)
        n_t = tiles(area("n", 0, KT * T), KT)
        x_tm = tiles(area("x", 0, TT * D), TT)
        xhat = tiles(area("vb", 0, TT * D), TT)
        qa, ka = tiles(area("qa", 0, 4 * T), 4), area("ka", 0, T)
        iq, ik = tiles(area("iq", 0, 2 * T), 2), area("ik", 0, T)
        qb, kb = tiles(area("qb", 0, 4 * T), 4), tiles(area("kb", 0, 4 * T), 4)
        cqk = area("cq", 0, 4 * T)
        ca = area("ca", 0, T, 0, 16)
        va = tiles(area("va", 0, TT * 68), TT)
        vb, vc, rc = (tiles(area(k, 0, TT * T), TT) for k in ("vb", "vc", "rc"))
        ya, yb, yc = (tiles(area(k, 0, 4 * T), 4) for k in ("ya", "yb", "yc"))
        sq = [area("sq", T * i, T) for i in range(2)]

        def pen(qt):
            return area("pen", A_OFF[qt], P * (qt + 1))

        irelu = [area("yb", T * i, T) for i in range(2)]
        st_var, st_rt, st_r, st_t = (area("ya", T * i, T, 0, 16) for i in range(4))
        prob = [area("x", T * i, T) for i in range(3)]
        probT = [area("x", 1536 + T * i, T) for i in range(2)]
        o_tm = area("x", 2560, T)
        spb = [area("x", B_COLS * i, B_COLS) for i in range(2)]
        keep = [area("x", 2 * B_COLS, B_COLS), area("qa", 0, B_COLS)]
        beta = [area("qa", B_COLS, B_COLS), area("qa", 2 * B_COLS, B_COLS), area("pen", 0, B_COLS)]
        c_qk = [area("x", 0, 4 * T), area("x", 4 * T, 4 * T)]
        c_e = area("qa", 0, 4 * T)
        c_qk0 = area("qa", 4 * T, 4 * T)
        c_att = area("qb", 0, 4 * T)
        c_state = area("kb", 0, 2 * P * NCH)
        c_b = area("sq", 0, 2 * T)
        c_kdt = area("pen", 0, 2 * T)

        def kv_at(c, i):
            return 1024 * (c % 2) + 2 * P * (c // 2) + P * i

        def head_at(t, h):
            return P * (8 * (h % 2) + 2 * t + h // 2)

        merged = tiles(area("qb", 0, KT * T), KT)
        gates = [area("qa", 4 * T + T * i, T) for i in range(2)]
        gated = area("qa", 6 * T, T)

        h_t = tiles(area("ya", 0, KT * T), KT)
        yg = [area("yc", T * i, T) for i in range(2)]
        nvar, nrt, nr, ntmp = (area("yc", T * i, T) for i in range(4))
        h_tm = x_tm
        n2_tm = tiles(area("vb", 0, TT * D), TT)
        NU = TT * PH
        R = 8
        pq_slot = area("cq", 0, 2 * D + 2 * NK)
        qp = sq
        g2row = area("yc", 0, D)
        g2tmp = tiles(area("yc", D, D), KT)
        u_ring = [area("qa", D * i, D) for i in range(R)]
        v_ring = [area("w", D * i, D) for i in range(R)]
        acc_tmp = area("ya", 0, D)
        PICK_STEPS = 20
        at = AT["rc"]
        pick = {}
        for nm, n in (("sc", 2 * NK), ("left", 2 * NK), ("top", 32), ("best", 16), ("cand", 256), ("cleft", 256),
                      ("eq", 512), ("hl", 32), ("ixf", 32), ("ef", 32)):
            pick[nm] = sb[:, at:at + n]
            at += n
        ix_u = sb[:, at:at + 32].bitcast(U32)
        bj_u = sb[:, at + 32:at + 48].bitcast(U32)
        hl_u = sb[:, at + 48:at + 80].bitcast(U32)
        assert at + 80 <= AT["rc"] + TT * T
        at = AT["const"] + C_RESET
        dgw = [sb[:, at + P * i:at + P * (i + 1)] for i in range(4)]
        experts = [area("pen", PK * i, PK).bitcast(U32) for i in range(TT)]
        best = [area("pen", PK * (TT + i), PK) for i in range(TT)]
        at = AT["stat"]
        dots, gelu, ebest, wgt = ([sb[:, at + 32 * j + 16 * i:at + 32 * j + 16 * i + 16] for i in range(2)] for j in range(4))
        zsum = [sb[:, at + 128 + i:at + 129 + i] for i in range(2)]
        zinv = [sb[:, at + 130 + i:at + 131 + i] for i in range(2)]

        ld_const, ld_vec, ld_x, ld_ws, ld_wa = (sem(s) for s in ("ld_const", "ld_vec", "ld_x", "ld_ws", "ld_wa"))
        w_in = [sem(f"w_in{i}") for i in range(NSLOT)]
        w_used = sem("w_used")
        v_step, a_step, g_step = sem("v_step"), sem("a_step"), sem("g_step")
        names = """csig cact_ready xss_ready xvar_ready xrt_ready xhat_ready mod1_done mod1_read tr_done nt_ready
                   proj_done proj_out sq_ready sq_used stat_var stat_rt stat_r xa_done xa_read xi_done xi_read
                   irelu_used xb_done xb_read pen_ready mod2_done mod2_read
                   la_done la_read nmax_ready prob_ready pt_done pt_out pv_done o_ready ot_done ot_out
                   zb_done zb_abs zb_relu zb_min sp_ready beta_ready keep_ready lt_done sum_ready b_exp a_exp b_ready yb_done yb_out
                   cu_done cu_ready cabs csp cb_ready ce_ready cex_ready cqk_ready kdt_done kdt_out kv_done ebl_ready st_ready
                   cmin lev_done lev_read att_ready co_done css_ready cvar_ready crt_ready rsil rgain co_ready yct_done yct_out
                   gl_done gate_ready ob_done gate_used merged_ready yo_done yg_ready yg_used xt_done ht_ready
                   hsq_ready hsq_used nvar_ready nrt_ready nr_ready n2_ready att_zero ld_pq pq_used ld_x2
                   tm_done tm_out pq_done pq_out sc_done sc_read g2t_ready g2_done g2_ready picked pool_go acc_free
                   u_used dots_ready gelu_ready z_ready w_ready dg_ready dg_used acc_done added p_step stored zi_ready gated2 p_go""".split()
        u_in = [sem(f"u_in{i}") for i in range(R)]
        v_in = [sem(f"v_in{i}") for i in range(R)]
        s = {nm: sem(nm) for nm in names}

        def slot_view(i):
            return area("w", WSLOT * (i % NSLOT), WSLOT)

        jobs = jobs_of_projection()
        NJ = len(jobs)
        N_STAT = sum(j[4] is not None for j in jobs)
        J_SMALL = max(i for i, j in enumerate(jobs) if j[0] == "c")
        M_SLOTS = (12, 20)
        G_SLOT, O_SLOT, N_SLOTS = 20, 28, 30

        block = ctx.enter_context(nc.Block())

        @block.sync
        def _(sp):
            sp.dma_start(area("const", 0, C_END), cst).then_inc(ld_const, 16)
            sp.dma_start(area("vec", 0, V_END), vec).then_inc(ld_vec, 16)
            sp.dma_start(x_tm[:, :, :], x.rearrange("(t p) d -> p t d", p=P)).then_inc(ld_x, 16)
            wm = w_mod.rearrange("(k p) n -> p k n", p=P)
            for i in range(N_SLOTS):
                if i >= NSLOT:
                    sp.wait_ge(w_used, i - NSLOT + 1)
                dst = slot_view(i)
                if i < 4:
                    dst, src = tiles(dst[:, 0:4096], 2), wm[:, 2 * i:2 * i + 2, 0:2 * D]
                elif i < M_SLOTS[0]:
                    dst, src = dst[:, 0:4096], w_proj[i - 4]
                elif i < M_SLOTS[1]:
                    dst, src = dst[:, 0:4096], wm[:, i - M_SLOTS[0], 2 * D:6 * D]
                elif i < O_SLOT:
                    src = w_merge[i - G_SLOT]
                else:
                    dst, src = dst[:, 0:4096], w_out[i - O_SLOT]
                sp.dma_start(dst, src).then_inc(w_in[i % NSLOT], 16)
                if i == 3:
                    sp.dma_start(area("wsmall", 0, KT * SMALL), w_small).then_inc(ld_ws, 16)
                    sp.dma_start(walpha, w_alpha).then_inc(ld_wa, 16)
                if i == G_SLOT:
                    sp.wait_ge(s["lev_done"], len(LEVELS) + 1)
                    sp.dma_start(x_tm[:, :, :], x.rearrange("(t p) d -> p t d", p=P)).then_inc(s["ld_x2"], 16)
                    sp.dma_start(pq_slot, w_pq[0]).then_inc(s["ld_pq"], 16)
            for h in range(1, PH):
                sp.wait_ge(s["pq_used"], h)
                sp.dma_start(pq_slot, w_pq[h]).then_inc(s["ld_pq"], 16)
            for t in range(TT):
                sp.wait_ge(s["added"], TT * (PH - 1) + t + 1)
                sp.dma_start(out[P * t:P * (t + 1), :], h_tm[:, t, :]).then_inc(s["stored"], 16)
            sp.wait_ge(s["stored"], 16 * TT)

        def slot_ready(pe, i):
            pe.wait_ge(w_in[i % NSLOT], 16 * (i // NSLOT + 1))

        @block.tensor
        def _(pe):
            pe.wait_ge(s["cact_ready"], 1)
            for i in range(4):
                slot_ready(pe, i)
                w = tiles(slot_view(i)[:, 0:4096], 2)
                for k in range(2):
                    for j in range(16):
                        mm = pe.matmul(bank(7, 1, j), w[:, k, P * j:P * (j + 1)], cact[:, 2 * i + k:2 * i + k + 1],
                                       start=(i == 0 and k == 0 and j == 0), stop=(i == 3 and k == 1),
                                       skip_group_check=True)
                mm.then_inc(w_used, 1)
            pe.wait_ge(w_used, 4)
            pe.sem_inc(s["mod1_done"], 1)
            pe.wait_ge(ld_const, 16)
            pe.wait_ge(s["xhat_ready"], TT)
            for k in range(KT):
                if k >= 4:
                    pe.wait_ge(s["nt_ready"], k - 3)
                for t in range(TT):
                    mm = pe.transpose(bank(k % 4, P, P * t), xhat[:, t, P * k:P * (k + 1)], ident)
                mm.then_inc(s["tr_done"], 1)
            pe.wait_ge(s["nt_ready"], KT)
            pe.wait_ge(ld_ws, 16)

            def square_sums(i):
                pe.wait_ge(s["sq_ready"], i + 1)
                t, b = (i, 6) if i < 5 else (i - 5, 7)
                if i == 5:
                    pe.wait_ge(s["mod1_read"], 1)
                sel = area("const", C_SEL + 16 * t, 16)
                pe.matmul(bank(b, T, 0, 0, 16), sel, sq[i % 2], start=(t == 0), stop=(i in (4, N_STAT - 1)))\
                  .then_inc(s["sq_used"], 1)

            def spread(done, read, i, t, n0):
                if n0 + i >= 2:
                    pass
                sel = area("const", C_SELT + P * t, P, 0, 16)
                pe.matmul(bank(4 + i % 2), sel, st_r, start=True, stop=True).then_inc(done, 1)

            waiting = []
            for j, (kind, slot, i, dst, stat) in enumerate(jobs):
                if kind in "dt" and i == 0:
                    slot_ready(pe, slot)
                if j >= 4:
                    pe.wait_ge(s["proj_out"], j - 3)
                for k in range(KT):
                    if kind == "d":
                        w = slot_view(slot)[:, 0:4096].rearrange("p (i k n) -> p i k n", i=4, k=KT)
                        mm = pe.matmul(bank(j % 4), w[:, i, k, :], n_t[:, k, :], start=(k == 0), stop=(k == KT - 1))
                    elif kind == "t":
                        w = tiles(slot_view(slot)[:, 0:4096], KT)
                        mm = pe.matmul(bank(j % 4), n_t[:, k, P * i:P * (i + 1)], w[:, k, :],
                                       start=(k == 0), stop=(k == KT - 1))
                    elif kind == "s":
                        mm = pe.matmul(bank(j % 4, 68), n_t[:, k, P * i:P * (i + 1)], wsmall[:, k, 0:68],
                                       start=(k == 0), stop=(k == KT - 1))
                    else:
                        mm = pe.matmul(bank(j % 4, T, 0, 0, 16), wsmall[:, k, 68:84], n_t[:, k, :],
                                       start=(k == 0), stop=(k == KT - 1))
                mm.then_inc(s["proj_done"], 1)
                if kind in "dt" and i == 3:
                    pe.wait_ge(s["proj_done"], j + 1)
                    pe.sem_inc(w_used, 1)
                while waiting:
                    square_sums(waiting.pop())
                if stat is not None:
                    waiting.append(stat)
                if j == J_SMALL:
                    pe.wait_ge(s["stat_r"], 1)
                    for t in range(5):
                        if t >= 2:
                            pe.wait_ge(s["xa_read"], t - 1)
                        spread(s["xa_done"], s["xa_read"], t, t, 0)
                    pe.wait_ge(s["proj_out"], J_SMALL + 1)
                    pe.wait_ge(s["xa_read"], 5)
                    m = 0
                    for qt in range(1, TT):
                        for h in range(NI):
                            if m >= 2:
                                pe.wait_ge(s["xi_read"], m - 1)
                            r = HD * (h % 2)
                            pe.matmul(bank(4 + m % 2, P * (qt + 1)), iq[r:r + HD, h // 2, P * qt:P * (qt + 1)],
                                      ik[r:r + HD, 0:P * (qt + 1)], start=True, stop=True).then_inc(s["xi_done"], 1)
                            m += 1
            pe.wait_ge(s["stat_r"], 1)
            for k in range(KT):
                slot_ready(pe, M_SLOTS[0] + k)
                w = slot_view(M_SLOTS[0] + k)
                for j in range(32):
                    mm = pe.matmul(bank(6, 1, j), w[:, P * j:P * (j + 1)], cact[:, k:k + 1],
                                   start=(k == 0 and j == 0), stop=(k == KT - 1), skip_group_check=True)
                mm.then_inc(w_used, 1)
            pe.wait_ge(w_used, M_SLOTS[1])
            pe.sem_inc(s["mod2_done"], 1)
            pe.wait_ge(s["stat_r"], 2)
            pe.wait_ge(s["xi_read"], 12)
            for t in range(8):
                if t >= 2:
                    pe.wait_ge(s["xb_read"], t - 1)
                spread(s["xb_done"], s["xb_read"], t, t, 2)

            pe.wait_ge(s["proj_out"], NJ)
            pe.wait_ge(s["mod2_read"], 1)
            NA = TT * HA
            for it in range(NA + 5):
                if it < NA:
                    qt, h = divmod(it, HA)
                    r = HD * (h % 2)
                    if it == 0:
                        pe.wait_ge(s["xa_read"], 5)
                    if it >= 2:
                        pe.wait_ge(s["la_read"], it - 1)
                    pe.matmul(bank(it % 2, P * (qt + 1)), qa[r:r + HD, h // 2, P * qt:P * (qt + 1)],
                              ka[r:r + HD, 0:P * (qt + 1)], start=True, stop=True).then_inc(s["la_done"], 1)
                if 1 <= it <= NA:
                    j = it - 1
                    qt = j // HA
                    pe.wait_ge(s["prob_ready"], j + 1)
                    if j >= 2:
                        pe.wait_ge(s["pt_out"], j - 1)
                    for st in range(qt + 1):
                        mm = pe.transpose(bank(2 + j % 2, P, P * st), prob[j % 3][:, P * st:P * (st + 1)], ident)
                    mm.then_inc(s["pt_done"], 1)
                if 2 <= it <= NA + 1:
                    j = it - 2
                    qt, h = divmod(j, HA)
                    pe.wait_ge(s["pt_out"], j + 1)
                    if j == 0:
                        pe.wait_ge(s["xb_read"], 8)
                    if h == 0 and qt >= 2:
                        pe.wait_ge(s["o_ready"], qt - 1)
                    for st in range(qt + 1):
                        mm = pe.matmul(bank(4 + qt % 2, HD, HD * h), probT[j % 2][:, P * st:P * (st + 1)],
                                       va[:, st, 0:HD], start=(st == 0), stop=(st == qt))
                    mm.then_inc(s["pv_done"], 1)
                if it >= 4 and (it - 4) % HA == HA - 1:
                    qt = (it - 4) // HA
                    pe.wait_ge(s["o_ready"], qt + 1)
                    if qt >= 1:
                        pe.wait_ge(s["ot_out"], qt)
                    for f in range(4):
                        mm = pe.transpose(bank(6, P, P * f), o_tm[:, P * f:P * (f + 1)], ident)
                    mm.then_inc(s["ot_done"], 1)

            pe.wait_ge(s["ot_out"], TT)
            for it in range(HB + 2):
                if it < HB:
                    r = HD * (it % 2)
                    if it >= 1:
                        pe.wait_ge(s["zb_abs"], it)
                        pe.wait_ge(s["zb_relu"], it)
                        pe.wait_ge(s["zb_min"], it)
                    for st in range(TT):
                        n = T - P * st
                        mm = pe.matmul(ps[:, B_OFF[st]:B_OFF[st] + n], kb[r:r + HD, it // 2, P * st:P * (st + 1)],
                                       qb[r:r + HD, it // 2, P * st:T], start=True, stop=True)
                    mm.then_inc(s["zb_done"], 1)
                if 1 <= it <= HB:
                    h = it - 1
                    pe.wait_ge(s["keep_ready"], h + 1)
                    if h >= 1:
                        pe.wait_ge(s["sum_ready"], h)
                    for st in range(TT):
                        o = 1536 + B_OFF[st]
                        mm = pe.matmul(ps[:, o:o + T - P * st], later_tri, keep[h % 2][:, B_OFF[st]:B_OFF[st] + T - P * st],
                                       start=True, stop=(st == TT - 1), skip_group_check=True)
                        for jt in range(st + 1, TT):
                            mm = pe.matmul(ps[:, o + P * (jt - st):o + T - P * st], ones,
                                           keep[h % 2][:, B_OFF[jt]:B_OFF[jt] + T - P * jt],
                                           start=False, stop=(jt == TT - 1), skip_group_check=True)
                    mm.then_inc(s["lt_done"], 1)
                if it >= 2:
                    h = it - 2
                    pe.wait_ge(s["b_ready"], h + 1)
                    if h % 2 == 0 and h >= 4:
                        pe.wait_ge(s["yb_out"], h // 2 - 1)
                    r = HD * (h % 2)
                    for st in range(TT):
                        mm = pe.matmul(bank(6 + h // 2 % 2, T - P * st, P * st, r, r + HD), vb[:, st, HD * h:HD * (h + 1)],
                                       beta[h % 3][:, B_OFF[st]:B_OFF[st] + T - P * st],
                                       start=(st == 0), stop=(st == TT - 1), skip_group_check=True)
                    mm.then_inc(s["yb_done"], 1)

            pe.wait_ge(ld_wa, 16)
            pe.wait_ge(s["zb_abs"], HB)
            pe.wait_ge(s["zb_relu"], HB)
            pe.wait_ge(s["zb_min"], HB)
            for i in range(2):
                mm = pe.matmul(bank(i), walpha[:, P * i:P * (i + 1)], ca, start=True, stop=True)
            mm.then_inc(s["cu_done"], 1)
            pe.wait_ge(s["cqk_ready"], 1)
            pe.wait_ge(s["sum_ready"], HB)
            for t in range(TT):
                for i in range(2):
                    mm = pe.transpose(bank(4, P, 2 * P * t + P * i), c_qk0[:, 2 * T + T * i + P * t:2 * T + T * i + P * (t + 1)], ident)
            mm.then_inc(s["kdt_done"], 1)
            pe.wait_ge(s["kdt_out"], 1)
            pe.wait_ge(s["cu_ready"], 1)
            kdt = tiles(c_kdt, TT)
            for c in range(NCH):
                for h in range(HC):
                    r, q = CH * (c % 2), HD * (h % 2)
                    o = kv_at(c, h // 2)
                    mm = pe.matmul(ps[q:q + HD, o:o + P], kdt[r:r + CH, c // 2, HD * h:HD * (h + 1)],
                                   vc[r:r + CH, c // 2, CV * h:CV * (h + 1)], start=True, stop=True)
            mm.then_inc(s["kv_done"], 1)
            pe.wait_ge(s["yb_out"], 4)
            for lv in range(len(LEVELS) + 1):
                pe.wait_ge(s["cqk_ready"], min(lv + 2, len(LEVELS) + 1))
                if lv == 1:
                    pe.wait_ge(s["st_ready"], NCH - 1)
                if lv >= 2:
                    pe.wait_ge(s["lev_read"], lv - 1)
                qk = cqk if lv == len(LEVELS) else c_qk[lv % 2]
                base = 2048 if lv % 2 == 0 else 0
                for t in range(TT):
                    for h in range(HC):
                        q = HD * (h % 2)
                        a = T * (h // 2) + P * t
                        mm = pe.matmul(ps[:, base + head_at(t, h):base + head_at(t, h) + P],
                                       qk[q:q + HD, 2 * T + a:2 * T + a + P], qk[q:q + HD, a:a + P],
                                       start=True, stop=True)
                mm.then_inc(s["lev_done"], 1)
            pe.wait_ge(s["lev_read"], len(LEVELS))
            pe.wait_ge(s["att_ready"], 1)
            for t in range(TT):
                for h in range(HC):
                    o = head_at(t, h)
                    pe.matmul(ps[:, o:o + CV], c_att[:, o:o + CV], vc[:, t, CV * h:CV * (h + 1)],
                              start=(t % 2 == 0 and h < 2), stop=True, skip_group_check=True)
            for t in range(TT):
                for c in (2 * t, 2 * t + 1):
                    if c == 0:
                        continue
                    for h in range(HC):
                        r, q = CH * (c % 2), HD * (h % 2)
                        a = T * (h // 2) + CH * c
                        so = 2 * P * c + P * (h // 2)
                        o = head_at(t, h)
                        mm = pe.matmul(ps[r:r + CH, o:o + CV], c_qk0[q:q + HD, a:a + CH],
                                       c_state[q:q + HD, so:so + P], start=False, stop=True, skip_group_check=True)
            mm.then_inc(s["co_done"], 1)
            pe.wait_ge(s["co_ready"], 1)
            for f in range(4):
                for t in range(TT):
                    mm = pe.transpose(bank(4 + f, P, P * t), c_e[:, head_at(t, f):head_at(t, f) + P], ident)
            mm.then_inc(s["yct_done"], 1)

            for n in range(3 * KT):
                c, b = divmod(n, 3)
                if b == 0:
                    slot_ready(pe, G_SLOT + c)
                w = slot_view(G_SLOT + c)[:, 0:WSLOT]
                if n >= 2:
                    pe.wait_ge(s["gate_ready"], n - 1)
                for k in range(KT):
                    o = (b * KT + k) * P
                    mm = pe.matmul(bank(n % 2), w[:, o:o + P], n_t[:, k, :], start=(k == 0), stop=(k == KT - 1))
                mm.then_inc(s["gl_done"], 1)
                if n == 0:
                    pe.wait_ge(s["yct_out"], 1)
                if n >= 2:
                    pe.wait_ge(s["gate_used"], n - 1)
                y = (ya, yb, yc)[b]
                for k in range(4):
                    o = (3 * KT + b * 4 + k) * P
                    mm = pe.matmul(bank(2 + n % 2), w[:, o:o + P], y[:, k, :], start=(k == 0), stop=(k == 3))
                mm.then_inc(s["ob_done"], 1)
                if b == 2:
                    pe.wait_ge(s["ob_done"], n + 1)
                    pe.sem_inc(w_used, 1)

            pe.wait_ge(s["merged_ready"], KT)
            pe.wait_ge(s["ld_x2"], 16)
            pe.wait_ge(s["gate_ready"], 3 * KT)
            for c in range(KT + 1):
                if c < KT:
                    if c % 4 == 0:
                        slot_ready(pe, O_SLOT + c // 4)
                    w = slot_view(O_SLOT + c // 4)[:, 0:4096].rearrange("p (i k n) -> p i k n", i=4, k=KT)
                    if c >= 2:
                        pe.wait_ge(s["yg_ready"], c - 1)
                    for k in range(KT):
                        mm = pe.matmul(bank(4 + c % 2), w[:, c % 4, k, :], merged[:, k, :], start=(k == 0), stop=(k == KT - 1))
                    mm.then_inc(s["yo_done"], 1)
                    if c >= 2:
                        pe.wait_ge(s["ht_ready"], c - 1)
                    for t in range(TT):
                        mm = pe.transpose(bank(6 + c % 2, P, P * t), x_tm[:, t, P * c:P * (c + 1)], ident)
                    mm.then_inc(s["xt_done"], 1)
                    if c % 4 == 3:
                        pe.wait_ge(s["yo_done"], c + 1)
                        pe.sem_inc(w_used, 1)
                if c >= 1:
                    pe.wait_ge(s["hsq_ready"], c)
                    pe.matmul(bank(0), ones, sq[(c - 1) % 2], start=(c == 1), stop=(c == KT)).then_inc(s["hsq_used"], 1)

            def to_tokens(m):
                src, q = (h_t, m) if m < 2 * TT else (n_t, m - 2 * TT)
                if m == 0:
                    pe.wait_ge(s["ht_ready"], KT)
                if m >= 2:
                    pe.wait_ge(s["tm_out"], m - 1)
                for f in range(4):
                    mm = pe.transpose(bank((6 if m < 2 * TT else 0) + m % 2, P, P * f),
                                      src[:, 4 * (q % 2) + f, P * (q // 2):P * (q // 2 + 1)], ident)
                mm.then_inc(s["tm_done"], 1)

            def query(h, c):
                if c == 0:
                    pe.wait_ge(s["ld_pq"], (h + 1) * 16)
                w = pq_slot[:, 0:2 * D].rearrange("p (i k n) -> p i k n", i=2, k=KT)
                for k in range(KT):
                    mm = pe.matmul(bank(4 + c), w[:, c, k, :], n_t[:, k, :], start=(k == 0), stop=(k == KT - 1))
                mm.then_inc(s["pq_done"], 1)

            def score(h, half):
                for t in (2 * half, 2 * half + 1):
                    for c in range(2):
                        mm = pe.matmul(bank(6 + half, NK, NK * (2 * (t % 2) + c)), qp[c][:, P * t:P * (t + 1)],
                                       pq_slot[:, 2 * D + NK * c:2 * D + NK * (c + 1)], start=True, stop=True)
                mm.then_inc(s["sc_done"], 1)
                if half == 1:
                    pe.wait_ge(s["sc_done"], 2 * h + 2)
                    pe.sem_inc(s["pq_used"], 1)

            for m in range(2 * TT):
                to_tokens(m)
            pe.wait_ge(s["yo_done"], KT)
            pe.sem_inc(s["u_used"], R)
            pe.sem_inc(s["dg_used"], R)
            pe.wait_ge(s["yg_ready"], KT)
            pe.wait_ge(s["hsq_used"], KT)
            pe.wait_ge(s["n2_ready"], KT)
            query(0, 0)
            query(0, 1)
            pe.wait_ge(s["pq_out"], 2)
            pe.wait_ge(s["tm_out"], 2 * TT)
            score(0, 0)
            score(0, 1)
            for m in range(2 * TT, 4 * TT):
                to_tokens(m)
            pe.wait_ge(s["g2t_ready"], 1)
            for c in range(KT):
                mm = pe.matmul(ps[:, 2 * T + P * c:2 * T + P * (c + 1)], g2tmp[:, c, :], ident, start=True, stop=True)
            mm.then_inc(s["g2_done"], 1)
            pe.wait_ge(s["g2_ready"], 1)
            pe.wait_ge(s["tm_out"], 4 * TT)
            pe.sem_inc(s["acc_free"], 2)

            def weigh(u, par):
                pe.wait_ge(s["acc_free"], u + 1)
                for i in range(PK):
                    pe.wait_ge(s["dg_ready"], u * PK + i + 1)
                    pe.wait_ge(v_in[i % R], (u * (PK // R) + i // R + 1) * 16)
                    for f in range(2):
                        mm = pe.matmul(bank(2 * par + f), dgw[i % 4], v_ring[i % R][:, T * f:T * (f + 1)],
                                       start=(i == 0), stop=(i == PK - 1))
                    if i == PK - 1:
                        mm.then_inc(s["acc_done"], 1)
                        pe.wait_ge(s["acc_done"], u + 1)
                        pe.sem_inc(s["dg_used"], 1)
                    else:
                        mm.then_inc(s["dg_used"], 1)

            with pe.Fori(0, PH - 1) as h:
                query(h + 1, 0)
                weigh(h * TT, 0)
                query(h + 1, 1)
                pe.wait_ge(s["pq_out"], h * 2 + 4)
                pe.wait_ge(s["sc_read"], h * TT + 2)
                score(h + 1, 0)
                weigh(h * TT + 1, 1)
                pe.wait_ge(s["sc_read"], h * TT + 4)
                score(h + 1, 1)
                weigh(h * TT + 2, 0)
                weigh(h * TT + 3, 1)
            for t in range(TT):
                weigh(TT * (PH - 1) + t, t % 2)

        @block.scalar
        def _(act):
            act.wait_ge(ld_vec, 16)
            act.activation(ct1[:, 0:8], vcol(V_C, 8), ACT.Sigmoid).then_inc(s["csig"], 1)
            act.wait_ge(ld_x, 16)
            for t in range(TT):
                act.activation(area("ya", D * t, D), x_tm[:, t, :], ACT.Square, accum_out=xss[:, t:t + 1])\
                   .then_inc(s["xss_ready"], 1)
            act.wait_ge(s["xvar_ready"], 1)
            act.activation(xrt, xvar, ACT.Sqrt).then_inc(s["xrt_ready"], 1)
            for j, (kind, slot, i, dst, stat) in enumerate(jobs):
                act.wait_ge(s["proj_done"], j + 1)
                if kind == "d":
                    o = area(dst[0], T * dst[1], T)
                    scale = HD ** -0.5 if dst[0] == "cq" else 1.0
                    c = act.activation(o, bank(j % 4), ACT.Copy, scale=scale)
                    if stat is not None:
                        if stat >= 2:
                            act.wait_ge(s["sq_used"], stat - 1)
                        act.activation(sq[stat % 2], bank(j % 4), ACT.Square).then_inc(s["sq_ready"], 1)
                        act.wait_ge(s["sq_ready"], stat + 1)
                        act.sem_inc(s["proj_out"], 1)
                    else:
                        c.then_inc(s["proj_out"], 1)
                elif kind == "t":
                    act.activation(area(dst, T * i, T), bank(j % 4), ACT.Copy).then_inc(s["proj_out"], 1)
                elif kind == "s":
                    act.activation(va[:, i, :], bank(j % 4, 68), ACT.Copy).then_inc(s["proj_out"], 1)
                else:
                    act.activation(ca, bank(j % 4, T, 0, 0, 16), ACT.Copy).then_inc(s["proj_out"], 1)
                if j == J_SMALL:
                    act.wait_ge(s["stat_var"], 1)
                    act.activation(st_rt, st_var, ACT.Sqrt).then_inc(s["stat_rt"], 1)
                    for m in range(12):
                        w = P * (m // NI + 2)
                        act.wait_ge(s["xi_done"], m + 1)
                        if m >= 2:
                            act.wait_ge(s["irelu_used"], m - 1)
                        act.activation(irelu[m % 2][:, 0:w], bank(4 + m % 2, w), ACT.Relu).then_inc(s["xi_read"], 1)
            act.wait_ge(s["stat_var"], 2)
            act.activation(st_rt, st_var, ACT.Sqrt).then_inc(s["stat_rt"], 1)

            NA = TT * HA
            for it in range(NA + 5):
                if it < NA:
                    n = P * (it // HA + 1)
                    act.wait_ge(s["nmax_ready"], it + 1)
                    act.activation(prob[it % 3][:, 0:n], prob[it % 3][:, 0:n], ACT.Exp, bias=anmax[:, it:it + 1],
                                   accum_out=asum[:, it:it + 1]).then_inc(s["prob_ready"], 1)
                if 1 <= it <= NA:
                    j = it - 1
                    n = P * (j // HA + 1)
                    act.wait_ge(s["pt_done"], j + 1)
                    if j >= 2:
                        act.wait_ge(s["pv_done"], j - 1)
                    act.activation(probT[j % 2][:, 0:n], bank(2 + j % 2, n), ACT.Copy).then_inc(s["pt_out"], 1)
                if it >= 4 and (it - 4) % HA == HA - 1:
                    qt = (it - 4) // HA
                    act.wait_ge(s["ot_done"], qt + 1)
                    if qt == 0:
                        act.wait_ge(s["stat_r"], 2)
                        act.wait_ge(s["xb_read"], 8)
                    act.activation(ya[:, :, P * qt:P * (qt + 1)], tiles(bank(6), 4), ACT.Copy).then_inc(s["ot_out"], 1)

            for it in range(HB + 2):
                if it < HB:
                    z = ps[:, 0:B_COLS]
                    sp_, kp = spb[it % 2], keep[it % 2]
                    act.wait_ge(s["zb_done"], it + 1)
                    if it >= 2:
                        act.wait_ge(s["keep_ready"], it - 1)
                        act.wait_ge(s["beta_ready"], it - 1)
                    act.activation(sp_, z, ACT.Abs, scale=HD ** -0.5).then_inc(s["zb_abs"], 1)
                    if it >= 2:
                        act.wait_ge(s["lt_done"], it - 1)
                    act.activation(kp, z, ACT.Relu, scale=HD ** -0.5).then_inc(s["zb_relu"], 1)
                    act.wait_ge(s["zb_abs"], it + 1)
                    act.activation(sp_, sp_, ACT.Exp, scale=-1.0).then_inc(s["b_exp"], 1)
                    act.wait_ge(s["b_exp"], it + 1)
                    act.activation(sp_, sp_, ACT.Ln, bias=1.0).then_inc(s["sp_ready"], 1)
                if 1 <= it <= HB:
                    h = it - 1
                    act.wait_ge(s["sum_ready"], h + 1)
                    act.activation(beta[h % 3], beta[h % 3], ACT.Exp).then_inc(s["a_exp"], 1)
                if it >= 2 and it % 2 == 1:
                    h = it - 2
                    act.wait_ge(s["yb_done"], h + 1)
                    act.activation(yb[:, h // 2, :], bank(6 + h // 2 % 2), ACT.Copy).then_inc(s["yb_out"], 1)

            act.activation(area("rc", 0, TT * T), area("rc", 0, TT * T), ACT.Silu).then_inc(s["rsil"], 1)
            act.wait_ge(s["cu_ready"], 1)
            sp_ = c_e[:, 2 * T:4 * T]
            act.activation(sp_, c_e[:, 0:2 * T], ACT.Abs).then_inc(s["cabs"], 1)
            act.wait_ge(s["cabs"], 1)
            act.activation(sp_, sp_, ACT.Exp, scale=-1.0).then_inc(s["cabs"], 1)
            act.wait_ge(s["cabs"], 2)
            act.activation(sp_, sp_, ACT.Ln, bias=1.0).then_inc(s["csp"], 1)
            act.wait_ge(s["cb_ready"], 1)
            act.activation(tiles(ebl, 2), c_b.rearrange("p (i c l) -> p i c l", i=2, l=CH)[:, :, :, CH - 1], ACT.Exp,
                           scale=1 / TAU).then_inc(s["ebl_ready"], 1)
            for lv in range(len(LEVELS) + 1):
                act.wait_ge(s["ce_ready"], lv + 1)
                act.activation(c_e, c_e, ACT.Exp, scale=1 / TAU).then_inc(s["cex_ready"], 1)
                if lv == 1:
                    act.wait_ge(s["kdt_done"], 1)
                    act.activation(c_kdt, ps[:, 2048:2048 + 2 * T], ACT.Copy).then_inc(s["kdt_out"], 1)
            act.wait_ge(s["co_done"], 1)
            act.activation(c_e, ps[:, 0:4 * T], ACT.Square).then_inc(s["css_ready"], 1)
            act.wait_ge(s["cvar_ready"], 1)
            act.activation(crt, cvar, ACT.Sqrt).then_inc(s["crt_ready"], 1)
            act.wait_ge(s["yct_done"], 1)
            act.activation(area("yc", 0, 4 * T), ps[:, 2048:4096], ACT.Copy).then_inc(s["yct_out"], 1)

            for n in range(3 * KT):
                c, b = divmod(n, 3)
                act.wait_ge(s["gl_done"], n + 1)
                if n >= 2:
                    act.wait_ge(s["gate_used"], n - 1)
                act.activation(gates[n % 2], bank(n % 2), ACT.Sigmoid, bias=vcol(V_BG + b * KT + c))\
                   .then_inc(s["gate_ready"], 1)

            for c in range(KT + 1):
                if c < KT:
                    act.wait_ge(s["yo_done"], c + 1)
                    if c >= 2:
                        act.wait_ge(s["ht_ready"], c - 1)
                    act.activation(yg[c % 2], bank(4 + c % 2), ACT.Copy, scale=mcol(GT1 + c)).then_inc(s["yg_ready"], 1)
                if c >= 1:
                    act.wait_ge(s["ht_ready"], c)
                    if c >= 3:
                        act.wait_ge(s["hsq_used"], c - 2)
                    act.activation(sq[(c - 1) % 2], h_t[:, c - 1, :], ACT.Square).then_inc(s["hsq_ready"], 1)

            def tokens_out(m):
                act.wait_ge(s["tm_done"], m + 1)
                dst, q = (h_tm, m) if m < 2 * TT else (n2_tm, m - 2 * TT)
                act.activation(dst[:, q // 2, T * (q % 2):T * (q % 2 + 1)], bank((6 if m < 2 * TT else 0) + m % 2), ACT.Copy)\
                   .then_inc(s["tm_out"], 1)

            act.wait_ge(s["nvar_ready"], 1)
            act.activation(nrt, nvar, ACT.Sqrt).then_inc(s["nrt_ready"], 1)
            for m in range(2 * TT):
                tokens_out(m)

            def query_out(h, c):
                act.wait_ge(s["pq_done"], h * 2 + c + 1)
                act.wait_ge(s["sc_done"], h * 2)
                act.activation(qp[c], bank(4 + c), ACT.Copy).then_inc(s["pq_out"], 1)

            def weights(u, r):
                act.wait_ge(s["dots_ready"], u + 1)
                act.activation(gelu[r % 2], dots[r % 2], ACT.Gelu).then_inc(s["gelu_ready"], 1)
                act.activation(ebest[r % 2], best[r], ACT.Exp, accum_out=zsum[r % 2]).then_inc(s["z_ready"], 1)

            def diagonals(u, r):
                act.wait_ge(s["w_ready"], u + 1)
                for i in range(PK):
                    act.wait_ge(s["dg_used"], u * PK + i + 1 + R - 4)
                    act.activation(dgw[i % 4], ident, ACT.Copy, scale=wgt[r % 2][:, i:i + 1]).then_inc(s["dg_ready"], 1)

            for c in range(2):
                act.wait_ge(s["pq_done"], c + 1)
                act.activation(qp[c], bank(4 + c), ACT.Copy).then_inc(s["pq_out"], 1)
            for m in range(2 * TT, 4 * TT):
                tokens_out(m)
            with act.Fori(0, PH - 1) as h:
                for r in range(TT):
                    weights(h * TT + r, r)
                    if r < 2:
                        query_out(h + 1, r)
                    diagonals(h * TT + r, r)
            for r in range(TT):
                weights(TT * (PH - 1) + r, r)
                diagonals(TT * (PH - 1) + r, r)

        @block.vector
        def _(dve):
            def done(ins):
                v_count[0] += 1
                ins.then_inc(v_step, 1)
                dve.wait_ge(v_step, v_count[0])

            v_count = [0]

            def inverse_root(r, root, var, tmp):
                done(dve.reciprocal(r, root))
                done(dve.tensor_tensor(tmp, r, r, ALU.mult))
                done(dve.tensor_tensor(tmp, tmp, var, ALU.mult))
                done(dve.tensor_scalar(tmp, tmp, -0.5, 1.5, ALU.mult, ALU.add))
                return dve.tensor_tensor(r, r, tmp, ALU.mult)

            dve.wait_ge(s["csig"], 1)
            dve.tensor_tensor(cact, vcol(V_C, 8), ct1[:, 0:8], ALU.mult).then_inc(s["cact_ready"], 1)
            dve.wait_ge(s["xss_ready"], TT)
            dve.tensor_scalar(xvar, xss, 1 / D, EPS, ALU.mult, ALU.add).then_inc(s["xvar_ready"], 1)
            dve.wait_ge(s["xrt_ready"], 1)
            done(inverse_root(xr, xrt, xvar, xt1))
            for t in range(TT):
                dve.tensor_scalar(xhat[:, t, :], x_tm[:, t, :], xr[:, t:t + 1], None, ALU.mult).then_inc(s["xhat_ready"], 1)
            dve.wait_ge(s["mod1_done"], 1)
            dve.tensor_tensor(mcol(0, 16), bank(7, 16), vcol(V_BMOD, 16), ALU.add).then_inc(s["mod1_read"], 1)
            dve.wait_ge(s["mod1_read"], 1)
            done(dve.scalar_tensor_tensor(amp1, mcol(SC1, 8), 1.0, vcol(V_G1, 8), ALU.add, ALU.mult))
            for k in range(KT):
                dve.wait_ge(s["tr_done"], k + 1)
                dve.tensor_scalar(n_t[:, k, :], bank(k % 4), amp1[:, k:k + 1], mcol(SH1 + k), ALU.mult, ALU.add)\
                   .then_inc(s["nt_ready"], 1)

            def head_factors(n, b):
                dve.wait_ge(s["sq_used"], (5, N_STAT)[n - 1])
                dve.tensor_scalar(st_var, bank(b, T, 0, 0, 16), 1 / HD, EPS, ALU.mult, ALU.add).then_inc(s["stat_var"], 1)
                dve.wait_ge(s["stat_rt"], n)
                inverse_root(st_r, st_rt, st_var, st_t).then_inc(s["stat_r"], 1)

            head_factors(1, 6)
            dve.wait_ge(s["proj_out"], 5)
            for t in range(5):
                dst = qa[:, t, :] if t < 4 else ka
                dve.wait_ge(s["xa_done"], t + 1)
                dve.scalar_tensor_tensor(dst, dst, vcol(V_GAIN + t // 4), bank(4 + t % 2), ALU.mult, ALU.mult)\
                   .then_inc(s["xa_read"], 1)
            m = 0
            for qt in range(1, TT):
                for h in range(NI):
                    dve.wait_ge(s["xi_read"], m + 1)
                    wcol = va[:, qt, HD + h:HD + h + 1]
                    if h == 0:
                        ins = dve.tensor_scalar(pen(qt), irelu[m % 2][:, 0:P * (qt + 1)], wcol, None, ALU.mult)
                    else:
                        dve.wait_ge(s["irelu_used"], m)
                        ins = dve.scalar_tensor_tensor(pen(qt), irelu[m % 2][:, 0:P * (qt + 1)], wcol, pen(qt),
                                                       ALU.mult, ALU.add)
                    ins.then_inc(s["irelu_used"], 1)
                    m += 1
            dve.wait_ge(s["irelu_used"], m)
            for qt in range(1, TT):
                done(dve.memset(pen(qt)[0:CH, P * qt + CH:P * (qt + 1)], HIDDEN))
            for qt in range(1, TT):
                for r in range(TOPK // 8):
                    done(dve.max(out=top8, in_=pen(qt)))
                    done(dve.match_replace(out=pen(qt), in_to_replace=top8, in_values=pen(qt), imm_value=PICKED))
                done(dve.tensor_scalar(pen(qt), pen(qt), (HIDDEN + PICKED) / 2, MASKED, ALU.is_gt, ALU.mult))
            done(dve.memset(pen(0), 0.0))
            done(dve.memset(pen(0)[0:CH, CH:P], MASKED))
            head_factors(2, 7)
            for t in range(8):
                dst = (qb, kb)[t // 4][:, t % 4, :]
                dve.wait_ge(s["xb_done"], t + 1)
                dve.scalar_tensor_tensor(dst, dst, vcol(V_GAIN + 2 + t // 4), bank(4 + t % 2), ALU.mult, ALU.mult)\
                   .then_inc(s["xb_read"], 1)
            dve.wait_ge(s["mod2_done"], 1)
            dve.tensor_tensor(mcol(16, 32), bank(6, 32), vcol(V_BMOD + 16, 32), ALU.add).then_inc(s["mod2_read"], 1)
            dve.wait_ge(s["mod2_read"], 1)
            done(dve.scalar_tensor_tensor(amp2, mcol(SC2, 8), 1.0, vcol(V_G2, 8), ALU.add, ALU.mult))

            NA = TT * HA
            for it in range(NA + 3):
                if it < NA:
                    qt = it // HA
                    n = P * (qt + 1)
                    dve.wait_ge(s["la_done"], it + 1)
                    if it >= 3:
                        dve.wait_ge(s["pt_done"], it - 2)
                    dve.tensor_tensor_reduce(out=prob[it % 3][:, 0:n], in0=bank(it % 2, n), in1=pen(qt),
                                             scale=HD ** -0.5, scalar=-3.4e38, op0=ALU.add, op1=ALU.max,
                                             accum_out=amax[:, it:it + 1]).then_inc(s["la_read"], 1)
                    dve.wait_ge(s["la_read"], it + 1)
                    dve.tensor_scalar(anmax[:, it:it + 1], amax[:, it:it + 1], -1.0, None, ALU.mult).then_inc(s["nmax_ready"], 1)
                if it >= 3 and (it - 3) % HA == HA - 1:
                    qt = (it - 3) // HA
                    c = slice(HA * qt, HA * (qt + 1))
                    dve.wait_ge(s["prob_ready"], HA * (qt + 1))
                    done(dve.reciprocal(arcp[:, c], asum[:, c]))
                    dve.wait_ge(s["pv_done"], HA * (qt + 1))
                    if qt >= 1:
                        dve.wait_ge(s["ot_done"], qt)
                    dve.tensor_tensor(tiles(o_tm, HA), tiles(bank(4 + qt % 2), HA),
                                      arcp[:, c].unsqueeze(2).broadcast_to([P, HA, HD]), ALU.mult).then_inc(s["o_ready"], 1)

            dve.wait_ge(s["ot_out"], TT)
            for it in range(HB + 1):
                if it < HB:
                    z = ps[:, 0:B_COLS]
                    kp, bt, sp_ = keep[it % 2], beta[it % 3], spb[it % 2]
                    dve.wait_ge(s["zb_relu"], it + 1)
                    if it >= 3:
                        dve.wait_ge(s["yb_done"], it - 2)
                    dve.tensor_scalar(bt, z, HD ** -0.5, 0.0, ALU.mult, ALU.min).then_inc(s["zb_min"], 1)
                    dve.wait_ge(s["sp_ready"], it + 1)
                    done(dve.scalar_tensor_tensor(kp, kp, -1.0, sp_, ALU.mult, ALU.subtract))
                    for st in range(TT):
                        d = kp[:, B_OFF[st]:B_OFF[st] + P]
                        ins = dve.tensor_tensor(d, d, past_tri, ALU.mult)
                    ins.then_inc(s["keep_ready"], 1)
                if it >= 1:
                    h = it - 1
                    dve.wait_ge(s["lt_done"], h + 1)
                    dve.wait_ge(s["beta_ready"], h + 1)
                    dve.tensor_tensor(beta[h % 3], beta[h % 3], ps[:, 1536:1536 + B_COLS], ALU.add).then_inc(s["sum_ready"], 1)

            dve.wait_ge(s["cu_done"], 1)
            dve.wait_ge(s["yb_done"], HB)
            for i in range(2):
                u = dve.tensor_scalar(c_e[:, T * i:T * (i + 1)], bank(i), vcol(V_BA + i), None, ALU.add)
            u.then_inc(s["cu_ready"], 1)
            dve.wait_ge(s["cabs"], 1)
            done(dve.tensor_scalar(c_e[:, 0:2 * T], c_e[:, 0:2 * T], 0.0, None, ALU.min))
            dve.wait_ge(s["csp"], 1)
            done(dve.tensor_tensor(c_e[:, 0:2 * T], c_e[:, 0:2 * T], c_e[:, 2 * T:4 * T], ALU.subtract))
            for i in range(2):
                last = dve.tensor_tensor_scan(c_b[:, T * i:T * (i + 1)], reset, c_e[:, T * i:T * (i + 1)], 0.0,
                                              ALU.mult, ALU.add)
            last.then_inc(s["cb_ready"], 1)
            dve.wait_ge(s["cb_ready"], 1)
            bch = c_b.rearrange("p (c l) -> p c l", l=CH)
            dve.tensor_copy(c_e[:, 0:2 * T], c_b)
            dve.tensor_tensor(c_e[:, 2 * T:4 * T].rearrange("p (c l) -> p c l", l=CH),
                              bch[:, :, CH - 1:CH].broadcast_to([P, 2 * NCH, CH]), bch, ALU.subtract).then_inc(s["ce_ready"], 1)
            dve.wait_ge(s["cex_ready"], 1)
            dve.tensor_tensor(c_qk0, cqk, c_e, ALU.mult).then_inc(s["cqk_ready"], 1)
            dve.wait_ge(s["cqk_ready"], 1)

            def level(lv):
                w = LEVELS[lv]
                e0 = c_e[:, 0:2 * T].rearrange("p (c l) -> p c l", l=2 * w)
                bb = c_b.rearrange("p (c l) -> p c l", l=2 * w)
                done(dve.tensor_tensor(e0, bb, bb[:, :, w - 1:w].broadcast_to([P, T // w, 2 * w]), ALU.subtract))
                done(dve.tensor_scalar(c_e[:, 2 * T:4 * T], c_e[:, 0:2 * T], -1.0, 0.0, ALU.mult, ALU.min))
                dve.tensor_scalar(c_e[:, 0:2 * T], c_e[:, 0:2 * T], 0.0, None, ALU.min).then_inc(s["ce_ready"], 1)
                dve.wait_ge(s["cex_ready"], lv + 2)
                if lv >= 2:
                    dve.wait_ge(s["lev_done"], lv - 1)
                dve.tensor_tensor(c_qk[lv % 2], cqk, c_e, ALU.mult).then_inc(s["cqk_ready"], 1)
                dve.wait_ge(s["cqk_ready"], lv + 2)

            def level_read(lv):
                base = 2048 if lv % 2 == 0 else 0
                m = area("const", C_LEVEL + P * lv, P).bitcast(U32)
                dve.wait_ge(s["lev_done"], lv + 1)
                dve.copy_predicated(out=tiles(c_att, 16), mask=m.unsqueeze(1).broadcast_to([P, 16, P]),
                                    data=tiles(ps[:, base:base + 2048], 16)).then_inc(s["lev_read"], 1)
                dve.wait_ge(s["lev_read"], lv + 1)

            level(0)
            level(1)
            dve.wait_ge(s["kv_done"], 1)
            dve.wait_ge(s["ebl_ready"], 1)
            for c in range(1, NCH):
                for i in range(2):
                    new = c_state[:, 2 * P * c + P * i:2 * P * c + P * (i + 1)]
                    old = c_state[:, 2 * P * (c - 1) + P * i:2 * P * (c - 1) + P * (i + 1)]
                    kv = ps[:, kv_at(c - 1, i):kv_at(c - 1, i) + P]
                    if c == 1:
                        ins = dve.tensor_copy(new, kv)
                    else:
                        ins = dve.scalar_tensor_tensor(new, old, ebl[:, NCH * i + c - 1:NCH * i + c], kv, ALU.mult, ALU.add)
                ins.then_inc(s["st_ready"], 1)
                dve.wait_ge(s["st_ready"], c)
            dve.wait_ge(s["att_zero"], 1)
            for lv in range(len(LEVELS) + 1):
                level_read(lv)
                if lv + 2 < len(LEVELS):
                    level(lv + 2)
            dve.sem_inc(s["att_ready"], 1)
            dve.wait_ge(s["css_ready"], 1)
            done(dve.tensor_reduce(css, tiles(c_e, 16), AX, ALU.add))
            dve.tensor_scalar(cvar, css, 1 / CV, EPS, ALU.mult, ALU.add).then_inc(s["cvar_ready"], 1)
            dve.wait_ge(s["crt_ready"], 1)
            done(inverse_root(crs, crt, cvar, ct1))
            done(dve.tensor_tensor(tiles(c_e, 16), tiles(ps[:, 0:4 * T], 16), crs.unsqueeze(2).broadcast_to([P, 16, CV]),
                                   ALU.mult))
            dve.wait_ge(s["rgain"], 1)
            for b in range(2):
                e = c_e[:, 2 * T * b:2 * T * (b + 1)].rearrange("p (t a v) -> p t a v", t=TT, v=CV)
                g = area("rc", 0, TT * T).rearrange("p (t a b v) -> p t a b v", t=TT, b=2, v=CV)[:, :, :, b, :]
                ins = dve.tensor_tensor(e, e, g, ALU.mult)
            ins.then_inc(s["co_ready"], 1)

            for n in range(3 * KT):
                c, b = divmod(n, 3)
                dve.wait_ge(s["gate_ready"], n + 1)
                dve.wait_ge(s["ob_done"], n + 1)
                if b == 0:
                    done(dve.tensor_tensor(merged[:, c, :], gates[n % 2], bank(2 + n % 2), ALU.mult))
                    dve.sem_inc(s["gate_used"], 1)
                else:
                    dve.tensor_tensor(gated, gates[n % 2], bank(2 + n % 2), ALU.mult).then_inc(s["gate_used"], 1)
                    dve.wait_ge(s["gate_used"], n + 1)
                    done(dve.tensor_tensor(merged[:, c, :], merged[:, c, :], gated, ALU.add))
                if b == 2:
                    dve.sem_inc(s["merged_ready"], 1)

            for c in range(KT):
                dve.wait_ge(s["yg_ready"], c + 1)
                dve.wait_ge(s["xt_done"], c + 1)
                dve.tensor_tensor(h_t[:, c, :], yg[c % 2], bank(6 + c % 2), ALU.add).then_inc(s["ht_ready"], 1)
            dve.wait_ge(s["hsq_used"], KT)
            dve.tensor_scalar(nvar, bank(0), 1 / D, EPS, ALU.mult, ALU.add).then_inc(s["nvar_ready"], 1)
            dve.wait_ge(s["nrt_ready"], 1)
            done(inverse_root(nr, nrt, nvar, ntmp))
            for c in range(KT):
                done(dve.scalar_tensor_tensor(n_t[:, c, :], h_t[:, c, :], amp2[:, c:c + 1], nr, ALU.mult, ALU.mult))
                dve.tensor_scalar(n_t[:, c, :], n_t[:, c, :], mcol(SH2 + c), None, ALU.add).then_inc(s["n2_ready"], 1)
            for c in range(KT):
                ins = dve.tensor_scalar(g2tmp[:, c, :], ones, mcol(GT2 + c), None, ALU.mult)
            ins.then_inc(s["g2t_ready"], 1)
            k = pick
            iota = area("const", C_IOTA, 16)

            def pick_experts(u, r, scored):
                n = [0]
                base = u * PICK_STEPS

                def step(ins, own=False):
                    n[0] += 1
                    ins.then_inc(s["p_step"], 1)
                    dve.wait_ge(s["p_step"], base + n[0])
                    if own:
                        dve.sem_inc(s["p_go"], 1)

                dve.wait_ge(s["sc_done"], scored)
                step(dve.tensor_copy(k["sc"], bank(6 + r // 2, 2 * NK, 2 * NK * (r % 2))), own=True)
                dve.sem_inc(s["sc_read"], 1)
                for c in range(2):
                    row, left = k["sc"][:, NK * c:NK * (c + 1)], k["left"][:, NK * c:NK * (c + 1)]
                    t0, t1 = k["top"][:, 16 * c:16 * c + 8], k["top"][:, 16 * c + 8:16 * c + 16]
                    step(dve.max(out=t0, in_=row), own=True)
                    dve.max_index(out=ix_u[:, 16 * c:16 * c + 8], in_max=t0, in_values=row)
                    step(dve.match_replace(out=left, in_to_replace=t0, in_values=row, imm_value=PICKED), own=True)
                    step(dve.max(out=t1, in_=left), own=True)
                    step(dve.max_index(out=ix_u[:, 16 * c + 8:16 * c + 16], in_max=t1, in_values=left), own=True)
                step(dve.tensor_tensor(tiles(k["cand"], 16), k["top"][:, 0:16].unsqueeze(2).broadcast_to([P, 16, 16]),
                                       k["top"][:, 16:32].unsqueeze(1).broadcast_to([P, 16, 16]), ALU.add), own=True)
                b0, b1 = k["best"][:, 0:8], k["best"][:, 8:16]
                step(dve.max(out=b0, in_=k["cand"]), own=True)
                dve.max_index(out=bj_u[:, 0:8], in_max=b0, in_values=k["cand"])
                step(dve.match_replace(out=k["cleft"], in_to_replace=b0, in_values=k["cand"], imm_value=PICKED), own=True)
                step(dve.max(out=b1, in_=k["cleft"]), own=True)
                step(dve.max_index(out=bj_u[:, 8:16], in_max=b1, in_values=k["cleft"]))
                dve.tensor_scalar(hl_u[:, 0:16], bj_u, 4, None, ALU.logical_shift_right)
                step(dve.tensor_scalar(hl_u[:, 16:32], bj_u, 15, None, ALU.bitwise_and))
                dve.tensor_copy(k["hl"], hl_u)
                step(dve.tensor_copy(k["ixf"], ix_u))
                step(dve.tensor_tensor(tiles(k["eq"], 32), iota.unsqueeze(1).broadcast_to([P, 32, 16]),
                                       k["hl"].unsqueeze(2).broadcast_to([P, 32, 16]), ALU.is_equal))
                e = k["eq"].rearrange("p (c j a) -> p c j a", c=2, j=16)
                step(dve.tensor_tensor(e, e, tiles(k["ixf"], 2).unsqueeze(2).broadcast_to([P, 2, 16, 16]), ALU.mult))
                step(dve.tensor_reduce(k["ef"], tiles(k["eq"], 32), AX, ALU.add))
                dve.scalar_tensor_tensor(experts[r], k["ef"][:, 0:16], float(NK), k["ef"][:, 16:32],
                                         ALU.mult, ALU.add)
                step(dve.tensor_scalar(best[r], k["best"], k["best"][:, 0:1], None, ALU.subtract))
                dve.sem_inc(s["picked"], 1)
                assert n[0] == PICK_STEPS

            def dot(u, r):
                for i in range(PK):
                    dve.wait_ge(u_in[i % R], (u * (PK // R) + i // R + 1) * 16)
                    dve.tensor_tensor_reduce(out=u_ring[i % R], in0=u_ring[i % R], in1=n2_tm[:, r, :], scale=1.0, scalar=0.0,
                                             op0=ALU.mult, op1=ALU.add, accum_out=dots[r % 2][:, i:i + 1]).then_inc(s["u_used"], 1)
                dve.wait_ge(s["u_used"], (u + 1) * PK + R)
                dve.sem_inc(s["dots_ready"], 1)

            def weight(u, r):
                dve.wait_ge(s["z_ready"], u + 1)
                dve.reciprocal(zinv[r % 2], zsum[r % 2]).then_inc(s["zi_ready"], 1)
                dve.wait_ge(s["zi_ready"], u + 1)
                dve.wait_ge(s["gelu_ready"], u + 1)
                dve.scalar_tensor_tensor(wgt[r % 2], gelu[r % 2], zinv[r % 2], ebest[r % 2], ALU.mult, ALU.mult)\
                   .then_inc(s["w_ready"], 1)

            def add(u, r):
                dve.wait_ge(s["acc_done"], u + 1)
                dve.tensor_tensor(acc_tmp, ps[:, D * (r % 2):D * (r % 2 + 1)], g2row, ALU.mult).then_inc(s["gated2"], 1)
                dve.wait_ge(s["gated2"], u + 1)
                dve.sem_inc(s["acc_free"], 1)
                dve.tensor_tensor(h_tm[:, r, :], h_tm[:, r, :], acc_tmp, ALU.add).then_inc(s["added"], 1)
                dve.wait_ge(s["added"], u + 1)

            pick_experts(0, 0, 1)
            dve.wait_ge(s["g2_done"], 1)
            dve.tensor_copy(g2row, ps[:, 2 * T:2 * T + D]).then_inc(s["g2_ready"], 1)
            dve.wait_ge(s["g2_ready"], 1)
            pick_experts(1, 1, 1)
            dve.wait_ge(s["tm_out"], 4 * TT)
            dot(0, 0)
            weight(0, 0)
            pick_experts(2, 2, 2)
            with dve.Fori(0, PH - 1) as b:
                for j in range(1, TT + 1):
                    u, r, nxt = b * TT + j, j % TT, (j + 2) % TT
                    dot(u, r)
                    weight(u, r)
                    pick_experts(u + 2, nxt, b * 2 + (2 if j == 1 else (3 if nxt < 2 else 4)))
                    add(u - 1, (r - 1) % TT)
            for u in range(NU - 3, NU):
                dot(u, u % TT)
                weight(u, u % TT)
                if u == NU - 3:
                    pick_experts(NU - 1, TT - 1, 2 * PH)
                add(u - 1, (u - 1) % TT)
            add(NU - 1, TT - 1)

        @block.gpsimd
        def _(pool):
            for it in range(HB + 1):
                if it < HB:
                    pool.wait_ge(s["zb_min"], it + 1)
                    pool.wait_ge(s["sp_ready"], it + 1)
                    pool.tensor_tensor(beta[it % 3], beta[it % 3], spb[it % 2], ALU.subtract).then_inc(s["beta_ready"], 1)
                if it >= 1:
                    h = it - 1
                    pool.wait_ge(s["a_exp"], h + 1)
                    for st in range(TT):
                        d = beta[h % 3][:, B_OFF[st]:B_OFF[st] + P]
                        ins = pool.tensor_tensor(d, d, past_tri, ALU.mult)
                    ins.then_inc(s["b_ready"], 1)
            pool.wait_ge(s["zb_done"], HB)
            pool.memset(c_att, 0.0).then_inc(s["att_zero"], 1)
            pool.wait_ge(s["rsil"], 1)
            pool.tensor_tensor(rc, rc, vcol(V_ONG, T).unsqueeze(1).broadcast_to([P, TT, T]), ALU.mult).then_inc(s["rgain"], 1)

            GROUP = 4

            def rows(table, r, ring, arrived, used, u, i0):
                pool.wait_ge(used, u * PK + i0 + GROUP)
                pool.sem_inc(s["pool_go"], 1)
                for i in range(i0, i0 + GROUP):
                    pool.indirect_dma_start(out=ring[i % R], out_offset=None, in_=table,
                                            in_offset=bass.IndirectOffsetOnAxis(ap=experts[r][:, i:i + 1], axis=0))\
                        .then_inc(arrived[i % R], 16)

            def rows_u(u, r, i0):
                if i0 == 0:
                    pool.wait_ge(s["picked"], u + 1)
                rows(u_table, r, u_ring, u_in, s["u_used"], u, i0)

            def rows_v(u, r, i0):
                rows(v_table, r, v_ring, v_in, s["dg_used"], u, i0)

            for i0 in range(0, PK, GROUP):
                rows_u(0, 0, i0)
            with pool.Fori(0, PH - 1) as b:
                for j in range(1, TT + 1):
                    for i0 in range(0, PK, GROUP):
                        rows_u(b * TT + j, j % TT, i0)
                        rows_v(b * TT + j - 1, j - 1, i0)
            for u in range(NU - 3, NU):
                for i0 in range(0, PK, GROUP):
                    rows_u(u, u % TT, i0)
                    rows_v(u - 1, (u - 1) % TT, i0)
            for i0 in range(0, PK, GROUP):
                rows_v(NU - 1, TT - 1, i0)


def laid_out(inp):
    d = {k: np.asarray(v) for k, v in inp.items()}
    w = d["w_in"][0]
    o = np.cumsum([0, 512, 64, 64, 256, 64, 4, 512, 512, 512, 256, 256, 512, 512, 16, 3 * D])
    aq, ak, av, iq, ik, iw, bq, bk, bv, cq, ck, cv, cr, ca, gl = (w[:, o[i]:o[i + 1]] for i in range(15))

    def by_tile(m):
        return m.reshape(-1, P, m.shape[1] // P, P).transpose(1, 2, 0, 3).reshape(P, -1)

    def by_row(m):
        return m.reshape(-1, P, m.shape[1]).transpose(1, 0, 2).reshape(P, -1)

    proj = np.stack([by_tile(aq), by_tile(np.concatenate([ak, ak, iq, ik, ik], 1)), by_tile(bq), by_tile(bk),
                     by_row(bv), by_row(cv), by_tile(np.concatenate([cq, ck], 1)), by_row(cr)])
    merge = []
    wo = [d[k][0] for k in ("w_oa", "w_ob", "w_oc")]
    for c in range(KT):
        cols = slice(P * c, P * (c + 1))
        merge.append(np.concatenate([by_row(gl[:, D * b:D * (b + 1)][:, cols]) for b in range(3)]
                                    + [by_row(m[:, cols]) for m in wo], 1))

    def groups(m):
        return np.stack([by_tile(m[:, 512 * g:512 * (g + 1)]) for g in range(m.shape[1] // 512)])

    def col(v):
        return v.reshape(-1, P).T

    vec = np.concatenate(
        [col(d["c"][0]), col(d["b_mod"][0]), col(d["norm1_g"][0]), col(d["norm2_g"][0]), col(d["b_gate"][0]),
         col(d["c_b_alpha"][0])] + [np.tile(d[k][0], 2)[:, None] for k in ("a_qn_g", "a_kn_g", "b_qn_g", "b_kn_g")]
        + [np.tile(d["c_on_g"][0], (P, 1))], 1)
    small = np.concatenate([av, iw, ca], 1)
    keys = d["peer_subkeys"][0].transpose(0, 3, 1, 2).reshape(PH, P, 2 * NK)
    pq = np.stack([np.concatenate([by_tile(d["peer_wq"][0][:, 2 * P * h:2 * P * (h + 1)]), keys[h]], 1) for h in range(PH)])
    return {
        "cst": shape_constants(), "vec": vec, "x": d["x"][0], "w_mod": d["w_mod"][0], "w_proj": proj,
        "w_small": by_row(small), "w_alpha": d["c_w_alpha"][0], "w_merge": np.stack(merge),
        "w_out": groups(d["w_out"][0]), "w_pq": pq,
        "u_table": d["peer_u"][0], "v_table": d["peer_v"][0],
    }


def kernel(**inputs):
    import concourse.bacc as bacc
    from concourse.bass_utils import run_bass_kernel_spmd

    nc = bacc.Bacc("TRN2", target_bir_lowering=False, num_devices=1)
    arrays = {k: np.ascontiguousarray(v) for k, v in laid_out(inputs).items()}
    args = [nc.dram_tensor(k, a.shape, mybir.dt.from_np(a.dtype), kind="ExternalInput").ap() for k, a in arrays.items()]
    out = nc.dram_tensor("out", (T, D), F32, kind="ExternalOutput").ap()
    encoder_layer(nc, *args, out)
    r = run_bass_kernel_spmd(nc, [arrays], core_ids=[0])
    return np.asarray(r.results[0]["out"]).reshape(1, T, D)
```

```python
from contextlib import ExitStack

import numpy as np

import concourse.bass as bass
from concourse import mybir

ALU = mybir.AluOpType
ACT = mybir.ActivationFunctionType
F32 = mybir.dt.float32
U32 = mybir.dt.uint32
AX = mybir.AxisListType.X

P = 128
T, D = 512, 1024
KT, TT = D // P, T // P
EPS = 1e-6
HA = HB = 8
HD = 64
NI = 4
TOPK = T // 4
HC, CV = 4, 128
CH = 64
NCH = T // CH
TAU = 16.0
PH, NK, PK = 8, 128, 16
LEVELS = (32, 16, 8, 4, 2, 1)
MASKED = -1e30
HIDDEN, PICKED = -3.0e38, -3.4e38
SMALL = 84
WSLOT, NSLOT = 4608, 3
GROUPS = (3, 3, 2)
OUT_TILES = ((0, 4), (4, 5), (5, 8))
UNIT_W = (KT + 4) * P

C_ID, C_LATER, C_ONES, C_PAST, C_SEL, C_RESET = 0, 128, 256, 384, 512, 640
C_SELT, C_LEVEL = 1152, 2176
C_IOTA = C_LEVEL + 128 * (len(LEVELS) + 1)
C_END = C_IOTA + 16
V_C, V_BMOD, V_G1, V_G2, V_BG, V_BA, V_GAIN, V_ONG = 0, 8, 56, 64, 72, 96, 98, 102
V_END = V_ONG + HC * CV

B_OFF = (0, 512, 1024, 896)
B_COLS = 1280
A_OFF = (0, 128, 384, 768)


def shape_constants():
    c = np.zeros((P, C_END), np.float32)
    p = np.arange(P)[:, None]
    f = np.arange(P)[None, :]
    c[:, C_ID:C_ID + P] = p == f
    c[:, C_LATER:C_LATER + P] = p > f
    c[:, C_ONES:C_ONES + P] = 1.0
    c[:, C_PAST:C_PAST + P] = p < f
    for t in range(8):
        c[:, C_SEL + 16 * t:C_SEL + 16 * (t + 1)] = np.arange(16)[None, :] == 2 * t + p // HD
        c[0:16, C_SELT + P * t:C_SELT + P * (t + 1)] = p[0:16] == 2 * t + f // HD
    c[:, C_RESET:C_RESET + T] = np.arange(T)[None, :] % CH != 0
    for i, w in enumerate(LEVELS):
        same = p // (2 * w) == f // (2 * w)
        c[:, C_LEVEL + P * i:C_LEVEL + P * (i + 1)] = same & (p % (2 * w) < w) & (f % (2 * w) >= w)
    c[:, C_LEVEL + P * len(LEVELS):C_LEVEL + P * (len(LEVELS) + 1)] = p == f
    c[:, C_IOTA:C_IOTA + 16] = np.arange(16)[None, :]
    return c


def places(sizes):
    at, end = {}, 0
    for name, n in sizes:
        at[name] = end
        end += n
    return at, end


AT, SPACE_END = places([
    ("const", C_END), ("vec", V_END), ("mod", 64), ("stat", 320), ("walpha", 256), ("wsmall", KT * SMALL),
    ("w", WSLOT * NSLOT), ("n", KT * T), ("x", TT * D),
    ("qa", 4 * T), ("ka", T), ("iq", 2 * T), ("ik", T), ("qb", 4 * T), ("kb", 4 * T),
    ("cq", 2 * T), ("ck", 2 * T), ("ca", T), ("va", TT * 68), ("vb", TT * T), ("vc", TT * T), ("rc", TT * T),
    ("ya", 4 * T), ("yb", 4 * T), ("yc", 4 * T), ("sq", 2 * T), ("pen", 1280),
])


def weight_stream():
    order = [("mod1", i) for i in range(KT // 2)] + [("proj", 0)]
    for i in range(KT):
        order += ([("proj", i + 1)] if i + 1 < KT else []) + [("mod2", i)]
    stream = [(kind, i, n % NSLOT) for n, (kind, i) in enumerate(order)]
    merges = [("merge", i, i % (NSLOT - 1)) for i in range(3 * len(GROUPS))]
    return stream + merges + [("out", 0, 1), ("out", 1, NSLOT), ("out", 2, 0)]


def jobs_of_projection():
    jobs = [("d", 0, i, ("qa", i), i) for i in range(4)]
    jobs += [("d", 1, 0, ("ka", 0), 4), ("d", 1, 1, ("iq", 0), None), ("d", 1, 2, ("iq", 1), None)]
    jobs += [("s", None, t, "va", None) for t in range(TT)] + [("c", None, 0, "ca", None)]
    jobs += [("d", 2, i, ("qb", i), 5 + i) for i in range(4)] + [("d", 3, i, ("kb", i), 9 + i) for i in range(4)]
    jobs += [("t", 4, t, "vb", None) for t in range(TT)] + [("t", 5, t, "vc", None) for t in range(TT)]
    jobs += [("d", 6, i, (("cq", 0), ("cq", 1), ("ck", 0), ("ck", 1))[i], None) for i in range(4)]
    jobs += [("t", 7, t, "rc", None) for t in range(TT)]
    return jobs


def encoder_layer(nc, cst, vec, x, x_turned, w_mod, w_proj, w_small, w_alpha, w_merge, w_out, w_pq,
                  u_table, v_table, out):
    with ExitStack() as ctx:
        sb = ctx.enter_context(nc.sbuf_tensor("sb", [P, SPACE_END + 32], F32))
        ps = ctx.enter_context(nc.psum_tensor("ps", [P, 8 * 512], F32))

        def sem(name):
            return ctx.enter_context(nc.semaphore(name))

        def area(name, lo=0, n=None, p0=0, p1=P):
            a = AT[name] + lo
            return sb[p0:p1, a:a + n]

        def bank(b, n=512, lo=0, p0=0, p1=P):
            return ps[p0:p1, 512 * b + lo:512 * b + lo + n]

        def tiles(ap, n):
            return ap.rearrange("p (a b) -> p a b", a=n)

        ident = area("const", C_ID, P)
        later_tri = area("const", C_LATER, P)
        ones = area("const", C_ONES, P)
        past_tri = area("const", C_PAST, P)
        reset = area("const", C_RESET, T)

        def vcol(i, n=1):
            return area("vec", i, n)

        SH1, SC1, GT1, SH2, SC2, GT2 = (8 * i for i in range(6))

        def mcol(i, n=1):
            return area("mod", i, n)

        amp1 = area("mod", 48, 8)
        amp2 = area("mod", 56, 8)
        cact = area("stat", 0, 8)
        xss, xvar, xrt, xr, xt1 = (area("stat", 8 + 4 * i, 4) for i in range(5))
        top8 = area("stat", 28, 8)
        amax = area("stat", 40, 32)
        anmax = area("stat", 72, 32)
        asum = area("stat", 104, 32)
        arcp = area("stat", 136, 32)
        ebl = area("stat", 168, 16)
        css, cvar, crt, crs, ct1 = (area("stat", 184 + 16 * i, 16) for i in range(5))
        walpha = area("walpha", 0, 256, 0, 16)
        wsmall = tiles(area("wsmall", 0, KT * SMALL), KT)
        n_t = tiles(area("n", 0, KT * T), KT)
        x_tm = tiles(area("x", 0, TT * D), TT)
        xhat = tiles(area("vb", 0, TT * D), TT)
        qa, ka = tiles(area("qa", 0, 4 * T), 4), area("ka", 0, T)
        iq, ik = tiles(area("iq", 0, 2 * T), 2), area("ik", 0, T)
        qb, kb = tiles(area("qb", 0, 4 * T), 4), tiles(area("kb", 0, 4 * T), 4)
        cqk = area("cq", 0, 4 * T)
        ca = area("ca", 0, T, 0, 16)
        ca_tm = area("vb", 0, 16 * TT)
        va = tiles(area("va", 0, TT * 68), TT)
        vb, vc, rc = (tiles(area(k, 0, TT * T), TT) for k in ("vb", "vc", "rc"))
        ya, yb, yc = (tiles(area(k, 0, 4 * T), 4) for k in ("ya", "yb", "yc"))
        sq = [area("sq", T * i, T) for i in range(2)]

        def pen(qt):
            return area("pen", A_OFF[qt], P * (qt + 1))

        irelu = [area("rc", T * i, T) for i in range(2)]
        st_var, st_rt, st_r, st_t = (area("ya", T * i, T, 0, 16) for i in range(4))
        prob = [area("x", T * i, T) for i in range(3)]
        probT = [area("x", 1536 + T * i, T) for i in range(2)]
        o_tm = area("x", 2560, T)
        spb = [area("x", B_COLS * i, B_COLS) for i in range(2)]
        keep = [area("x", 2 * B_COLS, B_COLS), area("qa", 0, B_COLS)]
        beta = [area("qa", B_COLS, B_COLS), area("qa", 2 * B_COLS, B_COLS), area("pen", 0, B_COLS)]
        keep_sum = area("wsmall", 0, 3 * P)
        c_qk = [area("x", 0, 4 * T), area("x", 4 * T, 4 * T)]
        c_e = area("qa", 0, 4 * T)
        c_qk0 = area("qa", 4 * T, 4 * T)
        c_att = area("qb", 0, 4 * T)
        c_state = area("kb", 0, 2 * P * NCH)
        c_b = area("vb", 0, 2 * T)
        c_kdt = area("pen", 0, 2 * T)

        def kv_at(c, i):
            return 1024 * (c % 2) + 2 * P * (c // 2) + P * i

        def head_at(t, h):
            return P * (8 * (h % 2) + 2 * t + h // 2)

        merged = tiles(area("w", WSLOT * (NSLOT - 1), KT * T), KT)
        gates = sq
        gated = area("vb", 2 * T, T)
        NG = 3 * KT

        def gate_bank(n):
            if n < KT:
                return 7
            return 6 if n < KT + 2 else 0 if n < 2 * KT else 4 + n % 2 if n < 2 * KT + 2 else n % 2

        def out_bank(n):
            return 7 if n < KT + 2 else 1 if n < 2 * KT else 2 + n % 2

        h_t = tiles(area("ya", 0, KT * T), KT)
        x_ch = tiles(area("x", 0, KT * T), KT)
        yg = [tiles(area("yc", D * i, D), KT) for i in range(2)]
        squares = tiles(area("const", C_SELT, D), KT)
        nvar, nrt, nr, ntmp, hsq_sum = (area("pen", P * (i + 1), P) for i in range(5))
        h_tm = x_tm
        n2_tm = tiles(area("vb", 0, TT * D), TT)
        NU = TT * PH
        R = 8
        pq_slot = area("cq", 0, 2 * D + 2 * NK)
        qp = sq
        g2row = area("yc", 0, D)
        g2tmp = squares
        u_ring = [area("qa", D * i, D) for i in range(R)]
        v_ring = [area("w", D * i, D) for i in range(R)]
        acc_tmp = area("ya", 0, D)
        PICK_STEPS = 20
        at = AT["rc"]
        pick = {}
        for nm, n in (("sc", 2 * NK), ("left", 2 * NK), ("top", 32), ("best", 16), ("cand", 256), ("cleft", 256),
                      ("eq", 512), ("hl", 32), ("ixf", 32), ("ef", 32)):
            pick[nm] = sb[:, at:at + n]
            at += n
        ix_u = sb[:, at:at + 32].bitcast(U32)
        bj_u = sb[:, at + 32:at + 48].bitcast(U32)
        hl_u = sb[:, at + 48:at + 80].bitcast(U32)
        assert at + 80 <= AT["rc"] + TT * T
        at = AT["const"] + C_RESET
        dgw = [sb[:, at + P * i:at + P * (i + 1)] for i in range(4)]
        experts = [area("pen", PK * i, PK).bitcast(U32) for i in range(TT)]
        best = [area("pen", PK * (TT + i), PK) for i in range(TT)]
        at = AT["stat"]
        dots, gelu, ebest, wgt = ([sb[:, at + 32 * j + 16 * i:at + 32 * j + 16 * i + 16] for i in range(2)] for j in range(4))
        zsum = [sb[:, at + 128 + i:at + 129 + i] for i in range(2)]
        zinv = [sb[:, at + 130 + i:at + 131 + i] for i in range(2)]

        ld_const, ld_small, ld_vec, ld_x = (sem(s) for s in ("ld_const", "ld_small", "ld_vec", "ld_x"))
        w_in = [sem(f"w_in{i}") for i in range(NSLOT + 1)]
        w_used = sem("w_used")
        v_step = sem("v_step")
        names = """csig cact_ready mod1_used mod2_scaled mod2_used xss_ready xvar_ready xrt_ready xhat_ready mod1_done
                   mod1_read tr_done nt_ready proj_done proj_out sq_ready sq_used stat_var stat_rt
                   stat_r xa_done xa_read ik_out ik_twice ka_twice xi_done xi_read irelu_used xb_done xb_read mod2_done
                   mod2_read la_done la_read nmax_ready prob_ready pt_done pt_out pv_done o_ready
                   ot_done ot_out zb_done zb_abs zb_relu zb_min sp_ready beta_ready keep_ready ksum_step ksum_ready
                   lt_done sum_ready b_exp a_exp b_ready yb_done yb_out cu_done cu_ready cabs csp
                   cb_ready ce_ready cex_ready cqk_ready kdt_done kdt_out kv_done ebl_ready st_ready
                   lev_done lev_read att_ready co_done css_ready cvar_ready crt_ready rsil rgain
                   co_ready yct_done yct_out gl_done gate_ready ob_done gate_used merged_ready
                   yo_done yg_ready ht_ready hsq_ready hsq_summed hsq_used nvar_ready nrt_ready
                   nx_ready n2_ready att_zero ld_pq pq_used ld_x2 first_q first_q_out first_sc
                   tm_done tm_out pq_done pq_out sc_done sc_read g2t_ready g2_done g2_ready picked
                   pool_go acc_free u_used dots_ready gelu_ready z_ready w_ready dg_ready dg_used
                   acc_done added p_step stored zi_ready gated2 p_go""".split()
        u_in = [sem(f"u_in{i}") for i in range(R)]
        v_in = [sem(f"v_in{i}") for i in range(R)]
        s = {nm: sem(nm) for nm in names}

        stream = weight_stream()

        def slot_of(kind, i):
            n = [e[:2] for e in stream].index((kind, i))
            place = stream[n][2]
            view = area("w", WSLOT * place, WSLOT) if place < NSLOT else area("w", WSLOT - KT * P, KT * P)
            return view, w_in[place], 16 * sum(e[2] == place for e in stream[:n + 1])

        def reader(n):
            return stream[n][0] if stream[n][0] in ("mod1", "mod2") else "pe"

        def place_free(n):
            if stream[n][2] == NSLOT:
                before = [m for m in range(n) if stream[m][2] == 0][:-1]
            else:
                before = [m for m in range(n) if stream[m][2] == stream[n][2]]
            if not before:
                return None
            kind = reader(before[-1])
            count = sum(reader(m) == kind for m in range(before[-1] + 1))
            return {"mod1": s["mod1_used"], "mod2": s["mod2_used"], "pe": w_used}[kind], count

        jobs = jobs_of_projection()
        NJ = len(jobs)
        N_STAT = sum(j[4] is not None for j in jobs)
        J_A = min(i for i, j in enumerate(jobs) if j[3] == "vc")

        def job_bank(j):
            return j % 4 if j < J_A else 7

        J_SMALL = max(i for i, j in enumerate(jobs) if j[0] == "c")
        mod1_sum, mod2_sum = area("qa", 0, 2 * D), area("yb", 0, 4 * D)

        block = ctx.enter_context(nc.Block())

        @block.sync
        def _(sp):
            sp.dma_start(area("vec", 0, V_END), vec).then_inc(ld_vec, 16)
            sp.dma_start(x_tm[:, :, :], x.rearrange("(t p) d -> p t d", p=P)).then_inc(ld_x, 16)
            wm = w_mod.rearrange("(k p) n -> p k n", p=P)
            for n, (kind, i, place) in enumerate(stream):
                dst = slot_of(kind, i)[0]
                if place_free(n):
                    sp.wait_ge(*place_free(n))
                if kind == "mod1":
                    dst, src = tiles(dst[:, 0:4096], 2), wm[:, 2 * i:2 * i + 2, 0:2 * D]
                elif kind == "mod2":
                    dst, src = dst[:, 0:4096], wm[:, i, 2 * D:6 * D]
                elif kind == "proj":
                    dst, src = dst[:, 0:4096], w_proj[i]
                elif kind == "merge":
                    dst, src = dst[:, 0:GROUPS[i % 3] * UNIT_W], w_merge[i][:, 0:GROUPS[i % 3] * UNIT_W]
                else:
                    lo, hi = OUT_TILES[i]
                    dst, src = dst[:, 0:(hi - lo) * KT * P], w_out[:, lo * KT * P:hi * KT * P]
                sp.dma_start(dst, src).then_inc(w_in[place], 16)
                if (kind, i) == ("mod1", 1):
                    sp.dma_start(area("const", 0, C_SEL), cst[:, 0:C_SEL]).then_inc(ld_const, 16)
                if (kind, i) == ("mod1", 3):
                    sp.dma_start(area("const", C_SEL, C_END - C_SEL), cst[:, C_SEL:C_END]).then_inc(ld_small, 16)
                    sp.dma_start(area("wsmall", 0, KT * SMALL), w_small).then_inc(ld_small, 16)
                    sp.dma_start(walpha, w_alpha).then_inc(ld_small, 16)
                if (kind, i) == ("merge", 7):
                    sp.wait_ge(s["lev_done"], len(LEVELS) + 1)
                    sp.dma_start(area("x", 0, KT * T), x_turned).then_inc(s["ld_x2"], 16)
                    sp.dma_start(pq_slot, w_pq[0]).then_inc(s["ld_pq"], 16)
            for h in range(1, PH):
                sp.wait_ge(s["pq_used"], h)
                sp.dma_start(pq_slot, w_pq[h]).then_inc(s["ld_pq"], 16)
            for t in range(TT):
                sp.wait_ge(s["added"], TT * (PH - 1) + t + 1)
                sp.dma_start(out[P * t:P * (t + 1), :], h_tm[:, t, :]).then_inc(s["stored"], 16)
            sp.wait_ge(s["stored"], 16 * TT)

        TURNS = [(which, t, half) for which, t in [("n", t) for t in range(TT)] + [("h", t) for t in range(TT)] for half in range(2)]
        def query_place(g, c):
            n = FIRST[g][1]
            return bank(3, n, n * c + (2 * P if g == 1 else 0))

        def turn_bank(m):
            return m if m < 2 else 4 + m % 2

        FIRST = ((0, P), (P, P), (2 * P, 2 * P))

        def arrived(eng, kind, i):
            view, sem_, count = slot_of(kind, i)
            eng.wait_ge(sem_, count)
            return view

        MOD_AT = (31, 33)

        def job_after(it):
            j = J_A + it // 3
            return j if it % 3 == 1 and j < NJ else None

        @block.tensor
        def _(pe):
            def column_sums(b, shares, n):
                for j in range(n):
                    mm = pe.matmul(bank(b, 1, j), shares[:, P * j:P * (j + 1)], ones[:, 0:1],
                                   start=(j == 0), stop=True, skip_group_check=True)
                return mm

            pe.wait_ge(ld_const, 16)
            def turn(k):
                for t in range(TT):
                    mm = pe.transpose(bank(k, P, P * t), xhat[:, t, P * k:P * (k + 1)], ident)
                mm.then_inc(s["tr_done"], 1)

            pe.wait_ge(s["xhat_ready"], TT)
            for k in range(KT - 1):
                turn(k)
            pe.wait_ge(s["mod1_used"], KT // 2)
            column_sums(7, mod1_sum, 2 * KT).then_inc(s["mod1_done"], 1)
            pe.wait_ge(s["mod1_read"], 1)
            turn(KT - 1)
            pe.wait_ge(ld_small, 3 * 16)

            def square_sums(i):
                pe.wait_ge(s["sq_ready"], i + 1)
                t, b = (i, 6) if i < 5 else (i - 5, 7)
                if i == 5:
                    pe.wait_ge(s["mod1_read"], 1)
                sel = area("const", C_SEL + 16 * t, 16)
                pe.matmul(bank(b, T, 0, 0, 16), sel, sq[i % 2], start=(t == 0), stop=(i in (4, N_STAT - 1)))\
                  .then_inc(s["sq_used"], 1)

            def spread(done, i, t):
                sel = area("const", C_SELT + P * t, P, 0, 16)
                pe.matmul(bank(4 + i % 2), sel, st_r, start=True, stop=True).then_inc(done, 1)

            views = {}

            def project(j):
                kind, slot, i, dst, stat = jobs[j]
                if kind in "dt" and i == 0:
                    views[slot] = arrived(pe, "proj", slot)[:, 0:4096]
                if j >= J_A:
                    pe.wait_ge(s["proj_out"], j)
                elif j >= 4:
                    pe.wait_ge(s["proj_out"], j - 3)
                b = job_bank(j)
                for k in range(KT):
                    if j == 0:
                        pe.wait_ge(s["nt_ready"], k + 1)
                    if kind == "d":
                        w = views[slot].rearrange("p (i k n) -> p i k n", i=4, k=KT)
                        mm = pe.matmul(bank(b), w[:, i, k, :], n_t[:, k, :], start=(k == 0), stop=(k == KT - 1))
                    elif kind == "t":
                        mm = pe.matmul(bank(b), n_t[:, k, P * i:P * (i + 1)], tiles(views[slot], KT)[:, k, :],
                                       start=(k == 0), stop=(k == KT - 1))
                    elif kind == "s":
                        mm = pe.matmul(bank(b, SMALL), n_t[:, k, P * i:P * (i + 1)], wsmall[:, k, :],
                                       start=(k == 0), stop=(k == KT - 1))
                if kind == "c":
                    pe.wait_ge(s["proj_out"], j)
                    for t in range(TT):
                        mm = pe.transpose(bank(b, P, P * t, 0, 16), ca_tm[:, 16 * t:16 * (t + 1)], ident)
                mm.then_inc(s["proj_done"], 1)
                if kind in "dt" and (j + 1 == NJ or jobs[j + 1][1] != slot):
                    pe.wait_ge(s["proj_done"], j + 1)
                    pe.sem_inc(w_used, 1)

            for j in range(J_A):
                project(j)
                if j >= 1 and jobs[j - 1][4] is not None:
                    square_sums(jobs[j - 1][4])
                if j == J_SMALL:
                    pe.wait_ge(s["stat_r"], 1)
                    for t in range(5):
                        if t >= 2:
                            pe.wait_ge(s["xa_read"], t - 1)
                        spread(s["xa_done"], t, t)
                    pe.wait_ge(s["proj_out"], J_SMALL + 1)
                    pe.wait_ge(s["xa_read"], 5)
                    pe.wait_ge(s["ik_twice"], 16)
                    m = 0
                    for qt in range(1, TT):
                        for h in range(NI):
                            if m >= 2:
                                pe.wait_ge(s["xi_read"], m - 1)
                            r = HD * (h % 2)
                            pe.matmul(bank(4 + m % 2, P * (qt + 1)), iq[r:r + HD, h // 2, P * qt:P * (qt + 1)],
                                      ik[r:r + HD, 0:P * (qt + 1)], start=True, stop=True).then_inc(s["xi_done"], 1)
                            m += 1
            pe.wait_ge(s["stat_r"], 2)
            pe.wait_ge(s["xi_read"], 12)
            for t in range(8):
                if t >= 2:
                    pe.wait_ge(s["xb_read"], t - 1)
                spread(s["xb_done"], t, t)

            pe.wait_ge(s["proj_out"], J_A)
            NA = TT * HA
            for it in range(NA + 5):
                if it < NA:
                    qt, h = divmod(it, HA)
                    r = HD * (h % 2)
                    if it == 0:
                        pe.wait_ge(s["ka_twice"], 16)
                    if it >= 2:
                        pe.wait_ge(s["la_read"], it - 1)
                    pe.matmul(bank(it % 2, P * (qt + 1)), qa[r:r + HD, h // 2, P * qt:P * (qt + 1)],
                              ka[r:r + HD, 0:P * (qt + 1)], start=True, stop=True).then_inc(s["la_done"], 1)
                if 1 <= it <= NA:
                    j = it - 1
                    qt = j // HA
                    pe.wait_ge(s["prob_ready"], j + 1)
                    if j >= 2:
                        pe.wait_ge(s["pt_out"], j - 1)
                    for st in range(qt + 1):
                        mm = pe.transpose(bank(2 + j % 2, P, P * st), prob[j % 3][:, P * st:P * (st + 1)], ident)
                    mm.then_inc(s["pt_done"], 1)
                if 2 <= it <= NA + 1:
                    j = it - 2
                    qt, h = divmod(j, HA)
                    pe.wait_ge(s["pt_out"], j + 1)
                    if j == 0:
                        pe.wait_ge(s["xb_read"], 8)
                    if h == 0 and qt >= 2:
                        pe.wait_ge(s["o_ready"], qt - 1)
                    for st in range(qt + 1):
                        mm = pe.matmul(bank(4 + qt % 2, HD, HD * h), probT[j % 2][:, P * st:P * (st + 1)],
                                       va[:, st, 0:HD], start=(st == 0), stop=(st == qt))
                    mm.then_inc(s["pv_done"], 1)
                if it >= 4 and (it - 4) % HA == HA - 1:
                    qt = (it - 4) // HA
                    pe.wait_ge(s["o_ready"], qt + 1)
                    if qt >= 1:
                        pe.wait_ge(s["ot_out"], qt)
                    for f in range(4):
                        mm = pe.transpose(bank(6, P, P * f), o_tm[:, P * f:P * (f + 1)], ident)
                    mm.then_inc(s["ot_done"], 1)
                if job_after(it) is not None:
                    project(job_after(it))
                if it == NA + 1:
                    pe.wait_ge(s["mod2_used"], KT)
                    pe.wait_ge(s["o_ready"], TT - 1)
                    column_sums(4, mod2_sum, 4 * KT).then_inc(s["mod2_done"], 1)

            def gate_product(n):
                br, c = divmod(n, KT)
                if c % 3 == 0:
                    views[br, c // 3] = arrived(pe, "merge", 3 * br + c // 3)
                w = views[br, c // 3][:, UNIT_W * (c % 3):UNIT_W * (c % 3 + 1)]
                if n >= 1:
                    pe.wait_ge(s["gate_ready"], n)
                    if gate_bank(n) == 7:
                        pe.wait_ge(s["gate_used"], n)
                for k in range(KT):
                    mm = pe.matmul(bank(gate_bank(n)), w[:, P * k:P * (k + 1)], n_t[:, k, :], start=(k == 0), stop=(k == KT - 1))
                mm.then_inc(s["gl_done"], 1)

            def out_product(n):
                br, c = divmod(n, KT)
                w = views[br, c // 3][:, UNIT_W * (c % 3):UNIT_W * (c % 3 + 1)]
                if gate_bank(n) == 7:
                    pe.wait_ge(s["gate_ready"], n + 1)
                if n >= 2 * KT + 1:
                    pe.wait_ge(s["gate_used"], n - 1)
                elif n >= 1:
                    pe.wait_ge(s["gate_used"], n)
                for k in range(4):
                    mm = pe.matmul(bank(out_bank(n)), w[:, P * (KT + k):P * (KT + k + 1)], (ya, yb, yc)[br][:, k, :],
                                   start=(k == 0), stop=(k == 3))
                mm.then_inc(s["ob_done"], 1)
                if c % 3 == 2 or c == KT - 1:
                    pe.wait_ge(s["ob_done"], n + 1)
                    pe.sem_inc(w_used, 1)

            pe.wait_ge(s["ot_out"], TT)
            pe.wait_ge(s["mod2_read"], 1)
            pe.wait_ge(s["proj_out"], NJ)

            for it in range(HB + 2):
                if it < HB:
                    r = HD * (it % 2)
                    if it >= 1:
                        pe.wait_ge(s["zb_abs"], it)
                        pe.wait_ge(s["zb_relu"], it)
                        pe.wait_ge(s["zb_min"], it)
                    for st in range(TT):
                        n = T - P * st
                        mm = pe.matmul(ps[:, B_OFF[st]:B_OFF[st] + n], kb[r:r + HD, it // 2, P * st:P * (st + 1)],
                                       qb[r:r + HD, it // 2, P * st:T], start=True, stop=True)
                    mm.then_inc(s["zb_done"], 1)
                    gate_product(it)
                if 1 <= it <= HB:
                    h = it - 1
                    pe.wait_ge(s["keep_ready"], h + 1)
                    if h >= 1:
                        pe.wait_ge(s["sum_ready"], h)
                    pe.wait_ge(s["ksum_ready"], h + 1)
                    kp = keep[h % 2]
                    for st in range(TT):
                        o = 1536 + B_OFF[st]
                        mm = pe.matmul(ps[:, o:o + T - P * st], later_tri, kp[:, B_OFF[st]:B_OFF[st] + T - P * st],
                                       start=True, stop=(st == TT - 1), skip_group_check=True)
                        if st < TT - 1:
                            mm = pe.matmul(ps[:, o + P:o + 2 * P], ones, kp[:, B_OFF[st + 1]:B_OFF[st + 1] + P],
                                           start=False, stop=(st == TT - 2), skip_group_check=True)
                        if st < TT - 2:
                            mm = pe.matmul(ps[:, o + 2 * P:o + T - P * st], ones, keep_sum[:, 2 * P * st:2 * P * st + T - P * (st + 2)],
                                           start=False, stop=True, skip_group_check=True)
                    mm.then_inc(s["lt_done"], 1)
                if it < HB:
                    out_product(it)
                if it >= 2:
                    h = it - 2
                    pe.wait_ge(s["b_ready"], h + 1)
                    if h % 2 == 0 and h >= 2:
                        pe.wait_ge(s["yb_out"], h // 2)
                    r = HD * (h % 2)
                    for st in range(TT):
                        mm = pe.matmul(bank(6, T - P * st, P * st, r, r + HD), vb[:, st, HD * h:HD * (h + 1)],
                                       beta[h % 3][:, B_OFF[st]:B_OFF[st] + T - P * st],
                                       start=(st == 0), stop=(st == TT - 1), skip_group_check=True)
                    mm.then_inc(s["yb_done"], 1)

            pe.wait_ge(s["zb_abs"], HB)
            pe.wait_ge(s["zb_relu"], HB)
            pe.wait_ge(s["zb_min"], HB)
            for i in range(2):
                mm = pe.matmul(bank(i), walpha[:, P * i:P * (i + 1)], ca, start=True, stop=True)
            mm.then_inc(s["cu_done"], 1)
            pe.wait_ge(s["yb_out"], 4)
            gate_product(KT)
            out_product(KT)
            gate_product(KT + 1)
            pe.wait_ge(s["cqk_ready"], 1)
            pe.wait_ge(s["sum_ready"], HB)
            for t in range(TT):
                for i in range(2):
                    mm = pe.transpose(bank(4, P, 2 * P * t + P * i), c_qk0[:, 2 * T + T * i + P * t:2 * T + T * i + P * (t + 1)], ident)
            mm.then_inc(s["kdt_done"], 1)
            out_product(KT + 1)
            pe.wait_ge(s["kdt_out"], 1)
            pe.wait_ge(s["cu_ready"], 1)
            kdt = tiles(c_kdt, TT)
            for c in range(NCH):
                for h in range(HC):
                    r, q = CH * (c % 2), HD * (h % 2)
                    o = kv_at(c, h // 2)
                    mm = pe.matmul(ps[q:q + HD, o:o + P], kdt[r:r + CH, c // 2, HD * h:HD * (h + 1)],
                                   vc[r:r + CH, c // 2, CV * h:CV * (h + 1)], start=True, stop=True)
            mm.then_inc(s["kv_done"], 1)
            pe.wait_ge(s["gate_used"], KT + 2)
            for lv in range(len(LEVELS) + 1):
                pe.wait_ge(s["cqk_ready"], min(lv + 2, len(LEVELS) + 1))
                if lv >= 1:
                    pe.wait_ge(s["lev_read"], lv)
                qk = cqk if lv == len(LEVELS) else c_qk[lv % 2]
                for t in range(TT):
                    for h in range(HC):
                        q = HD * (h % 2)
                        a = T * (h // 2) + P * t
                        mm = pe.matmul(ps[:, 2048 + head_at(t, h):2048 + head_at(t, h) + P],
                                       qk[q:q + HD, 2 * T + a:2 * T + a + P], qk[q:q + HD, a:a + P],
                                       start=True, stop=True)
                mm.then_inc(s["lev_done"], 1)
                if lv == 0:
                    pe.wait_ge(s["st_ready"], NCH - 1)
                if lv < len(LEVELS):
                    gate_product(KT + 2 + lv)
                if lv < len(LEVELS) - 1:
                    out_product(KT + 2 + lv)
            out_product(2 * KT - 1)
            pe.wait_ge(s["gate_ready"], 2 * KT)
            pe.wait_ge(s["gate_used"], 2 * KT)
            pe.wait_ge(s["att_ready"], 1)
            for t in range(TT):
                for h in range(HC):
                    o = head_at(t, h)
                    pe.matmul(ps[:, o:o + CV], c_att[:, o:o + CV], vc[:, t, CV * h:CV * (h + 1)],
                              start=(t % 2 == 0 and h < 2), stop=True, skip_group_check=True)
            for t in range(TT):
                for c in (2 * t, 2 * t + 1):
                    if c == 0:
                        continue
                    for h in range(HC):
                        r, q = CH * (c % 2), HD * (h % 2)
                        a = T * (h // 2) + CH * c
                        so = 2 * P * c + P * (h // 2)
                        o = head_at(t, h)
                        mm = pe.matmul(ps[r:r + CH, o:o + CV], c_qk0[q:q + HD, a:a + CH],
                                       c_state[q:q + HD, so:so + P], start=False, stop=True, skip_group_check=True)
            mm.then_inc(s["co_done"], 1)
            gate_product(2 * KT)
            gate_product(2 * KT + 1)
            pe.wait_ge(s["gate_ready"], 2 * KT + 2)
            pe.wait_ge(s["co_ready"], 1)
            for f in range(4):
                for t in range(TT):
                    mm = pe.transpose(bank(4 + f, P, P * t), c_e[:, head_at(t, f):head_at(t, f) + P], ident)
            mm.then_inc(s["yct_done"], 1)

            pe.wait_ge(s["yct_out"], 1)
            for n in range(2 * KT, NG):
                out_product(n)
                if n + 2 < NG:
                    gate_product(n + 2)

            pe.wait_ge(s["merged_ready"], 1)
            pe.wait_ge(s["gate_ready"], NG)
            pe.sem_inc(s["u_used"], R)
            w_o = {}

            def output(t, c):
                if c % 4 == 0 and t >= 1:
                    pe.wait_ge(s["yg_ready"], 2 * t - 1 + c // 4)
                for i, (lo, hi) in enumerate(OUT_TILES):
                    if (t, c) == (0, lo):
                        view = arrived(pe, "out", i)
                        for o in range(lo, hi):
                            w_o[o] = tiles(view[:, KT * P * (o - lo):KT * P * (o - lo + 1)], KT)
                for k in range(KT):
                    mm = pe.matmul(bank(4 + c // 4, P, P * (c % 4)), w_o[c][:, k, :], merged[:, k, P * t:P * (t + 1)],
                                   start=(k == 0), stop=(k == KT - 1))
                if c % 4 == 3:
                    mm.then_inc(s["yo_done"], 1)

            def squares_sum(t):
                if t >= 1:
                    pe.wait_ge(s["nvar_ready"], t)
                pe.wait_ge(s["hsq_summed"], t + 1)
                pe.matmul(bank(2, P), ones, hsq_sum, start=True, stop=True).then_inc(s["hsq_used"], 1)

            def first_query(g):
                lo, n = FIRST[g]
                pe.wait_ge(s["ld_pq"], 16)
                if g >= 1:
                    pe.wait_ge(s["sc_read"], 1)
                w = pq_slot[:, 0:2 * D].rearrange("p (i k n) -> p i k n", i=2, k=KT)
                for c in range(2):
                    for k in range(KT):
                        pe.wait_ge(s["n2_ready"], KT * ((lo + n) // P - 1) + k + 1)
                        mm = pe.matmul(query_place(g, c), w[:, c, k, :], n_t[:, k, lo:lo + n],
                                       start=(k == 0), stop=(k == KT - 1))
                mm.then_inc(s["first_q"], 1)

            def first_score(g):
                pe.wait_ge(s["first_q_out"], g + 1)
                lo, n = FIRST[g]
                for t in range(lo // P, (lo + n) // P):
                    for c in range(2):
                        dst = bank(3, NK, NK * c) if t == 0 else bank(6 + t // 2, NK, NK * (2 * (t % 2) + c))
                        mm = pe.matmul(dst, qp[c][:, P * t:P * (t + 1)], pq_slot[:, 2 * D + NK * c:2 * D + NK * (c + 1)],
                                       start=True, stop=True)
                mm.then_inc(s["first_sc"] if g == 0 else s["sc_done"], 1)

            def to_tokens(m):
                which, t, half = TURNS[m]
                if m >= 2:
                    pe.wait_ge(s["tm_out"], m - 1)
                for f in range(4):
                    mm = pe.transpose(bank(turn_bank(m), P, P * f),
                                      {"h": h_t, "n": n_t}[which][:, 4 * half + f, P * t:P * (t + 1)], ident)
                mm.then_inc(s["tm_done"], 1)

            def query(h, c):
                if c == 0:
                    pe.wait_ge(s["ld_pq"], (h + 1) * 16)
                w = pq_slot[:, 0:2 * D].rearrange("p (i k n) -> p i k n", i=2, k=KT)
                for k in range(KT):
                    mm = pe.matmul(bank(4 + c), w[:, c, k, :], n_t[:, k, :], start=(k == 0), stop=(k == KT - 1))
                mm.then_inc(s["pq_done"], 1)

            def score(h, half):
                for t in (2 * half, 2 * half + 1):
                    for c in range(2):
                        mm = pe.matmul(bank(6 + half, NK, NK * (2 * (t % 2) + c)), qp[c][:, P * t:P * (t + 1)],
                                       pq_slot[:, 2 * D + NK * c:2 * D + NK * (c + 1)], start=True, stop=True)
                mm.then_inc(s["sc_done"], 1)
                if half == 1:
                    pe.wait_ge(s["sc_done"], 2 * h + 2)
                    pe.sem_inc(s["pq_used"], 1)

            def between(t, c):
                if (t, c) == (1, 1):
                    squares_sum(0)
                elif (t, c) == (1, 5):
                    first_query(0)
                elif (t, c) == (1, 6):
                    first_score(0)
                elif (t, c) == (1, 7):
                    to_tokens(0)
                    to_tokens(1)
                elif (t, c) == (2, 3):
                    squares_sum(1)
                elif (t, c) == (3, 1):
                    first_query(1)
                elif (t, c) == (3, 3):
                    first_score(1)
                elif (t, c) == (3, 5):
                    squares_sum(2)

            for t in range(TT):
                for c in range(KT):
                    output(t, c)
                    between(t, c)
            pe.wait_ge(s["yo_done"], 2 * TT)
            pe.sem_inc(s["dg_used"], R)
            pe.wait_ge(s["yg_ready"], 2 * TT)
            to_tokens(2)
            to_tokens(3)
            squares_sum(3)
            first_query(2)
            first_score(2)
            pe.wait_ge(s["sc_done"], 2)
            pe.sem_inc(s["pq_used"], 1)
            pe.wait_ge(s["g2t_ready"], 1)
            pe.wait_ge(s["first_q_out"], 3)
            pe.wait_ge(s["nvar_ready"], TT)
            for c in range(KT):
                mm = pe.matmul(ps[:, 2 * T + P * c:2 * T + P * (c + 1)], g2tmp[:, c, :], ident, start=True, stop=True)
            mm.then_inc(s["g2_done"], 1)
            for m in range(4, 2 * TT):
                to_tokens(m)
            pe.wait_ge(s["tm_out"], 2)
            pe.sem_inc(s["acc_free"], 2)

            def weigh(u, par):
                pe.wait_ge(s["acc_free"], u + 1)
                for i in range(PK):
                    pe.wait_ge(s["dg_ready"], u * PK + i + 1)
                    pe.wait_ge(v_in[i % R], (u * (PK // R) + i // R + 1) * 16)
                    for f in range(2):
                        mm = pe.matmul(bank(2 * par + f), dgw[i % 4], v_ring[i % R][:, T * f:T * (f + 1)],
                                       start=(i == 0), stop=(i == PK - 1))
                    if i == PK - 1:
                        mm.then_inc(s["acc_done"], 1)
                        pe.wait_ge(s["acc_done"], u + 1)
                        pe.sem_inc(s["dg_used"], 1)
                    else:
                        mm.then_inc(s["dg_used"], 1)

            weigh(0, 0)
            for m in range(2 * TT, 4 * TT):
                to_tokens(m)
            pe.wait_ge(s["tm_out"], 4 * TT)
            pe.wait_ge(s["g2_ready"], 1)
            query(1, 0)

            def units(h, last=False):
                query(h + 1, 1)
                pe.wait_ge(s["pq_out"], h * 2 + 2)
                pe.wait_ge(s["sc_read"], h * TT + 2)
                score(h + 1, 0)
                weigh(h * TT + 1, 1)
                pe.wait_ge(s["sc_read"], h * TT + 4)
                score(h + 1, 1)
                weigh(h * TT + 2, 0)
                weigh(h * TT + 3, 1)
                if not last:
                    query(h + 2, 0)
                weigh(h * TT + 4, 0)

            with pe.Fori(0, PH - 2) as h:
                units(h)
            units(PH - 2, last=True)
            for t in range(1, TT):
                weigh(TT * (PH - 1) + t, t % 2)

        @block.scalar
        def _(act):
            act.wait_ge(ld_vec, 16)
            act.activation(ct1[:, 0:8], vcol(V_C, 8), ACT.Sigmoid).then_inc(s["csig"], 1)
            act.wait_ge(ld_x, 16)
            for t in range(TT):
                act.activation(area("ya", D * t, D), x_tm[:, t, :], ACT.Square, accum_out=xss[:, t:t + 1])\
                   .then_inc(s["xss_ready"], 1)
            act.wait_ge(s["xvar_ready"], 1)
            act.activation(xrt, xvar, ACT.Sqrt).then_inc(s["xrt_ready"], 1)
            def project_out(j):
                kind, slot, i, dst, stat = jobs[j]
                b = job_bank(j)
                act.wait_ge(s["proj_done"], j + 1)
                if kind == "d":
                    o = area(dst[0], T * dst[1], T)
                    scale = HD ** -0.5 if dst[0] == "cq" else 1.0
                    if dst[0] == "ka":
                        act.activation(ik[HD:P], bank(b, T, 0, HD, P), ACT.Copy).then_inc(s["ik_out"], 1)
                        act.wait_ge(s["ik_out"], 1)
                        act.dma_start(ik[0:HD], ik[HD:P]).then_inc(s["ik_twice"], 16)
                        c = act.activation(ka[0:HD], bank(b, T, 0, 0, HD), ACT.Copy)
                    else:
                        c = act.activation(o, bank(b), ACT.Copy, scale=scale)
                    if stat is not None:
                        if stat >= 2:
                            act.wait_ge(s["sq_used"], stat - 1)
                        act.activation(sq[stat % 2], bank(b), ACT.Square).then_inc(s["sq_ready"], 1)
                        act.wait_ge(s["sq_ready"], stat + 1)
                        act.sem_inc(s["proj_out"], 1)
                    else:
                        c.then_inc(s["proj_out"], 1)
                elif kind == "t":
                    act.activation(area(dst, T * i, T), bank(b), ACT.Copy).then_inc(s["proj_out"], 1)
                elif kind == "s":
                    act.activation(va[:, i, :], bank(b, 68), ACT.Copy)
                    act.activation(ca_tm[:, 16 * i:16 * (i + 1)], bank(b, 16, 68), ACT.Copy).then_inc(s["proj_out"], 1)
                else:
                    act.activation(ca, bank(b, T, 0, 0, 16), ACT.Copy).then_inc(s["proj_out"], 1)

            for j in range(J_A):
                project_out(j)
                if j == 6:
                    act.wait_ge(s["stat_var"], 1)
                    act.activation(st_rt, st_var, ACT.Sqrt).then_inc(s["stat_rt"], 1)
                if j == J_SMALL:
                    act.wait_ge(s["xa_read"], 5)
                    act.dma_start(ka[HD:P], ka[0:HD]).then_inc(s["ka_twice"], 16)
                    for m in range(12):
                        w = P * (m // NI + 2)
                        act.wait_ge(s["xi_done"], m + 1)
                        if m >= 2:
                            act.wait_ge(s["irelu_used"], m - 1)
                        act.activation(irelu[m % 2][:, 0:w], bank(4 + m % 2, w), ACT.Relu).then_inc(s["xi_read"], 1)
                if j == J_A - 3:
                    act.wait_ge(s["stat_var"], 2)
                    act.activation(st_rt, st_var, ACT.Sqrt).then_inc(s["stat_rt"], 1)

            NA = TT * HA
            for it in range(NA + 5):
                if it < NA:
                    n = P * (it // HA + 1)
                    act.wait_ge(s["nmax_ready"], it + 1)
                    act.activation(prob[it % 3][:, 0:n], prob[it % 3][:, 0:n], ACT.Exp, bias=anmax[:, it:it + 1],
                                   accum_out=asum[:, it:it + 1]).then_inc(s["prob_ready"], 1)
                if 1 <= it <= NA:
                    j = it - 1
                    n = P * (j // HA + 1)
                    act.wait_ge(s["pt_done"], j + 1)
                    if j >= 2:
                        act.wait_ge(s["pv_done"], j - 1)
                    act.activation(probT[j % 2][:, 0:n], bank(2 + j % 2, n), ACT.Copy).then_inc(s["pt_out"], 1)
                if it >= 4 and (it - 4) % HA == HA - 1:
                    qt = (it - 4) // HA
                    act.wait_ge(s["ot_done"], qt + 1)
                    if qt == 0:
                        act.wait_ge(s["stat_r"], 2)
                        act.wait_ge(s["xb_read"], 8)
                    act.activation(ya[:, :, P * qt:P * (qt + 1)], tiles(bank(6), 4), ACT.Copy).then_inc(s["ot_out"], 1)
                if job_after(it) is not None:
                    project_out(job_after(it))

            def gate(n):
                act.wait_ge(s["gl_done"], n + 1)
                if n >= 2:
                    act.wait_ge(s["gate_used"], n - 1)
                act.activation(gates[n % 2], bank(gate_bank(n)), ACT.Sigmoid, bias=vcol(V_BG + n)).then_inc(s["gate_ready"], 1)

            for it in range(HB + 2):
                if it < HB:
                    z = ps[:, 0:B_COLS]
                    sp_, kp = spb[it % 2], keep[it % 2]
                    act.wait_ge(s["zb_done"], it + 1)
                    if it >= 2:
                        act.wait_ge(s["keep_ready"], it - 1)
                        act.wait_ge(s["beta_ready"], it - 1)
                    act.activation(sp_, z, ACT.Abs, scale=HD ** -0.5).then_inc(s["zb_abs"], 1)
                    if it >= 2:
                        act.wait_ge(s["lt_done"], it - 1)
                    act.activation(kp, z, ACT.Relu, scale=HD ** -0.5).then_inc(s["zb_relu"], 1)
                    act.wait_ge(s["zb_abs"], it + 1)
                    act.activation(sp_, sp_, ACT.Exp, scale=-1.0).then_inc(s["b_exp"], 1)
                    act.wait_ge(s["b_exp"], it + 1)
                    act.activation(sp_, sp_, ACT.Ln, bias=1.0).then_inc(s["sp_ready"], 1)
                    gate(it)
                if 1 <= it <= HB:
                    h = it - 1
                    act.wait_ge(s["sum_ready"], h + 1)
                    act.activation(beta[h % 3], beta[h % 3], ACT.Exp).then_inc(s["a_exp"], 1)
                if it >= 2 and it % 2 == 1:
                    h = it - 2
                    act.wait_ge(s["yb_done"], h + 1)
                    act.activation(yb[:, h // 2, :], bank(6), ACT.Copy).then_inc(s["yb_out"], 1)

            act.activation(area("rc", 0, TT * T), area("rc", 0, TT * T), ACT.Silu).then_inc(s["rsil"], 1)
            act.wait_ge(s["cu_ready"], 1)
            sp_ = c_e[:, 2 * T:4 * T]
            act.activation(sp_, c_e[:, 0:2 * T], ACT.Abs).then_inc(s["cabs"], 1)
            act.wait_ge(s["cabs"], 1)
            act.activation(sp_, sp_, ACT.Exp, scale=-1.0).then_inc(s["cabs"], 1)
            act.wait_ge(s["cabs"], 2)
            act.activation(sp_, sp_, ACT.Ln, bias=1.0).then_inc(s["csp"], 1)
            gate(KT)
            act.wait_ge(s["cb_ready"], 1)
            act.activation(tiles(ebl, 2), c_b.rearrange("p (i c l) -> p i c l", i=2, l=CH)[:, :, :, CH - 1], ACT.Exp,
                           scale=1 / TAU).then_inc(s["ebl_ready"], 1)
            for lv in range(len(LEVELS) + 1):
                act.wait_ge(s["ce_ready"], lv + 1)
                act.activation(c_e, c_e, ACT.Exp, scale=1 / TAU).then_inc(s["cex_ready"], 1)
                if lv == 1:
                    gate(KT + 1)
                    act.wait_ge(s["kdt_done"], 1)
                    act.activation(c_kdt, ps[:, 2048:2048 + 2 * T], ACT.Copy).then_inc(s["kdt_out"], 1)
                if lv >= 3:
                    gate(KT + lv - 1)
            for n in range(KT + len(LEVELS), 2 * KT):
                gate(n)
            act.wait_ge(s["co_done"], 1)
            act.activation(c_e, ps[:, 0:4 * T], ACT.Square).then_inc(s["css_ready"], 1)
            act.wait_ge(s["cvar_ready"], 1)
            act.activation(crt, cvar, ACT.Sqrt).then_inc(s["crt_ready"], 1)
            gate(2 * KT)
            gate(2 * KT + 1)
            act.wait_ge(s["yct_done"], 1)
            act.activation(area("yc", 0, 4 * T), ps[:, 2048:4096], ACT.Copy).then_inc(s["yct_out"], 1)
            for n in range(2 * KT + 2, NG):
                gate(n)

            def gated_output(t, a):
                act.wait_ge(s["yo_done"], 2 * t + a + 1)
                if t >= 2:
                    act.wait_ge(s["ht_ready"], t - 1)
                for c in range(4 * a, 4 * a + 4):
                    ins = act.activation(yg[t % 2][:, c, :], bank(4 + a, P, P * (c % 4)), ACT.Copy, scale=mcol(GT1 + c))
                ins.then_inc(s["yg_ready"], 1)

            def square(t):
                act.wait_ge(s["ht_ready"], t + 1)
                if t >= 1:
                    act.wait_ge(s["hsq_summed"], t)
                act.activation(squares, h_t[:, :, P * t:P * (t + 1)], ACT.Square).then_inc(s["hsq_ready"], 1)

            def root(t):
                act.wait_ge(s["nvar_ready"], t + 1)
                act.activation(nrt, nvar, ACT.Sqrt).then_inc(s["nrt_ready"], 1)

            def shifted(t):
                act.wait_ge(s["nx_ready"], t + 1)
                for c in range(KT):
                    n = n_t[:, c, P * t:P * (t + 1)]
                    act.activation(n, n, ACT.Identity, scale=amp2[:, c:c + 1], bias=mcol(SH2 + c)).then_inc(s["n2_ready"], 1)

            def first_query_out(g):
                lo, n = FIRST[g]
                act.wait_ge(s["first_q"], g + 1)
                for c in range(2):
                    ins = act.activation(qp[c][:, lo:lo + n], query_place(g, c), ACT.Copy)
                ins.then_inc(s["first_q_out"], 1)

            def tokens_out(m):
                which, t, half = TURNS[m]
                act.wait_ge(s["tm_done"], m + 1)
                act.activation({"h": h_tm, "n": n2_tm}[which][:, t, T * half:T * (half + 1)], bank(turn_bank(m)), ACT.Copy)\
                   .then_inc(s["tm_out"], 1)

            gated_output(0, 0)
            gated_output(0, 1)
            square(0)
            root(0)
            gated_output(1, 0)
            shifted(0)
            first_query_out(0)
            gated_output(1, 1)
            square(1)
            tokens_out(0)
            tokens_out(1)
            gated_output(2, 0)
            gated_output(2, 1)
            root(1)
            shifted(1)
            square(2)
            first_query_out(1)
            gated_output(3, 0)
            gated_output(3, 1)
            tokens_out(2)
            tokens_out(3)
            square(3)
            root(2)
            shifted(2)
            root(3)
            shifted(3)
            first_query_out(2)
            for m in range(4, 2 * TT):
                tokens_out(m)

            def query_out(h, c):
                act.wait_ge(s["pq_done"], h * 2 + c - 1)
                act.wait_ge(s["sc_done"], h * 2)
                act.activation(qp[c], bank(4 + c), ACT.Copy).then_inc(s["pq_out"], 1)

            def weights(u, r):
                act.wait_ge(s["dots_ready"], u + 1)
                act.activation(gelu[r % 2], dots[r % 2], ACT.Gelu).then_inc(s["gelu_ready"], 1)
                act.activation(ebest[r % 2], best[r], ACT.Exp, accum_out=zsum[r % 2]).then_inc(s["z_ready"], 1)

            def diagonals(u, r):
                act.wait_ge(s["w_ready"], u + 1)
                for i in range(PK):
                    act.wait_ge(s["dg_used"], u * PK + i + 1 + R - 4)
                    act.activation(dgw[i % 4], ident, ACT.Copy, scale=wgt[r % 2][:, i:i + 1]).then_inc(s["dg_ready"], 1)

            weights(0, 0)
            diagonals(0, 0)
            for m in range(2 * TT, 4 * TT):
                tokens_out(m)
            query_out(1, 0)

            def units(h, last=False):
                for t in range(1, TT + 1):
                    weights(h * TT + t, t % TT)
                    if t == 1:
                        query_out(h + 1, 1)
                    if t == TT and not last:
                        query_out(h + 2, 0)
                    diagonals(h * TT + t, t % TT)

            with act.Fori(0, PH - 2) as h:
                units(h)
            units(PH - 2, last=True)
            for t in range(1, TT):
                weights(TT * (PH - 1) + t, t)
                diagonals(TT * (PH - 1) + t, t)

        @block.vector
        def _(dve):
            def done(ins):
                v_count[0] += 1
                ins.then_inc(v_step, 1)
                dve.wait_ge(v_step, v_count[0])

            v_count = [0]

            def inverse_root(r, root, var, tmp):
                done(dve.reciprocal(r, root))
                done(dve.tensor_tensor(tmp, r, r, ALU.mult))
                done(dve.tensor_tensor(tmp, tmp, var, ALU.mult))
                done(dve.tensor_scalar(tmp, tmp, -0.5, 1.5, ALU.mult, ALU.add))
                return dve.tensor_tensor(r, r, tmp, ALU.mult)

            dve.wait_ge(s["csig"], 1)
            dve.tensor_tensor(cact, vcol(V_C, 8), ct1[:, 0:8], ALU.mult).then_inc(s["cact_ready"], 1)
            dve.wait_ge(s["xss_ready"], TT)
            dve.tensor_scalar(xvar, xss, 1 / D, EPS, ALU.mult, ALU.add).then_inc(s["xvar_ready"], 1)
            dve.wait_ge(s["xrt_ready"], 1)
            done(inverse_root(xr, xrt, xvar, xt1))
            for t in range(TT):
                dve.tensor_scalar(xhat[:, t, :], x_tm[:, t, :], xr[:, t:t + 1], None, ALU.mult).then_inc(s["xhat_ready"], 1)
            for k in range(KT):
                w = tiles(arrived(dve, "mod1", k // 2)[:, 0:4096], 2)[:, k % 2, :]
                if k == 0:
                    ins = dve.tensor_scalar(mod1_sum, w, cact[:, 0:1], None, ALU.mult)
                else:
                    ins = dve.scalar_tensor_tensor(mod1_sum, w, cact[:, k:k + 1], mod1_sum, ALU.mult, ALU.add)
                done(ins)
                if k % 2:
                    dve.sem_inc(s["mod1_used"], 1)
            dve.wait_ge(s["mod1_done"], 1)
            dve.tensor_tensor(mcol(0, 16), bank(7, 16), vcol(V_BMOD, 16), ALU.add).then_inc(s["mod1_read"], 1)
            dve.wait_ge(s["mod1_read"], 1)
            done(dve.scalar_tensor_tensor(amp1, mcol(SC1, 8), 1.0, vcol(V_G1, 8), ALU.add, ALU.mult))
            for k in range(KT):
                dve.wait_ge(s["tr_done"], k + 1)
                dve.tensor_scalar(n_t[:, k, :], bank(k), amp1[:, k:k + 1], mcol(SH1 + k), ALU.mult, ALU.add)\
                   .then_inc(s["nt_ready"], 1)

            def head_factors(n, b):
                dve.wait_ge(s["sq_used"], (5, N_STAT)[n - 1])
                dve.tensor_scalar(st_var, bank(b, T, 0, 0, 16), 1 / HD, EPS, ALU.mult, ALU.add).then_inc(s["stat_var"], 1)
                dve.wait_ge(s["stat_rt"], n)
                inverse_root(st_r, st_rt, st_var, st_t).then_inc(s["stat_r"], 1)

            head_factors(1, 6)
            dve.wait_ge(s["proj_out"], 5)
            for t in range(5):
                n = P if t < 4 else HD
                dst = qa[:, t, :] if t < 4 else ka[0:HD]
                dve.wait_ge(s["xa_done"], t + 1)
                dve.scalar_tensor_tensor(dst, dst, vcol(V_GAIN + t // 4)[0:n], bank(4 + t % 2, T, 0, 0, n), ALU.mult, ALU.mult)\
                   .then_inc(s["xa_read"], 1)
            m = 0
            for qt in range(1, TT):
                for h in range(NI):
                    dve.wait_ge(s["xi_read"], m + 1)
                    wcol = va[:, qt, HD + h:HD + h + 1]
                    if h == 0:
                        ins = dve.tensor_scalar(pen(qt), irelu[m % 2][:, 0:P * (qt + 1)], wcol, None, ALU.mult)
                    else:
                        dve.wait_ge(s["irelu_used"], m)
                        ins = dve.scalar_tensor_tensor(pen(qt), irelu[m % 2][:, 0:P * (qt + 1)], wcol, pen(qt),
                                                       ALU.mult, ALU.add)
                    ins.then_inc(s["irelu_used"], 1)
                    m += 1
            dve.wait_ge(s["irelu_used"], m)
            for qt in range(1, TT):
                done(dve.memset(pen(qt)[0:CH, P * qt + CH:P * (qt + 1)], HIDDEN))
            for qt in range(1, TT):
                for r in range(TOPK // 8):
                    done(dve.max(out=top8, in_=pen(qt)))
                    done(dve.match_replace(out=pen(qt), in_to_replace=top8, in_values=pen(qt), imm_value=PICKED))
                done(dve.tensor_scalar(pen(qt), pen(qt), (HIDDEN + PICKED) / 2, MASKED, ALU.is_gt, ALU.mult))
            done(dve.memset(pen(0), 0.0))
            done(dve.memset(pen(0)[0:CH, CH:P], MASKED))
            head_factors(2, 7)
            for t in range(8):
                dst = (qb, kb)[t // 4][:, t % 4, :]
                dve.wait_ge(s["xb_done"], t + 1)
                dve.scalar_tensor_tensor(dst, dst, vcol(V_GAIN + 2 + t // 4), bank(4 + t % 2), ALU.mult, ALU.mult)\
                   .then_inc(s["xb_read"], 1)

            NA = TT * HA
            for it in range(NA + 3):
                if it in MOD_AT:
                    half = slice(2 * D * MOD_AT.index(it), 2 * D * (MOD_AT.index(it) + 1))
                    w = arrived(dve, "mod2", KT - 1)[:, half]
                    dve.wait_ge(s["mod2_used"], KT - 1)
                    ins = dve.scalar_tensor_tensor(mod2_sum[:, half], w, cact[:, KT - 1:KT], mod2_sum[:, half], ALU.mult, ALU.add)
                    if it == MOD_AT[1]:
                        ins.then_inc(s["mod2_used"], 1)
                if it < NA:
                    qt = it // HA
                    n = P * (qt + 1)
                    dve.wait_ge(s["la_done"], it + 1)
                    if it >= 3:
                        dve.wait_ge(s["pt_done"], it - 2)
                    dve.tensor_tensor_reduce(out=prob[it % 3][:, 0:n], in0=bank(it % 2, n), in1=pen(qt),
                                             scale=HD ** -0.5, scalar=-3.4e38, op0=ALU.add, op1=ALU.max,
                                             accum_out=amax[:, it:it + 1]).then_inc(s["la_read"], 1)
                    dve.wait_ge(s["la_read"], it + 1)
                    dve.tensor_scalar(anmax[:, it:it + 1], amax[:, it:it + 1], -1.0, None, ALU.mult).then_inc(s["nmax_ready"], 1)
                if it >= 3 and (it - 3) % HA == HA - 1:
                    qt = (it - 3) // HA
                    c = slice(HA * qt, HA * (qt + 1))
                    dve.wait_ge(s["prob_ready"], HA * (qt + 1))
                    done(dve.reciprocal(arcp[:, c], asum[:, c]))
                    dve.wait_ge(s["pv_done"], HA * (qt + 1))
                    if qt >= 1:
                        dve.wait_ge(s["ot_done"], qt)
                    dve.tensor_tensor(tiles(o_tm, HA), tiles(bank(4 + qt % 2), HA),
                                      arcp[:, c].unsqueeze(2).broadcast_to([P, HA, HD]), ALU.mult).then_inc(s["o_ready"], 1)

            dve.wait_ge(s["mod2_done"], 1)
            dve.tensor_tensor(mcol(16, 32), bank(4, 32), vcol(V_BMOD + 16, 32), ALU.add).then_inc(s["mod2_read"], 1)
            dve.wait_ge(s["mod2_read"], 1)
            done(dve.scalar_tensor_tensor(amp2, mcol(SC2, 8), 1.0, vcol(V_G2, 8), ALU.add, ALU.mult))

            def merge(n):
                c = n % KT
                dve.wait_ge(s["gate_ready"], n + 1)
                dve.wait_ge(s["ob_done"], n + 1)
                if n < KT:
                    done(dve.tensor_tensor(merged[:, c, :], gates[n % 2], bank(out_bank(n)), ALU.mult))
                    dve.sem_inc(s["gate_used"], 1)
                else:
                    dve.tensor_tensor(gated, gates[n % 2], bank(out_bank(n)), ALU.mult).then_inc(s["gate_used"], 1)
                    dve.wait_ge(s["gate_used"], n + 1)
                    done(dve.tensor_tensor(merged[:, c, :], merged[:, c, :], gated, ALU.add))

            dve.wait_ge(s["ot_out"], TT)
            for it in range(HB + 1):
                if it < HB:
                    z = ps[:, 0:B_COLS]
                    kp, bt, sp_ = keep[it % 2], beta[it % 3], spb[it % 2]
                    dve.wait_ge(s["zb_relu"], it + 1)
                    if it >= 3:
                        dve.wait_ge(s["yb_done"], it - 2)
                    dve.tensor_scalar(bt, z, HD ** -0.5, 0.0, ALU.mult, ALU.min).then_inc(s["zb_min"], 1)
                    dve.wait_ge(s["sp_ready"], it + 1)
                    done(dve.scalar_tensor_tensor(kp, kp, -1.0, sp_, ALU.mult, ALU.subtract))
                    for st in range(TT):
                        d = kp[:, B_OFF[st]:B_OFF[st] + P]
                        ins = dve.tensor_tensor(d, d, past_tri, ALU.mult)
                    ins.then_inc(s["keep_ready"], 1)
                if it >= 1:
                    h = it - 1
                    dve.wait_ge(s["lt_done"], h + 1)
                    dve.wait_ge(s["beta_ready"], h + 1)
                    dve.tensor_tensor(beta[h % 3], beta[h % 3], ps[:, 1536:1536 + B_COLS], ALU.add).then_inc(s["sum_ready"], 1)
                if it < HB:
                    merge(it)

            dve.wait_ge(s["cu_done"], 1)
            dve.wait_ge(s["yb_done"], HB)
            for i in range(2):
                u = dve.tensor_scalar(c_e[:, T * i:T * (i + 1)], bank(i), vcol(V_BA + i), None, ALU.add)
            u.then_inc(s["cu_ready"], 1)
            dve.wait_ge(s["cabs"], 1)
            done(dve.tensor_scalar(c_e[:, 0:2 * T], c_e[:, 0:2 * T], 0.0, None, ALU.min))
            dve.wait_ge(s["csp"], 1)
            done(dve.tensor_tensor(c_e[:, 0:2 * T], c_e[:, 0:2 * T], c_e[:, 2 * T:4 * T], ALU.subtract))
            for i in range(2):
                last = dve.tensor_tensor_scan(c_b[:, T * i:T * (i + 1)], reset, c_e[:, T * i:T * (i + 1)], 0.0,
                                              ALU.mult, ALU.add)
            last.then_inc(s["cb_ready"], 1)
            dve.wait_ge(s["cb_ready"], 1)
            bch = c_b.rearrange("p (c l) -> p c l", l=CH)
            dve.tensor_copy(c_e[:, 0:2 * T], c_b)
            dve.tensor_tensor(c_e[:, 2 * T:4 * T].rearrange("p (c l) -> p c l", l=CH),
                              bch[:, :, CH - 1:CH].broadcast_to([P, 2 * NCH, CH]), bch, ALU.subtract).then_inc(s["ce_ready"], 1)
            dve.wait_ge(s["cex_ready"], 1)
            dve.tensor_tensor(c_qk0, cqk, c_e, ALU.mult).then_inc(s["cqk_ready"], 1)
            dve.wait_ge(s["cqk_ready"], 1)
            merge(KT)

            def level(lv):
                w = LEVELS[lv]
                e0 = c_e[:, 0:2 * T].rearrange("p (c l) -> p c l", l=2 * w)
                bb = c_b.rearrange("p (c l) -> p c l", l=2 * w)
                done(dve.tensor_tensor(e0, bb, bb[:, :, w - 1:w].broadcast_to([P, T // w, 2 * w]), ALU.subtract))
                done(dve.tensor_scalar(c_e[:, 2 * T:4 * T], c_e[:, 0:2 * T], -1.0, 0.0, ALU.mult, ALU.min))
                dve.tensor_scalar(c_e[:, 0:2 * T], c_e[:, 0:2 * T], 0.0, None, ALU.min).then_inc(s["ce_ready"], 1)
                dve.wait_ge(s["cex_ready"], lv + 2)
                if lv >= 2:
                    dve.wait_ge(s["lev_done"], lv - 1)
                dve.tensor_tensor(c_qk[lv % 2], cqk, c_e, ALU.mult).then_inc(s["cqk_ready"], 1)
                dve.wait_ge(s["cqk_ready"], lv + 2)

            def level_read(lv):
                m = area("const", C_LEVEL + P * lv, P).bitcast(U32)
                dve.wait_ge(s["lev_done"], lv + 1)
                dve.copy_predicated(out=tiles(c_att, 16), mask=m.unsqueeze(1).broadcast_to([P, 16, P]),
                                    data=tiles(ps[:, 2048:4096], 16)).then_inc(s["lev_read"], 1)
                dve.wait_ge(s["lev_read"], lv + 1)

            level(0)
            level(1)
            merge(KT + 1)
            dve.wait_ge(s["kv_done"], 1)
            dve.wait_ge(s["ebl_ready"], 1)
            for c in range(1, NCH):
                for i in range(2):
                    new = c_state[:, 2 * P * c + P * i:2 * P * c + P * (i + 1)]
                    old = c_state[:, 2 * P * (c - 1) + P * i:2 * P * (c - 1) + P * (i + 1)]
                    kv = ps[:, kv_at(c - 1, i):kv_at(c - 1, i) + P]
                    if c == 1:
                        ins = dve.tensor_copy(new, kv)
                    else:
                        ins = dve.scalar_tensor_tensor(new, old, ebl[:, NCH * i + c - 1:NCH * i + c], kv, ALU.mult, ALU.add)
                ins.then_inc(s["st_ready"], 1)
                dve.wait_ge(s["st_ready"], c)
            dve.wait_ge(s["att_zero"], 1)
            for lv in range(len(LEVELS) + 1):
                level_read(lv)
                if lv + 2 < len(LEVELS):
                    level(lv + 2)
                if lv < len(LEVELS) - 1:
                    merge(KT + 2 + lv)
            merge(2 * KT - 1)
            dve.sem_inc(s["att_ready"], 1)
            dve.wait_ge(s["css_ready"], 1)
            done(dve.tensor_reduce(css, tiles(c_e, 16), AX, ALU.add))
            dve.tensor_scalar(cvar, css, 1 / CV, EPS, ALU.mult, ALU.add).then_inc(s["cvar_ready"], 1)
            dve.wait_ge(s["crt_ready"], 1)
            done(inverse_root(crs, crt, cvar, ct1))
            done(dve.tensor_tensor(tiles(c_e, 16), tiles(ps[:, 0:4 * T], 16), crs.unsqueeze(2).broadcast_to([P, 16, CV]),
                                   ALU.mult))
            dve.wait_ge(s["rgain"], 1)
            for b in range(2):
                e = c_e[:, 2 * T * b:2 * T * (b + 1)].rearrange("p (t a v) -> p t a v", t=TT, v=CV)
                g = area("rc", 0, TT * T).rearrange("p (t a b v) -> p t a b v", t=TT, b=2, v=CV)[:, :, :, b, :]
                ins = dve.tensor_tensor(e, e, g, ALU.mult)
            ins.then_inc(s["co_ready"], 1)

            for n in range(2 * KT, NG):
                merge(n)
            dve.sem_inc(s["merged_ready"], 1)

            def residual(t):
                dve.wait_ge(s["yg_ready"], 2 * t + 2)
                tile = slice(P * t, P * (t + 1))
                dve.tensor_tensor(h_t[:, :, tile], yg[t % 2], x_ch[:, :, tile], ALU.add).then_inc(s["ht_ready"], 1)
                dve.wait_ge(s["hsq_ready"], t + 1)
                if t >= 1:
                    dve.wait_ge(s["hsq_used"], t)
                dve.tensor_reduce(hsq_sum, squares.rearrange("p c t -> p t c"), AX, ALU.add).then_inc(s["hsq_summed"], 1)

            def normed(t):
                tile = slice(P * t, P * (t + 1))
                dve.wait_ge(s["hsq_used"], t + 1)
                dve.tensor_scalar(nvar, bank(2, P), 1 / D, EPS, ALU.mult, ALU.add).then_inc(s["nvar_ready"], 1)
                dve.wait_ge(s["nrt_ready"], t + 1)
                done(inverse_root(nr, nrt, nvar, ntmp))
                dve.tensor_tensor(n_t[:, :, tile], h_t[:, :, tile], nr.unsqueeze(1).broadcast_to([P, KT, P]), ALU.mult)\
                   .then_inc(s["nx_ready"], 1)
                dve.wait_ge(s["nx_ready"], t + 1)

            k = pick
            iota = area("const", C_IOTA, 16)

            def pick_experts(u, r, scored):
                n = [0]
                base = u * PICK_STEPS

                def step(ins, own=False):
                    n[0] += 1
                    ins.then_inc(s["p_step"], 1)
                    dve.wait_ge(s["p_step"], base + n[0])
                    if own:
                        dve.sem_inc(s["p_go"], 1)

                if scored is None:
                    dve.wait_ge(s["first_sc"], 1)
                    step(dve.tensor_copy(k["sc"], bank(3, 2 * NK)), own=True)
                else:
                    dve.wait_ge(s["sc_done"], scored)
                    step(dve.tensor_copy(k["sc"], bank(6 + r // 2, 2 * NK, 2 * NK * (r % 2))), own=True)
                dve.sem_inc(s["sc_read"], 1)
                half = [(k["sc"][:, NK * c:NK * (c + 1)], k["left"][:, NK * c:NK * (c + 1)], k["top"][:, 16 * c:16 * c + 8],
                         k["top"][:, 16 * c + 8:16 * c + 16], ix_u[:, 16 * c:16 * c + 8], ix_u[:, 16 * c + 8:16 * c + 16])
                        for c in range(2)]

                def pair(ins):
                    ins[0].then_inc(s["p_step"], 1)
                    n[0] += 1
                    step(ins[1], own=True)

                pair([dve.max(out=t0, in_=row) for row, left, t0, t1, i0, i1 in half])
                for row, left, t0, t1, i0, i1 in half:
                    dve.max_index(out=i0, in_max=t0, in_values=row)
                pair([dve.match_replace(out=left, in_to_replace=t0, in_values=row, imm_value=PICKED)
                      for row, left, t0, t1, i0, i1 in half])
                pair([dve.max(out=t1, in_=left) for row, left, t0, t1, i0, i1 in half])
                pair([dve.max_index(out=i1, in_max=t1, in_values=left) for row, left, t0, t1, i0, i1 in half])
                step(dve.tensor_tensor(tiles(k["cand"], 16), k["top"][:, 0:16].unsqueeze(2).broadcast_to([P, 16, 16]),
                                       k["top"][:, 16:32].unsqueeze(1).broadcast_to([P, 16, 16]), ALU.add), own=True)
                b0, b1 = k["best"][:, 0:8], k["best"][:, 8:16]
                step(dve.max(out=b0, in_=k["cand"]), own=True)
                dve.max_index(out=bj_u[:, 0:8], in_max=b0, in_values=k["cand"])
                step(dve.match_replace(out=k["cleft"], in_to_replace=b0, in_values=k["cand"], imm_value=PICKED), own=True)
                step(dve.max(out=b1, in_=k["cleft"]), own=True)
                step(dve.max_index(out=bj_u[:, 8:16], in_max=b1, in_values=k["cleft"]))
                dve.tensor_scalar(hl_u[:, 0:16], bj_u, 4, None, ALU.logical_shift_right)
                step(dve.tensor_scalar(hl_u[:, 16:32], bj_u, 15, None, ALU.bitwise_and))
                dve.tensor_copy(k["hl"], hl_u)
                step(dve.tensor_copy(k["ixf"], ix_u))
                step(dve.tensor_tensor(tiles(k["eq"], 32), iota.unsqueeze(1).broadcast_to([P, 32, 16]),
                                       k["hl"].unsqueeze(2).broadcast_to([P, 32, 16]), ALU.is_equal))
                e = k["eq"].rearrange("p (c j a) -> p c j a", c=2, j=16)
                step(dve.tensor_tensor(e, e, tiles(k["ixf"], 2).unsqueeze(2).broadcast_to([P, 2, 16, 16]), ALU.mult))
                step(dve.tensor_reduce(k["ef"], tiles(k["eq"], 32), AX, ALU.add))
                dve.scalar_tensor_tensor(experts[r], k["ef"][:, 0:16], float(NK), k["ef"][:, 16:32],
                                         ALU.mult, ALU.add)
                step(dve.tensor_scalar(best[r], k["best"], k["best"][:, 0:1], None, ALU.subtract))
                dve.sem_inc(s["picked"], 1)
                assert n[0] == PICK_STEPS

            def dot(u, r, rows=range(PK)):
                for i in rows:
                    dve.wait_ge(u_in[i % R], (u * (PK // R) + i // R + 1) * 16)
                    dve.tensor_tensor_reduce(out=u_ring[i % R], in0=u_ring[i % R], in1=n2_tm[:, r, :], scale=1.0, scalar=0.0,
                                             op0=ALU.mult, op1=ALU.add, accum_out=dots[r % 2][:, i:i + 1]).then_inc(s["u_used"], 1)
                if rows[-1] == PK - 1:
                    dve.wait_ge(s["u_used"], (u + 1) * PK + R)
                    dve.sem_inc(s["dots_ready"], 1)

            def weight(u, r):
                dve.wait_ge(s["z_ready"], u + 1)
                dve.reciprocal(zinv[r % 2], zsum[r % 2]).then_inc(s["zi_ready"], 1)
                dve.wait_ge(s["zi_ready"], u + 1)
                dve.wait_ge(s["gelu_ready"], u + 1)
                dve.scalar_tensor_tensor(wgt[r % 2], gelu[r % 2], zinv[r % 2], ebest[r % 2], ALU.mult, ALU.mult)\
                   .then_inc(s["w_ready"], 1)

            def add(u, r):
                dve.wait_ge(s["acc_done"], u + 1)
                dve.wait_ge(s["tm_out"], 4 * TT)
                dve.tensor_tensor(acc_tmp, ps[:, D * (r % 2):D * (r % 2 + 1)], g2row, ALU.mult).then_inc(s["gated2"], 1)
                dve.wait_ge(s["gated2"], u + 1)
                dve.sem_inc(s["acc_free"], 1)
                dve.tensor_tensor(h_tm[:, r, :], h_tm[:, r, :], acc_tmp, ALU.add).then_inc(s["added"], 1)
                dve.wait_ge(s["added"], u + 1)

            dve.wait_ge(s["ld_x2"], 16)
            residual(0)
            normed(0)
            residual(1)
            pick_experts(0, 0, None)
            normed(1)
            residual(2)
            dve.wait_ge(s["tm_out"], 2)
            dot(0, 0, range(R))
            pick_experts(1, 1, 1)
            residual(3)
            normed(2)
            normed(3)
            dve.wait_ge(s["hsq_summed"], TT)
            for c in range(KT):
                ins = dve.tensor_scalar(g2tmp[:, c, :], ones, mcol(GT2 + c), None, ALU.mult)
            ins.then_inc(s["g2t_ready"], 1)
            dot(0, 0, range(R, PK))
            weight(0, 0)
            dve.wait_ge(s["g2_done"], 1)
            dve.tensor_copy(g2row, ps[:, 2 * T:2 * T + D]).then_inc(s["g2_ready"], 1)
            dve.wait_ge(s["g2_ready"], 1)
            pick_experts(2, 2, 2)
            dve.wait_ge(s["tm_out"], 2 * TT)
            with dve.Fori(0, PH - 1) as b:
                for j in range(1, TT + 1):
                    u, r, nxt = b * TT + j, j % TT, (j + 2) % TT
                    dot(u, r)
                    weight(u, r)
                    pick_experts(u + 2, nxt, b * 2 + (2 if j == 1 else (3 if nxt < 2 else 4)))
                    add(u - 1, (r - 1) % TT)
            for u in range(NU - 3, NU):
                dot(u, u % TT)
                weight(u, u % TT)
                if u == NU - 3:
                    pick_experts(NU - 1, TT - 1, 2 * PH)
                add(u - 1, (u - 1) % TT)
            add(NU - 1, TT - 1)

        @block.gpsimd
        def _(pool):
            pool.wait_ge(s["cact_ready"], 1)
            pool.wait_ge(s["xhat_ready"], TT)
            for k in range(KT - 1):
                w = arrived(pool, "mod2", k)[:, 0:4096]
                if k == 0:
                    ins = pool.tensor_scalar(mod2_sum, w, cact[:, 0:1], None, ALU.mult)
                else:
                    pool.tensor_scalar(w, w, cact[:, k:k + 1], None, ALU.mult).then_inc(s["mod2_scaled"], 1)
                    pool.wait_ge(s["mod2_scaled"], k)
                    pool.wait_ge(s["mod2_used"], k)
                    ins = pool.tensor_tensor(mod2_sum, mod2_sum, w, ALU.add)
                ins.then_inc(s["mod2_used"], 1)
            for it in range(HB + 1):
                if it < HB:
                    pool.wait_ge(s["zb_min"], it + 1)
                    pool.wait_ge(s["sp_ready"], it + 1)
                    pool.tensor_tensor(beta[it % 3], beta[it % 3], spb[it % 2], ALU.subtract).then_inc(s["beta_ready"], 1)
                if it < HB:
                    kp = keep[it % 2]
                    pool.wait_ge(s["keep_ready"], it + 1)
                    if it >= 1:
                        pool.wait_ge(s["lt_done"], it)
                    a, b = B_OFF[1] + P, B_OFF[2]
                    pool.tensor_tensor(keep_sum[:, 2 * P:3 * P], kp[:, b + P:b + 2 * P], kp[:, B_OFF[3]:B_OFF[3] + P], ALU.add)\
                        .then_inc(s["ksum_step"], 1)
                    pool.tensor_tensor(keep_sum[:, 0:P], kp[:, a:a + P], kp[:, b:b + P], ALU.add)
                    pool.wait_ge(s["ksum_step"], it + 1)
                    pool.tensor_tensor(keep_sum[:, P:2 * P], kp[:, a + P:a + 2 * P], keep_sum[:, 2 * P:3 * P], ALU.add)\
                        .then_inc(s["ksum_ready"], 1)
                if it >= 1:
                    h = it - 1
                    pool.wait_ge(s["a_exp"], h + 1)
                    for st in range(TT):
                        d = beta[h % 3][:, B_OFF[st]:B_OFF[st] + P]
                        ins = pool.tensor_tensor(d, d, past_tri, ALU.mult)
                    ins.then_inc(s["b_ready"], 1)
            pool.wait_ge(s["zb_done"], HB)
            pool.memset(c_att, 0.0).then_inc(s["att_zero"], 1)
            pool.wait_ge(s["rsil"], 1)
            pool.tensor_tensor(rc, rc, vcol(V_ONG, T).unsqueeze(1).broadcast_to([P, TT, T]), ALU.mult).then_inc(s["rgain"], 1)

            GROUP = 4

            def rows(table, r, ring, arrived, used, u, i0):
                pool.wait_ge(used, u * PK + i0 + GROUP)
                pool.sem_inc(s["pool_go"], 1)
                for i in range(i0, i0 + GROUP):
                    pool.indirect_dma_start(out=ring[i % R], out_offset=None, in_=table,
                                            in_offset=bass.IndirectOffsetOnAxis(ap=experts[r][:, i:i + 1], axis=0))\
                        .then_inc(arrived[i % R], 16)

            def rows_u(u, r, i0):
                if i0 == 0:
                    pool.wait_ge(s["picked"], u + 1)
                rows(u_table, r, u_ring, u_in, s["u_used"], u, i0)

            def rows_v(u, r, i0):
                rows(v_table, r, v_ring, v_in, s["dg_used"], u, i0)

            def unit(u, r):
                for i0 in range(0, PK, GROUP):
                    rows_u(u, r, i0)
                    if i0 + GROUP < PK:
                        rows_v(u - 1, (r - 1) % TT, i0 + GROUP)
                    else:
                        rows_v(u, r, 0)

            for i0 in range(0, PK, GROUP):
                rows_u(0, 0, i0)
            rows_v(0, 0, 0)
            with pool.Fori(0, PH - 1) as b:
                for j in range(1, TT + 1):
                    unit(b * TT + j, j % TT)
            for u in range(NU - 3, NU):
                unit(u, u % TT)
            for i0 in range(GROUP, PK, GROUP):
                rows_v(NU - 1, TT - 1, i0)


def laid_out(inp):
    d = {k: np.asarray(v) for k, v in inp.items()}
    w = d["w_in"][0]
    o = np.cumsum([0, 512, 64, 64, 256, 64, 4, 512, 512, 512, 256, 256, 512, 512, 16, 3 * D])
    aq, ak, av, iq, ik, iw, bq, bk, bv, cq, ck, cv, cr, ca, gl = (w[:, o[i]:o[i + 1]] for i in range(15))

    def by_tile(m):
        return m.reshape(-1, P, m.shape[1] // P, P).transpose(1, 2, 0, 3).reshape(P, -1)

    def by_row(m):
        return m.reshape(-1, P, m.shape[1]).transpose(1, 0, 2).reshape(P, -1)

    keys_and_index = np.pad(by_tile(np.concatenate([ak, ik, iq], 1)), ((0, 0), (0, KT * P)))
    proj = np.stack([by_tile(aq), keys_and_index, by_tile(bq), by_tile(bk), by_row(bv), by_row(cv), by_tile(np.concatenate([cq, ck], 1)), by_row(cr)])
    merge = []
    wo = [d[k][0] for k in ("w_oa", "w_ob", "w_oc")]
    for b in range(3):
        units = [np.concatenate([by_row(m[:, P * c:P * (c + 1)]) for m in (gl[:, D * b:D * (b + 1)], wo[b])], 1)
                 for c in range(KT)]
        for c in range(0, KT, 3):
            group = np.concatenate(units[c:c + 3], 1)
            merge.append(np.pad(group, ((0, 0), (0, WSLOT - group.shape[1]))))

    def col(v):
        return v.reshape(-1, P).T

    vec = np.concatenate(
        [col(d["c"][0]), col(d["b_mod"][0]), col(d["norm1_g"][0]), col(d["norm2_g"][0]), col(d["b_gate"][0]),
         col(d["c_b_alpha"][0])] + [np.tile(d[k][0], 2)[:, None] for k in ("a_qn_g", "a_kn_g", "b_qn_g", "b_kn_g")]
        + [np.tile(d["c_on_g"][0], (P, 1))], 1)
    small = np.concatenate([av, iw, ca], 1)
    keys = d["peer_subkeys"][0].transpose(0, 3, 1, 2).reshape(PH, P, 2 * NK)
    pq = np.stack([np.concatenate([by_tile(d["peer_wq"][0][:, 2 * P * h:2 * P * (h + 1)]), keys[h]], 1) for h in range(PH)])
    return {
        "cst": shape_constants(), "vec": vec, "x": d["x"][0], "x_turned": by_row(d["x"][0].T), "w_mod": d["w_mod"][0], "w_proj": proj,
        "w_small": by_row(small), "w_alpha": d["c_w_alpha"][0], "w_merge": np.stack(merge),
        "w_out": by_tile(d["w_out"][0]), "w_pq": pq,
        "u_table": d["peer_u"][0], "v_table": d["peer_v"][0],
    }


def kernel(**inputs):
    import concourse.bacc as bacc
    from concourse.bass_utils import run_bass_kernel_spmd

    nc = bacc.Bacc("TRN2", target_bir_lowering=False, num_devices=1)
    arrays = {k: np.ascontiguousarray(v) for k, v in laid_out(inputs).items()}
    args = [nc.dram_tensor(k, a.shape, mybir.dt.from_np(a.dtype), kind="ExternalInput").ap() for k, a in arrays.items()]
    out = nc.dram_tensor("out", (T, D), F32, kind="ExternalOutput").ap()
    encoder_layer(nc, *args, out)
    r = run_bass_kernel_spmd(nc, [arrays], core_ids=[0])
    return np.asarray(r.results[0]["out"]).reshape(1, T, D)
```
